# Optimizing a Trainium2 kernel written in Bass

```python
import jax
import jax.numpy as jnp
from jax import lax
import numpy as np
import jax, jax.numpy as jnp

D_MODEL = 1024
BATCH = 1
SEQ = 512
DEPTH = 2

GRID_W = 64
CTX_LEN = 256
EPS = 1e-6
F_MIN = 1e-6
A_HEAD_DIM = 128
A_HEADS = D_MODEL // (2 * A_HEAD_DIM)
A_WIDTH = A_HEADS * A_HEAD_DIM
HGRN_CHUNK = 64
B_GROUPS = 4
B_WIDTH = D_MODEL - A_WIDTH
B_GROUP_DIM = B_WIDTH // B_GROUPS
B_CHUNK = 128
EV_IN = 5 * A_WIDTH + 2 * B_WIDTH
C_WIDTH = D_MODEL // 4
C_GROUPS = 4
C_GROUP_DIM = C_WIDTH // C_GROUPS
MLA_V_DIM = 128
MLA_HEADS = (D_MODEL - C_WIDTH) // MLA_V_DIM
MLA_NOPE = 128
MLA_ROPE = 64
MLA_QK = MLA_NOPE + MLA_ROPE
Q_LORA = 384
KV_LORA = 256
OD_IN = C_WIDTH + Q_LORA + KV_LORA + MLA_ROPE
ROPE_THETA = 10000.0
ATTN_BLOCK = 128
D_FF = 2816
CONV_W = 3


def rms_norm(x, w):
    xf = x.astype(jnp.float32)
    y = xf * lax.rsqrt(jnp.mean(xf * xf, axis=-1, keepdims=True) + EPS)
    return y.astype(x.dtype) * w

def modulate(x, norm_w, shift, scale):
    return rms_norm(x, norm_w) * (1 + scale) + shift

def to_heads(a, n_heads):
    bsz, t_len, width = a.shape
    return a.reshape(bsz, t_len, n_heads, width // n_heads).transpose(0, 2, 1, 3)

def flip_t(a):
    return a[:, :, ::-1]

def gla_chunked(q, k, v, log_f, s0):
    bsz, nh, t_len, _ = q.shape
    dv = v.shape[-1]
    n_chunks = t_len // HGRN_CHUNK

    def to_chunks(a):
        return a.reshape(bsz, nh, n_chunks, HGRN_CHUNK, a.shape[-1]).transpose(2, 0, 1, 3, 4)

    prefix_mask = jnp.tril(jnp.ones((HGRN_CHUNK, HGRN_CHUNK), dtype=bool))[:, :, None]

    def step(state, inp):
        qc, kc, vc, gc = inp
        b = jnp.cumsum(gc, axis=2)
        diff = b[:, :, :, None, :] - b[:, :, None, :, :]
        decay = jnp.where(prefix_mask, jnp.exp(jnp.minimum(diff, 0.0)), 0.0)
        scores = jnp.einsum('bhtk,bhsk,bhtsk->bhts', qc, kc, decay)
        out = (jnp.einsum('bhtk,bhkv->bhtv', qc * jnp.exp(b), state)
               + jnp.einsum('bhts,bhsv->bhtv', scores, vc))
        b_last = b[:, :, -1:, :]
        new_state = (jnp.exp(b_last[:, :, 0, :])[..., None] * state
                     + jnp.einsum('bhsk,bhsv->bhkv', kc * jnp.exp(b_last - b), vc))
        return new_state, out

    s_fin, o = lax.scan(step, s0, (to_chunks(q), to_chunks(k), to_chunks(v), to_chunks(log_f)))
    return o.transpose(1, 2, 0, 3, 4).reshape(bsz, nh, t_len, dv), s_fin

def hgrn2_features(p, lb):
    f32 = jnp.float32
    q = to_heads(jax.nn.silu(p[..., :A_WIDTH]).astype(f32), A_HEADS)
    v = to_heads(p[..., A_WIDTH:2 * A_WIDTH].astype(f32), A_HEADS)
    out = []
    for d in range(2):
        z = p[..., (2 + d) * A_WIDTH:(3 + d) * A_WIDTH].astype(f32)
        f = jnp.maximum(lb[d] + (1.0 - lb[d]) * jax.nn.sigmoid(z), F_MIN)
        log_f = jnp.log(f)
        k = 1.0 - f
        out.append((q, to_heads(k, A_HEADS), v, to_heads(log_f, A_HEADS)))
    return out

def hgrn2_readout(o, g, onorm_w):
    bsz, _, t_len, _ = o.shape
    o = rms_norm(o.transpose(0, 2, 1, 3), onorm_w).reshape(bsz, t_len, A_WIDTH)
    return (o * jax.nn.silu(g.astype(jnp.float32))).astype(g.dtype)

def hgrn2_mixer(pl, pc, lb, onorm_w, with_ctx):
    fwd_l, bwd_l = hgrn2_features(pl, lb)
    fwd_c, bwd_c = hgrn2_features(pc, lb)
    s0 = jnp.zeros((pl.shape[0], A_HEADS, A_HEAD_DIM, A_HEAD_DIM), jnp.float32)
    oc_f, sc_f = gla_chunked(*fwd_c, s0)
    ol_f, _ = gla_chunked(*fwd_l, sc_f)
    oc_b, sc_b = gla_chunked(*[flip_t(a) for a in bwd_c], s0)
    ol_b, _ = gla_chunked(*[flip_t(a) for a in bwd_l], sc_b)
    g_sl = slice(4 * A_WIDTH, 5 * A_WIDTH)
    yl = hgrn2_readout(ol_f + flip_t(ol_b), pl[..., g_sl], onorm_w)
    yc = None
    if with_ctx:
        yc = hgrn2_readout(oc_f + flip_t(oc_b), pc[..., g_sl], onorm_w)
    return yl, yc

def chunk_mlp(u_pre, v_pre, vnorm_w, ws, bs):
    bsz, t_len, _ = u_pre.shape
    n = t_len // B_CHUNK
    u = jax.nn.gelu(u_pre)
    v = rms_norm(jax.nn.gelu(v_pre).reshape(bsz, n, B_CHUNK, B_GROUPS, B_GROUP_DIM), vnorm_w)
    sv = jnp.einsum('gts,bnsgc->bntgc', ws, v) + bs.T[:, :, None]
    return u * sv.reshape(bsz, t_len, B_WIDTH)

def even_mixer(hl, hc, w_in, lb, onorm_w, vnorm_w, ws, bs, w_out, with_ctx):
    pl = hl @ w_in
    pc = hc @ w_in
    a_sl = slice(0, 5 * A_WIDTH)
    u_sl = slice(5 * A_WIDTH, 5 * A_WIDTH + B_WIDTH)
    v_sl = slice(5 * A_WIDTH + B_WIDTH, EV_IN)
    al, ac = hgrn2_mixer(pl[..., a_sl], pc[..., a_sl], lb, onorm_w, with_ctx)
    yl = jnp.concatenate([al, chunk_mlp(pl[..., u_sl], pl[..., v_sl], vnorm_w, ws, bs)], -1) @ w_out
    yc = None
    if with_ctx:
        yc = jnp.concatenate([ac, chunk_mlp(pc[..., u_sl], pc[..., v_sl], vnorm_w, ws, bs)], -1) @ w_out
    return yl, yc

def fourier_mix(p):
    bsz, t_len, _ = p.shape
    xg = p.reshape(bsz, t_len, C_GROUPS, C_GROUP_DIM).astype(jnp.float32)
    y = jnp.fft.fft2(xg, axes=(1, 3), norm='ortho').real
    return y.reshape(bsz, t_len, C_WIDTH).astype(p.dtype)

def rope_2d(x, cos, sin):
    xr = x.reshape(*x.shape[:-1], 2, 2, MLA_ROPE // 4)
    x1, x2 = xr[..., 0, :], xr[..., 1, :]
    return jnp.stack([x1 * cos - x2 * sin, x2 * cos + x1 * sin], axis=-2).reshape(x.shape)

def mla_project(p, qa_w, w_qb, kva_w, w_kvb, qn_w, kn_w, cos, sin):
    bsz, t_len, _ = p.shape
    q_lat = rms_norm(p[..., :Q_LORA], qa_w)
    kv_lat = rms_norm(p[..., Q_LORA:Q_LORA + KV_LORA], kva_w)
    k_pe = rms_norm(p[..., Q_LORA + KV_LORA:], kn_w[MLA_NOPE:])
    q = (q_lat @ w_qb).reshape(bsz, t_len, MLA_HEADS, MLA_QK)
    kv = (kv_lat @ w_kvb).reshape(bsz, t_len, MLA_HEADS, MLA_NOPE + MLA_V_DIM)
    q_nope = rms_norm(q[..., :MLA_NOPE], qn_w[:MLA_NOPE])
    q_pe = rms_norm(q[..., MLA_NOPE:], qn_w[MLA_NOPE:])
    k_nope = rms_norm(kv[..., :MLA_NOPE], kn_w[:MLA_NOPE])
    if cos is not None:
        q_pe = rope_2d(q_pe, cos[:, None], sin[:, None])
        k_pe = rope_2d(k_pe, cos, sin)
    k_pe = jnp.broadcast_to(k_pe[:, :, None, :], (bsz, t_len, MLA_HEADS, MLA_ROPE))
    q = jnp.concatenate([q_nope, q_pe], -1)
    k = jnp.concatenate([k_nope, k_pe], -1)
    return q, k, kv[..., MLA_NOPE:]

def attend(q, k, v):
    bsz, tq, nh, dq = q.shape
    nb = tq // ATTN_BLOCK
    qb = q.reshape(bsz, nb, ATTN_BLOCK, nh, dq).transpose(1, 0, 2, 3, 4)
    scale = dq ** -0.5

    def one_block(qblk):
        s = jnp.einsum('bqhd,bkhd->bhqk', qblk, k).astype(jnp.float32) * scale
        p = jax.nn.softmax(s, axis=-1).astype(v.dtype)
        return jnp.einsum('bhqk,bkhd->bqhd', p, v)

    o = lax.map(one_block, qb)
    return o.transpose(1, 0, 2, 3, 4).reshape(bsz, tq, nh * v.shape[-1])

def odd_mixer(hl, hc, w_in, qa_w, w_qb, kva_w, w_kvb, qn_w, kn_w, w_out, cos, sin, with_ctx):
    pl = hl @ w_in
    pc = hc @ w_in
    ql, kl, vl = mla_project(pl[..., C_WIDTH:], qa_w, w_qb, kva_w, w_kvb, qn_w, kn_w, cos, sin)
    qc, kc, vc = mla_project(pc[..., C_WIDTH:], qa_w, w_qb, kva_w, w_kvb, qn_w, kn_w, None, None)
    k_all = jnp.concatenate([kc, kl], axis=1)
    v_all = jnp.concatenate([vc, vl], axis=1)
    yl = jnp.concatenate([fourier_mix(pl[..., :C_WIDTH]), attend(ql, k_all, v_all)], -1) @ w_out
    yc = None
    if with_ctx:
        yc = jnp.concatenate([fourier_mix(pc[..., :C_WIDTH]), attend(qc, kc, vc)], -1) @ w_out
    return yl, yc

def conv_ffn(h, w_up, conv_w, conv_b, w_down):
    t_len = h.shape[1]
    up = h @ w_up
    gate, val = up[..., :D_FF], up[..., D_FF:]
    pad = CONV_W // 2
    gp = jnp.pad(gate, ((0, 0), (pad, pad), (0, 0)))
    gate_c = conv_b
    for j in range(CONV_W):
        gate_c = gate_c + gp[:, j:j + t_len] * conv_w[j]
    return (jax.nn.silu(gate_c) * val) @ w_down

def first_inputs(seed: int = 0) -> dict:
    key = jax.random.key(seed)
    ks = jax.random.split(key, 27)
    f32 = jnp.float32
    n_ev = (DEPTH + 1) // 2
    n_od = DEPTH // 2

    def normal(k, shape, scale):
        return jax.random.normal(k, shape, f32) * scale

    def gain(k, shape):
        return 1.0 + 0.02 * jax.random.normal(k, shape, f32)

    return {
        'x': normal(ks[0], (BATCH, SEQ, D_MODEL), 1.0),
        'c': normal(ks[1], (BATCH, D_MODEL), 1.0),
        'ctx': normal(ks[2], (BATCH, CTX_LEN, D_MODEL), 1.0),
        'c_ctx': normal(ks[3], (D_MODEL,), 1.0),
        'ada_w': normal(ks[4], (DEPTH, D_MODEL, 6 * D_MODEL), 0.5 * D_MODEL ** -0.5),
        'ada_b': normal(ks[5], (DEPTH, 6 * D_MODEL), 0.02),
        'norm_mix_w': gain(ks[6], (DEPTH, D_MODEL)),
        'norm_ffn_w': gain(ks[7], (DEPTH, D_MODEL)),
        'ev_w_in': normal(ks[8], (n_ev, D_MODEL, EV_IN), D_MODEL ** -0.5),
        'ev_lb_logits': normal(ks[9], (n_ev, 2, A_WIDTH), 1.0),
        'ev_onorm_w': gain(ks[10], (n_ev, A_HEAD_DIM)),
        'ev_vnorm_w': gain(ks[11], (n_ev, B_GROUPS, B_GROUP_DIM)),
        'ev_ws': normal(ks[12], (n_ev, B_GROUPS, B_CHUNK, B_CHUNK), B_CHUNK ** -0.5),
        'ev_bs': 1.0 + normal(ks[13], (n_ev, B_GROUPS, B_CHUNK), 0.1),
        'ev_w_out': normal(ks[14], (n_ev, D_MODEL, D_MODEL), D_MODEL ** -0.5),
        'od_w_in': normal(ks[15], (n_od, D_MODEL, OD_IN), D_MODEL ** -0.5),
        'od_qa_norm_w': gain(ks[16], (n_od, Q_LORA)),
        'od_w_qb': normal(ks[17], (n_od, Q_LORA, MLA_HEADS * MLA_QK), Q_LORA ** -0.5),
        'od_kva_norm_w': gain(ks[18], (n_od, KV_LORA)),
        'od_w_kvb': normal(ks[19], (n_od, KV_LORA, MLA_HEADS * (MLA_NOPE + MLA_V_DIM)), KV_LORA ** -0.5),
        'od_q_norm_w': gain(ks[20], (n_od, MLA_QK)),
        'od_k_norm_w': gain(ks[21], (n_od, MLA_QK)),
        'od_w_out': normal(ks[22], (n_od, D_MODEL, D_MODEL), D_MODEL ** -0.5),
        'ffn_w_up': normal(ks[23], (DEPTH, D_MODEL, 2 * D_FF), D_MODEL ** -0.5),
        'ffn_conv_w': normal(ks[24], (DEPTH, CONV_W, D_FF), CONV_W ** -0.5),
        'ffn_conv_b': normal(ks[25], (DEPTH, D_FF), 0.02),
        'ffn_w_down': normal(ks[26], (DEPTH, D_FF, D_MODEL), D_FF ** -0.5),
    }

def first_block(x, c, ctx, c_ctx, ada_w, ada_b, norm_mix_w, norm_ffn_w, ev_w_in, ev_lb_logits,
              ev_onorm_w, ev_vnorm_w, ev_ws, ev_bs, ev_w_out, od_w_in, od_qa_norm_w, od_w_qb,
              od_kva_norm_w, od_w_kvb, od_q_norm_w, od_k_norm_w, od_w_out, ffn_w_up, ffn_conv_w,
              ffn_conv_b, ffn_w_down):
    f32 = jnp.float32
    n_lat = x.shape[1]
    ROWS = n_lat // GRID_W
    row = jnp.repeat(jnp.arange(ROWS), GRID_W)
    col = jnp.tile(jnp.arange(GRID_W), ROWS)
    r_axis = MLA_ROPE // 2
    inv_freq = ROPE_THETA ** (-jnp.arange(0, r_axis, 2, dtype=f32) / r_axis)
    ang = jnp.stack([row, col], axis=-1).astype(f32)[:, :, None] * inv_freq
    cos = jnp.cos(ang).astype(x.dtype)
    sin = jnp.sin(ang).astype(x.dtype)
    lb_p = jax.nn.softmax(ev_lb_logits.astype(f32), axis=0)
    lbs = jnp.cumsum(lb_p, axis=0) - lb_p[0]

    silu_c = jax.nn.silu(c)
    silu_cc = jax.nn.silu(c_ctx)
    xl, xc = x, ctx
    for l in range(DEPTH):
        with_ctx = l < DEPTH - 1
        mod_l = (silu_c @ ada_w[l] + ada_b[l])[:, None, :]
        mod_c = (silu_cc @ ada_w[l] + ada_b[l])[None, None, :]
        sh1, sc1, g1, sh2, sc2, g2 = jnp.split(mod_l, 6, axis=-1)
        csh1, csc1, cg1, csh2, csc2, cg2 = jnp.split(mod_c, 6, axis=-1)
        hl = modulate(xl, norm_mix_w[l], sh1, sc1)
        hc = modulate(xc, norm_mix_w[l], csh1, csc1)
        if l % 2 == 0:
            e = l // 2
            yl, yc = even_mixer(hl, hc, ev_w_in[e], lbs[e], ev_onorm_w[e], ev_vnorm_w[e],
                                ev_ws[e], ev_bs[e], ev_w_out[e], with_ctx)
        else:
            o = l // 2
            yl, yc = odd_mixer(hl, hc, od_w_in[o], od_qa_norm_w[o], od_w_qb[o], od_kva_norm_w[o],
                               od_w_kvb[o], od_q_norm_w[o], od_k_norm_w[o], od_w_out[o],
                               cos, sin, with_ctx)
        xl = xl + g1 * yl
        xl = xl + g2 * conv_ffn(modulate(xl, norm_ffn_w[l], sh2, sc2), ffn_w_up[l],
                                ffn_conv_w[l], ffn_conv_b[l], ffn_w_down[l])
        if with_ctx:
            xc = xc + cg1 * yc
            xc = xc + cg2 * conv_ffn(modulate(xc, norm_ffn_w[l], csh2, csc2), ffn_w_up[l],
                                     ffn_conv_w[l], ffn_conv_b[l], ffn_w_down[l])
    return xl


DEPTH_2 = 1

DN_HEADS = 8
DN_DK = 128
DN_DV = 128
DN_QK_WIDTH = DN_HEADS * DN_DK
DN_WIDTH = DN_HEADS * DN_DV
CONV_K = 4
CHUNK = 64
DIL_CONFIGS = ((128, 1), (512, 4), (2048, 16))
HEADS_PER_GROUP = 4
ATTN_HEADS = HEADS_PER_GROUP * len(DIL_CONFIGS)
ATTN_HEAD_DIM = 64
ATTN_WIDTH = ATTN_HEADS * ATTN_HEAD_DIM
IN_SPLITS = (DN_QK_WIDTH, DN_QK_WIDTH, DN_WIDTH, DN_WIDTH, DN_HEADS, DN_HEADS,
             ATTN_WIDTH, ATTN_WIDTH, ATTN_WIDTH, ATTN_WIDTH, D_MODEL, D_MODEL)
N_IN = sum(IN_SPLITS)


def rms_norm_2(x, w):
    xf = x.astype(jnp.float32)
    y = xf * lax.rsqrt(jnp.mean(xf * xf, axis=-1, keepdims=True) + EPS)
    return (y * w.astype(jnp.float32)).astype(x.dtype)

def l2_normalize(x):
    xf = x.astype(jnp.float32)
    return xf * lax.rsqrt(jnp.sum(xf * xf, axis=-1, keepdims=True) + EPS)

def causal_dwconv_silu(x, w):
    k_w = w.shape[0]
    s = x.shape[1]
    xp = jnp.pad(x, ((0, 0), (k_w - 1, 0), (0, 0)))
    y = sum(xp[:, j:j + s] * w[j] for j in range(k_w))
    return jax.nn.silu(y)

def gated_delta_rule(q, k, v, g, beta):
    b, s, h, dk = q.shape
    n = s // CHUNK

    def to_chunks(t):
        return jnp.moveaxis(t.reshape((b, n, CHUNK) + t.shape[2:]), 3, 2)

    q, k, v, g, beta = map(to_chunks, (q * dk ** -0.5, k, v, g, beta))
    gc = jnp.cumsum(g, axis=-1)
    causal = jnp.tril(jnp.ones((CHUNK, CHUNK), dtype=bool))
    strict = jnp.tril(jnp.ones((CHUNK, CHUNK), dtype=bool), -1)
    decay = jnp.exp(jnp.where(causal, gc[..., :, None] - gc[..., None, :], -jnp.inf))
    k_beta = k * beta[..., None]
    v_beta = v * beta[..., None]
    lmat = jnp.where(strict, jnp.einsum('bnhcd,bnhed->bnhce', k_beta, k) * decay, 0.0)
    eye = jnp.eye(CHUNK, dtype=jnp.float32)
    t_inv = lax.linalg.triangular_solve(eye + lmat, jnp.broadcast_to(eye, lmat.shape),
                                        left_side=True, lower=True, unit_diagonal=True)
    u = jnp.einsum('bnhce,bnhed->bnhcd', t_inv, v_beta)
    w = jnp.einsum('bnhce,bnhed->bnhcd', t_inv, k_beta * jnp.exp(gc)[..., None])
    a_qk = jnp.einsum('bnhcd,bnhed->bnhce', q, k) * decay
    q_dec = q * jnp.exp(gc)[..., None]
    k_dec = k * jnp.exp(gc[..., -1:] - gc)[..., None]
    g_last = jnp.exp(gc[..., -1])

    def step(state, xs):
        q_c, k_c, u_c, w_c, a_c, gl = xs
        v_new = u_c - jnp.einsum('bhcd,bhde->bhce', w_c, state)
        o_c = jnp.einsum('bhcd,bhde->bhce', q_c, state) + jnp.einsum('bhce,bhed->bhcd', a_c, v_new)
        state = state * gl[..., None, None] + jnp.einsum('bhcd,bhce->bhde', k_c, v_new)
        return state, o_c

    xs = tuple(jnp.moveaxis(t, 1, 0) for t in (q_dec, k_dec, u, w, a_qk, g_last))
    state0 = jnp.zeros((b, h, dk, v.shape[-1]), jnp.float32)
    _, o = lax.scan(step, state0, xs)
    o = jnp.moveaxis(jnp.moveaxis(o, 0, 1), 2, 3)
    return o.reshape(b, s, h, -1)

def dilated_window_attention(q, k, v, window, dilation):
    b, s, h, dh = q.shape
    n_back = window // dilation
    sub_len = s // dilation
    nb = -(-sub_len // ATTN_BLOCK)
    lp = nb * ATTN_BLOCK
    bb = b * dilation

    def to_sub(t):
        t = t.reshape(b, sub_len, dilation, h, dh).transpose(0, 2, 1, 3, 4).reshape(bb, sub_len, h, dh)
        return jnp.pad(t, ((0, 0), (0, lp - sub_len), (0, 0), (0, 0)))

    def band(t):
        tp = jnp.pad(t, ((0, 0), (ATTN_BLOCK, 0), (0, 0), (0, 0))).reshape(bb, nb + 1, ATTN_BLOCK, h, dh)
        return jnp.concatenate([tp[:, :-1], tp[:, 1:]], axis=2)

    qb = to_sub(q).reshape(bb, nb, ATTN_BLOCK, h, dh)
    kb = band(to_sub(k))
    vb = band(to_sub(v))
    scores = jnp.einsum('bnqhd,bnkhd->bnhqk', qb, kb,
                        preferred_element_type=jnp.float32) * (dh ** -0.5)
    blk = jnp.arange(nb)[:, None, None]
    qpos = blk * ATTN_BLOCK + jnp.arange(ATTN_BLOCK)[None, :, None]
    kpos = (blk - 1) * ATTN_BLOCK + jnp.arange(2 * ATTN_BLOCK)[None, None, :]
    dist = qpos - kpos
    mask = (dist >= 0) & (dist <= n_back) & (kpos >= 0)
    scores = jnp.where(mask[None, :, None], scores, -jnp.inf)
    m = jnp.max(scores, axis=-1, keepdims=True)
    p = jnp.exp(scores - m)
    denom = jnp.sum(p, axis=-1, keepdims=True)
    o = jnp.einsum('bnhqk,bnkhd->bnqhd', (p / denom).astype(v.dtype), vb)
    lse = (m + jnp.log(denom))[..., 0]
    o = o.reshape(bb, lp, h, dh)[:, :sub_len]
    o = o.reshape(b, dilation, sub_len, h, dh).transpose(0, 2, 1, 3, 4).reshape(b, s, h, dh)
    lse = lse.transpose(0, 1, 3, 2).reshape(bb, lp, h)[:, :sub_len]
    lse = lse.reshape(b, dilation, sub_len, h).transpose(0, 2, 1, 3).reshape(b, s, h)
    return o, lse

def second_inputs(seed: int = 0) -> dict:
    key = jax.random.key(seed)
    ks = jax.random.split(key, 16)
    f32 = jnp.float32
    d = D_MODEL
    x = jax.random.normal(ks[0], (BATCH, SEQ, d), f32)
    c = jax.random.normal(ks[1], (BATCH, d), f32)
    norm_w = 1.0 + 0.02 * jax.random.normal(ks[2], (DEPTH_2, d), f32)
    ada_w = jax.random.normal(ks[3], (DEPTH_2, d, 3 * d), f32) * d ** -0.5
    ada_b = 0.01 * jax.random.normal(ks[4], (DEPTH_2, 3 * d), f32)
    w_in = jax.random.normal(ks[5], (DEPTH_2, d, N_IN), f32) * d ** -0.5
    conv_w = jax.random.normal(ks[6], (DEPTH_2, CONV_K, 2 * DN_QK_WIDTH + DN_WIDTH), f32) * CONV_K ** -0.5
    a_log = jnp.log(jax.random.uniform(ks[7], (DEPTH_2, DN_HEADS), f32, 1.0, 16.0))
    dt = jnp.exp(jax.random.uniform(ks[8], (DEPTH_2, DN_HEADS), f32, np.log(1e-3), np.log(1e-1)))
    dt_bias = dt + jnp.log(-jnp.expm1(-dt))
    dn_norm_w = 1.0 + 0.02 * jax.random.normal(ks[9], (DEPTH_2, DN_DV), f32)
    w_proj_a = jax.random.normal(ks[10], (DEPTH_2, DN_WIDTH, d), f32) * DN_WIDTH ** -0.5
    w_proj_b = jax.random.normal(ks[11], (DEPTH_2, ATTN_WIDTH, d), f32) * ATTN_WIDTH ** -0.5
    w_out = jax.random.normal(ks[12], (DEPTH_2, d, d), f32) * d ** -0.5
    final_norm_w = 1.0 + 0.02 * jax.random.normal(ks[13], (d,), f32)
    return {"x": x, "c": c, "norm_w": norm_w, "ada_w": ada_w, "ada_b": ada_b, "w_in": w_in,
            "conv_w": conv_w, "a_log": a_log, "dt_bias": dt_bias, "dn_norm_w": dn_norm_w,
            "w_proj_a": w_proj_a, "w_proj_b": w_proj_b, "w_out": w_out, "final_norm_w": final_norm_w}

def second_block(x, c, norm_w, ada_w, ada_b, w_in, conv_w, a_log, dt_bias, dn_norm_w,
              w_proj_a, w_proj_b, w_out, final_norm_w):
    b, s, _ = x.shape
    split_points = [int(p) for p in np.cumsum(IN_SPLITS)[:-1]]
    for l in range(DEPTH_2):
        mod = jax.nn.silu(c) @ ada_w[l] + ada_b[l]
        shift, scale, gate = jnp.split(mod, 3, axis=-1)
        h = rms_norm_2(x, norm_w[l]) * (1.0 + scale[:, None]) + shift[:, None]
        proj = h @ w_in[l]
        (qa, ka, va, za, beta_in, a_in, qb, kb, vb, zb, ga, gb) = jnp.split(proj, split_points, axis=-1)

        qkv = causal_dwconv_silu(jnp.concatenate([qa, ka, va], axis=-1), conv_w[l])
        qa, ka, va = jnp.split(qkv, [DN_QK_WIDTH, 2 * DN_QK_WIDTH], axis=-1)
        q_dn = l2_normalize(qa.reshape(b, s, DN_HEADS, DN_DK))
        k_dn = l2_normalize(ka.reshape(b, s, DN_HEADS, DN_DK))
        v_dn = va.reshape(b, s, DN_HEADS, DN_DV).astype(jnp.float32)
        beta = jax.nn.sigmoid(beta_in.astype(jnp.float32))
        g = -jnp.exp(a_log[l].astype(jnp.float32)) * jax.nn.softplus(
            a_in.astype(jnp.float32) + dt_bias[l].astype(jnp.float32))
        o_a = gated_delta_rule(q_dn, k_dn, v_dn, g, beta).astype(x.dtype)
        y_a = rms_norm_2(o_a, dn_norm_w[l]).reshape(b, s, DN_WIDTH) * jax.nn.silu(za)
        y_a = y_a @ w_proj_a[l]

        qb = qb.reshape(b, s, ATTN_HEADS, ATTN_HEAD_DIM)
        kb = kb.reshape(b, s, ATTN_HEADS, ATTN_HEAD_DIM)
        vb = vb.reshape(b, s, ATTN_HEADS, ATTN_HEAD_DIM)
        outs, lses = [], []
        for gi, (win, dil) in enumerate(DIL_CONFIGS):
            hs = slice(gi * HEADS_PER_GROUP, (gi + 1) * HEADS_PER_GROUP)
            o_g, lse_g = dilated_window_attention(qb[:, :, hs], kb[:, :, hs], vb[:, :, hs], win, dil)
            outs.append(o_g)
            lses.append(lse_g)
        o_b = jnp.stack(outs, axis=2)
        w_g = jax.nn.softmax(jnp.stack(lses, axis=2), axis=2)
        y_b = (o_b * w_g[..., None].astype(o_b.dtype)).reshape(b, s, ATTN_WIDTH) * jax.nn.silu(zb)
        y_b = y_b @ w_proj_b[l]

        merged = jax.nn.sigmoid(ga) * y_a + jax.nn.sigmoid(gb) * y_b
        x = x + gate[:, None] * (merged @ w_out[l])
    return rms_norm_2(x, final_norm_w)


def setup_inputs(seed=0):
    out = dict(first_inputs(seed))
    for name, value in second_inputs(seed + 1).items():
        if name != "x":
            out[name + "_2"] = value
    return out


def reference(
    x, c, ctx, c_ctx, ada_w, ada_b, norm_mix_w, norm_ffn_w, ev_w_in, ev_lb_logits, ev_onorm_w,
    ev_vnorm_w, ev_ws, ev_bs, ev_w_out, od_w_in, od_qa_norm_w, od_w_qb, od_kva_norm_w, od_w_kvb,
    od_q_norm_w, od_k_norm_w, od_w_out, ffn_w_up, ffn_conv_w, ffn_conv_b, ffn_w_down, c_2,
    norm_w_2, ada_w_2, ada_b_2, w_in_2, conv_w_2, a_log_2, dt_bias_2, dn_norm_w_2, w_proj_a_2,
    w_proj_b_2, w_out_2, final_norm_w_2,
):
    x = first_block(
        x, c, ctx, c_ctx, ada_w, ada_b, norm_mix_w, norm_ffn_w, ev_w_in, ev_lb_logits,
        ev_onorm_w, ev_vnorm_w, ev_ws, ev_bs, ev_w_out, od_w_in, od_qa_norm_w, od_w_qb,
        od_kva_norm_w, od_w_kvb, od_q_norm_w, od_k_norm_w, od_w_out, ffn_w_up, ffn_conv_w,
        ffn_conv_b, ffn_w_down,
    )
    return second_block(
        x, c_2, norm_w_2, ada_w_2, ada_b_2, w_in_2, conv_w_2, a_log_2, dt_bias_2, dn_norm_w_2,
        w_proj_a_2, w_proj_b_2, w_out_2, final_norm_w_2,
    )


_drawn_inputs = setup_inputs


def setup_inputs(seed=0):
    import zlib

    import numpy as np

    out = dict(_drawn_inputs(seed))
    spreads = {}
    factors = {'ctx': 6.292,
     'norm_mix_w': 7.522,
     'norm_ffn_w': 6.319,
     'ev_onorm_w': 8.0,
     'ev_vnorm_w': 8.0,
     'ev_bs': 3.466,
     'od_qa_norm_w': 8.0,
     'od_w_qb': 2.769,
     'od_kva_norm_w': 8.0,
     'od_q_norm_w': 8.0,
     'od_k_norm_w': 8.0,
     'ffn_conv_b': 8.0,
     'norm_w_2': 7.359,
     'ada_b_2': 8.0,
     'a_log_2': 2.986,
     'dn_norm_w_2': 8.0,
     'final_norm_w_2': 2.781}
    for name, (base, spread) in spreads.items():
        noise = np.random.default_rng([zlib.crc32(name.encode()), seed]).standard_normal(out[name].shape)
        drawn = base * np.exp(spread * noise) if base else spread * noise
        out[name] = jnp.asarray(drawn.astype(out[name].dtype))
    for name, factor in factors.items():
        out[name] = (out[name] * factor).astype(out[name].dtype)
    return out
```

```python
import concourse.bass as bass
from concourse import mybir
from contextlib import ExitStack, contextmanager

F32 = mybir.dt.float32
F32R = mybir.dt.float32r
ALU = mybir.AluOpType
ACT = mybir.ActivationFunctionType
AX = mybir.AxisListType

P = 128
D = 1024
DT = D // P
CTX = 256
LAT = 512
TOK = CTX + LAT
CHUNK = 128
EPS = 1e-6
F_MIN = 1e-6
D_FF = 2816
FT = D_FF // P
FH = FT // 2
RING_W = FH * P


class Core:

    def __init__(self, nc, ctx):
        self.nc = nc
        self.ctx = ctx
        self.spent = []
        self.names = 0
        self.raw = self.keep("w_raw", [P, 2, RING_W])
        self.whi = self.keep("w_hi", [P, 2, RING_W], F32R)
        self.wlo = self.keep("w_lo", [P, 2, RING_W], F32R)
        self.w_loaded = [ctx.enter_context(nc.semaphore(f"w_loaded{j}")) for j in range(2)]
        self.loads = [0, 0]

    def keep(self, name, shape, dt=F32):
        return self.ctx.enter_context(self.nc.sbuf_tensor(name, shape, dt))

    def signals(self, stage, names):
        new = [self.nc.alloc_semaphore(f"{stage}_{n}") for n in names.split()]
        if self.spent:
            self.nc.clear_and_free_semaphores(self.spent)
        self.spent = new
        return new

    def load_weights(self, sp, w, kt, i, j):
        sp.dma_start(self.raw[:, j, 0:kt * P], w[bass.ds(i * P, P), :]).then_inc(self.w_loaded[j], 16)

    def preload(self, sp, nxt):
        if nxt is None:
            return
        w, kt = nxt
        for j in range(2):
            self.load_weights(sp, w, kt, j, j)
            self.loads[j] += 1


def tile_pairs(eng, n, body):
    pairs = n // 2

    def pair(ip, first, last):
        for j in range(2):
            body(ip, j, 2 * ip + j, first, not (last and j == 1 and n % 2 == 0))

    pair(0, True, pairs == 1)
    if pairs > 4:
        with eng.Fori(1, pairs - 1) as ip:
            pair(ip, False, False)
    else:
        for ip in range(1, pairs - 1):
            pair(ip, False, False)
    if pairs > 1:
        pair(pairs - 1, False, True)
    if n % 2:
        body(pairs, 0, n - 1, False, False)


class Product:
    pass


def product(K, name, w, n, kt, rhs_hi, rhs_lo, t0, T, evac_act, evac_dve, nxt, extra=""):
    nc = K.nc
    with ExitStack() as c:
        acc = [c.enter_context(nc.psum_tensor(f"{name}_acc{j}", [P, 1024], F32)) for j in range(2)]
        hi_done, lo_done, mm_done, free0, free1, *more = K.signals(
            name, "hi_done lo_done mm_done free0 free1 " + extra)
        free = [free0, free1]
        g = Product()
        g.free, g.mm_done, g.more = free, mm_done, more
        g.out = [a[:, 1024 - T:1024] for a in acc]
        banks = [(1024 - T, T - LAT), (512, LAT)] if T > LAT else [(512, T)]
        base = [16 * x for x in K.loads]

        def slot_width():
            return kt * P

        with nc.Block() as block:
            @block.sync
            def _(sp):
                def load(ip, j, i, first, has_next):
                    if not first:
                        sp.wait_ge(hi_done, i - 1)
                        sp.wait_ge(lo_done, i - 1)
                        K.load_weights(sp, w, kt, i, j)
                tile_pairs(sp, n, load)
                if nxt is not None:
                    sp.wait_ge(hi_done, n)
                    sp.wait_ge(lo_done, n)
                K.loads[0] += (n + 1) // 2 - 1
                K.loads[1] += n // 2 - 1
                K.preload(sp, nxt)

            @block.scalar
            def _(act):
                def split_hi(ip, j, i, first):
                    act.wait_ge(K.w_loaded[j], 16 * ip + base[j])
                    if not first:
                        act.wait_ge(mm_done, i - 1)
                    nc.scalar.activation(K.whi[:, j, 0:slot_width()], K.raw[:, j, 0:slot_width()],
                                         ACT.Copy).then_inc(hi_done, 1)

                def step(ip, j, i, first, has_next):
                    if has_next:
                        split_hi(ip + j, 1 - j, i + 1, first and j == 0)
                    evac_act(act, g, ip, j, i, first)
                split_hi(0, 0, 0, True)
                tile_pairs(act, n, step)

            @block.vector
            def _(dve):
                def split_lo(ip, j, i, first):
                    dve.wait_ge(hi_done, i + 1)
                    if not first:
                        dve.wait_ge(mm_done, i - 1)
                    nc.vector.tensor_tensor(K.wlo[:, j, 0:slot_width()], K.raw[:, j, 0:slot_width()],
                                            K.whi[:, j, 0:slot_width()].bitcast(F32),
                                            ALU.subtract).then_inc(lo_done, 1)

                def step(ip, j, i, first, has_next):
                    if has_next:
                        split_lo(ip + j, 1 - j, i + 1, first and j == 0)
                    evac_dve(dve, g, ip, j, i, first)
                split_lo(0, 0, 0, True)
                tile_pairs(dve, n, step)

            @block.tensor
            def _(pe):
                def multiply(ip, j, i, first, has_next):
                    pe.wait_ge(lo_done, i + 1)
                    if not first:
                        pe.wait_ge(free[j], ip)
                    for col, width in banks:
                        at = col - (1024 - T)
                        for k in range(kt):
                            cols = slice(k * P, (k + 1) * P)
                            for part, (a, b) in enumerate(
                                    [(K.whi, rhs_hi), (K.whi, rhs_lo), (K.wlo, rhs_hi)]):
                                last = nc.tensor.matmul(
                                    acc[j][:, col:col + width], a[:, j, cols],
                                    b[:, k, t0 + at:t0 + at + width],
                                    start=(k == 0 and part == 0), stop=(k == kt - 1 and part == 2))
                    last.then_inc(mm_done, 1)
                tile_pairs(pe, n, multiply)


def no_evac(eng, g, ip, j, i, first):
    pass


def copy_out(K, dst, func, tile0=0):
    def evac(act, g, ip, j, i, first):
        act.wait_ge(g.mm_done, i + 1)
        T = dst.shape[2]
        K.nc.scalar.activation(dst[:, bass.ds(i + tile0, 1), :].rearrange("p a t -> p (a t)"), g.out[j],
                               func).then_inc(g.free[j], 1)
    return evac


def add_gated(K, x, segs, t0):
    def evac(dve, g, ip, j, i, first):
        dve.wait_ge(g.mm_done, i + 1)
        for a, b, gate in segs:
            xs = x[:, bass.ds(i, 1), a:b].rearrange("p a t -> p (a t)")
            last = K.nc.vector.scalar_tensor_tensor(
                out=xs, in0=g.out[j][:, a - t0:b - t0], scalar=gate[:, bass.ds(i, 1)], in1=xs,
                op0=ALU.mult, op1=ALU.add)
        last.then_inc(g.free[j], 1)
    return evac


def split_parts(K, name, src, hi, lo):
    nc = K.nc
    hi_done, lo_done = K.signals(name, "hi_done lo_done")
    n = src.shape[1]
    half = (n + 1) // 2
    parts = [(0, half), (half, n)]
    with nc.Block() as block:
        @block.scalar
        def _(act):
            for a, b in parts:
                nc.scalar.activation(hi[:, a:b, :], src[:, a:b, :], ACT.Copy).then_inc(hi_done, 1)

        @block.vector
        def _(dve):
            for m, (a, b) in enumerate(parts):
                dve.wait_ge(hi_done, m + 1)
                nc.vector.tensor_tensor(lo[:, a:b, :], src[:, a:b, :], hi[:, a:b, :].bitcast(F32),
                                        ALU.subtract)


def model_norm(K, name, x, t0, T, mods, hi=None, lo=None, plain=None, work=None):
    nc = K.nc
    H = DT // 2
    with ExitStack() as c:
        if work is None:
            work = c.enter_context(nc.sbuf_tensor(f"{name}_work", [P, DT, T], F32))
        sums = c.enter_context(nc.sbuf_tensor(f"{name}_sums", [P, 2, T], F32))
        root = c.enter_context(nc.sbuf_tensor(f"{name}_root", [P, T], F32))
        rstd = c.enter_context(nc.sbuf_tensor(f"{name}_rstd", [P, T], F32))
        ps = c.enter_context(nc.psum_tensor(f"{name}_ps", [P, 1024], F32))
        squared, summed, total, rooted, inv, scaled, shifted, hi_done = K.signals(
            name, "squared summed total rooted inv scaled shifted hi_done")
        banks = [(1024 - T, T - LAT), (512, LAT)] if T > LAT else [(512, T)]
        with nc.Block() as block:
            @block.scalar
            def _(act):
                for s in range(2):
                    nc.scalar.activation(work[:, s * H:(s + 1) * H, :], x[:, s * H:(s + 1) * H, t0:t0 + T],
                                         ACT.Square).then_inc(squared, 1)
                act.wait_ge(total, 1)
                nc.scalar.activation(root[:, :], ps[:, 1024 - T:1024], ACT.Sqrt, bias=K.eps[:, 0:1],
                                     scale=1.0 / D).then_inc(rooted, 1)
                if hi is not None:
                    for s in range(2):
                        act.wait_ge(shifted, s + 1)
                        nc.scalar.activation(hi[:, s * H:(s + 1) * H, :], work[:, s * H:(s + 1) * H, :],
                                             ACT.Copy).then_inc(hi_done, 1)

            @block.tensor
            def _(pe):
                pe.wait_ge(summed, 2)
                for col, width in banks:
                    at = col - (1024 - T)
                    for s in range(2):
                        last = nc.tensor.matmul(ps[:, col:col + width], K.ones[:, :],
                                                sums[:, s, at:at + width], start=(s == 0), stop=(s == 1))
                last.then_inc(total, 1)

            @block.vector
            def _(dve):
                for s in range(2):
                    dve.wait_ge(squared, s + 1)
                    nc.vector.tensor_reduce(sums[:, s, :],
                                            work[:, s * H:(s + 1) * H, :].rearrange("p k t -> p t k"),
                                            AX.X, ALU.add).then_inc(summed, 1)
                dve.wait_ge(rooted, 1)
                nc.vector.reciprocal(rstd[:, :], root[:, :]).then_inc(inv, 1)
                dve.wait_ge(inv, 1)
                for s in range(2):
                    nc.vector.tensor_tensor(work[:, s * H:(s + 1) * H, :], x[:, s * H:(s + 1) * H, t0:t0 + T],
                                            rstd[:, :].unsqueeze(1).to_broadcast([P, H, T]),
                                            ALU.mult).then_inc(scaled, 1)
                dst = work if plain is None else plain
                for s in range(2):
                    dve.wait_ge(scaled, s + 1)
                    for k in range(s * H, (s + 1) * H):
                        for a, b, scale, shift in mods:
                            if shift is None:
                                last = nc.vector.tensor_scalar(dst[:, k, a:b], work[:, k, a:b],
                                                               scale[:, k:k + 1], None, ALU.mult)
                            else:
                                last = nc.vector.tensor_scalar(dst[:, k, a:b], work[:, k, a:b],
                                                               scale[:, k:k + 1], shift[:, k:k + 1],
                                                               ALU.mult, ALU.add)
                    last.then_inc(shifted, 1)
                if hi is not None:
                    for s in range(2):
                        dve.wait_ge(hi_done, s + 1)
                        nc.vector.tensor_tensor(lo[:, s * H:(s + 1) * H, :], work[:, s * H:(s + 1) * H, :],
                                                hi[:, s * H:(s + 1) * H, :].bitcast(F32), ALU.subtract)


def group_norm(K, name, src, dst, n, kt, T, weights, ones, scale):
    nc = K.nc
    with ExitStack() as c:
        sq = c.enter_context(nc.sbuf_tensor(f"{name}_sq", [P, 2, kt, T], F32))
        root = c.enter_context(nc.sbuf_tensor(f"{name}_root", [P, 2, T], F32))
        ps = [c.enter_context(nc.psum_tensor(f"{name}_ps{j}", [P, 1024], F32)) for j in range(2)]
        squared, total, rooted, inv, done = K.signals(name, "squared total rooted inv done")
        banks = [(1024 - T, T - LAT), (512, LAT)] if T > LAT else [(512, T)]

        def group(t, i):
            return t[:, bass.ds(i * kt, kt), :]

        def turns(eng, body):
            if n > 4 and n % 2 == 0:
                for j in range(2):
                    body(0, j, j, True)
                with eng.Fori(1, n // 2) as ip:
                    for j in range(2):
                        body(ip, j, 2 * ip + j, False)
            else:
                for i in range(n):
                    body(i // 2, i % 2, i, i < 2)

        with nc.Block() as block:
            @block.scalar
            def _(act):
                def body(ip, j, i, first):
                    if not first:
                        act.wait_ge(total, i - 1)
                    nc.scalar.activation(sq[:, j], group(src, i), ACT.Square).then_inc(squared, 1)
                    act.wait_ge(total, i + 1)
                    if not first:
                        act.wait_ge(done, i - 1)
                    nc.scalar.activation(root[:, j, :], ps[j][:, 1024 - T:1024], ACT.Sqrt,
                                         bias=K.eps[:, 0:1], scale=scale).then_inc(rooted, 1)
                turns(act, body)

            @block.tensor
            def _(pe):
                def body(ip, j, i, first):
                    pe.wait_ge(squared, i + 1)
                    if not first:
                        pe.wait_ge(rooted, i - 1)
                    for col, width in banks:
                        at = col - (1024 - T)
                        for k in range(kt):
                            last = nc.tensor.matmul(ps[j][:, col:col + width], ones[:, :],
                                                    sq[:, j, k, at:at + width],
                                                    start=(k == 0), stop=(k == kt - 1))
                    last.then_inc(total, 1)
                turns(pe, body)

            @block.vector
            def _(dve):
                def body(ip, j, i, first):
                    dve.wait_ge(rooted, i + 1)
                    nc.vector.reciprocal(root[:, j, :], root[:, j, :]).then_inc(inv, 1)
                    dve.wait_ge(inv, i + 1)
                    for k in range(kt):
                        s = src[:, bass.ds(i * kt + k, 1), :].rearrange("p a t -> p (a t)")
                        d = dst[:, bass.ds(i * kt + k, 1), :].rearrange("p a t -> p (a t)")
                        if weights is None:
                            last = nc.vector.tensor_tensor(d, s, root[:, j, :], ALU.mult)
                        else:
                            last = nc.vector.scalar_tensor_tensor(
                                out=d, in0=s, scalar=weights[:, bass.ds(i * kt + k, 1)],
                                in1=root[:, j, :], op0=ALU.mult, op1=ALU.mult)
                    last.then_inc(done, 1)
                turns(dve, body)


def modulation(K, name, w, n, cols, vecs, bias, mod, nxt):
    nc = K.nc
    with ExitStack() as c:
        ps = [c.enter_context(nc.psum_tensor(f"{name}_ps{j}", [P, 512], F32)) for j in range(2)]
        mm_done, taken, biased = K.signals(name, "mm_done taken biased")
        base = [16 * x for x in K.loads]
        with nc.Block() as block:
            @block.sync
            def _(sp):
                def load(ip, j, i, first, has_next):
                    if not first:
                        sp.wait_ge(mm_done, i - 1)
                        K.load_weights(sp, w, DT, i, j)
                tile_pairs(sp, n, load)
                sp.wait_ge(mm_done, n)
                for j in range(2):
                    K.loads[j] += n // 2 - 1
                K.preload(sp, nxt)

            @block.tensor
            def _(pe):
                def multiply(ip, j, i, first, has_next):
                    pe.wait_ge(K.w_loaded[j], 16 * ip + base[j])
                    if not first:
                        pe.wait_ge(taken, i - 1)
                    for k in range(DT):
                        last = nc.tensor.matmul(ps[j][:, 0:vecs], K.raw[:, j, k * P:(k + 1) * P],
                                                cols[:, k, 0:vecs], start=(k == 0), stop=(k == DT - 1))
                    last.then_inc(mm_done, 1)
                tile_pairs(pe, n, multiply)

            @block.vector
            def _(dve):
                def take(ip, j, i, first, has_next):
                    dve.wait_ge(mm_done, i + 1)
                    nc.vector.tensor_copy(mod[:, bass.ds(i, 1), 0:vecs].rearrange("p a v -> p (a v)"),
                                          ps[j][:, 0:vecs]).then_inc(taken, 1)
                tile_pairs(dve, n, take)
                dve.wait_ge(taken, n)
                nc.vector.tensor_tensor(mod[:, :, 0:vecs], mod[:, :, 0:vecs],
                                        bias[:, :].unsqueeze(2).to_broadcast([P, n, vecs]), ALU.add)


def norm_scales(K, name, pairs):
    nc = K.nc
    one_more, = K.signals(name, "one_more")
    with nc.Block() as block:
        @block.vector
        def _(dve):
            for n, (out, norm_w, scale) in enumerate(pairs):
                nc.vector.tensor_scalar(out, scale, 1.0, None, ALU.add).then_inc(one_more, 1)
            for n, (out, norm_w, scale) in enumerate(pairs):
                dve.wait_ge(one_more, n + 1)
                nc.vector.tensor_tensor(out, out, norm_w, ALU.mult)


def feed_forward(K, name, x, t0, T, hi, lo, w_up, w_down, conv_w, conv_b, gates, nxt):
    nc = K.nc
    segs = [(0, CTX), (CTX, TOK)] if T > LAT else [(0, LAT)]
    with ExitStack() as c:
        hid_hi = c.enter_context(nc.sbuf_tensor(f"{name}_hid_hi", [P, FH, T], F32R))
        hid_lo = c.enter_context(nc.sbuf_tensor(f"{name}_hid_lo", [P, FH, T], F32R))
        for f in range(2):
            with ExitStack() as c2:
                gate_sb = c2.enter_context(nc.sbuf_tensor(f"{name}{f}_gate", [P, T], F32))
                conv = c2.enter_context(nc.sbuf_tensor(f"{name}{f}_conv", [P, T], F32))
                hid = c2.enter_context(nc.sbuf_tensor(f"{name}{f}_hid", [P, T], F32))

                def act_part(act, g, ip, j, i, first):
                    conv0, conv1, conv2, silu_done, hid_done, hi_out = g.more
                    act.wait_ge(g.mm_done, i + 1)
                    if j == 0:
                        if not first:
                            act.wait_ge(conv2, ip)
                        nc.scalar.activation(gate_sb[:, :], g.out[0], ACT.Copy).then_inc(g.free[0], 1)
                        act.wait_ge(conv2, ip + 1)
                        nc.scalar.activation(conv[:, :], conv[:, :], ACT.Silu).then_inc(silu_done, 1)
                    else:
                        act.wait_ge(g.free[1], ip + 1)
                        nc.scalar.activation(hid_hi[:, bass.ds(ip, 1), :].rearrange("p a t -> p (a t)"),
                                             hid[:, :], ACT.Copy).then_inc(hi_out, 1)

                def dve_part(dve, g, ip, j, i, first, f=f):
                    conv0, conv1, conv2, silu_done, hid_done, hi_out = g.more
                    if j == 0:
                        def tap(m):
                            return conv_w[:, bass.ds((ip + f * FH) * 3 + m, 1)]
                        dve.wait_ge(g.free[0], ip + 1)
                        if not first:
                            dve.wait_ge(g.free[1], ip)
                        nc.vector.tensor_scalar(conv[:, :], gate_sb[:, :], tap(1),
                                                conv_b[:, bass.ds(ip + f * FH, 1)],
                                                ALU.mult, ALU.add).then_inc(conv0, 1)
                        dve.wait_ge(conv0, ip + 1)
                        for a, b in segs:
                            last = nc.vector.scalar_tensor_tensor(
                                out=conv[:, a + 1:b], in0=gate_sb[:, a:b - 1], scalar=tap(0),
                                in1=conv[:, a + 1:b], op0=ALU.mult, op1=ALU.add)
                        last.then_inc(conv1, 1)
                        dve.wait_ge(conv1, ip + 1)
                        for a, b in segs:
                            last = nc.vector.scalar_tensor_tensor(
                                out=conv[:, a:b - 1], in0=gate_sb[:, a + 1:b], scalar=tap(2),
                                in1=conv[:, a:b - 1], op0=ALU.mult, op1=ALU.add)
                        last.then_inc(conv2, 1)
                    else:
                        dve.wait_ge(g.mm_done, i + 1)
                        dve.wait_ge(silu_done, ip + 1)
                        if not first:
                            dve.wait_ge(hid_done, ip)
                        nc.vector.tensor_tensor(hid[:, :], conv[:, :], g.out[1],
                                                ALU.mult).then_inc(g.free[1], 1)
                        dve.wait_ge(hi_out, ip + 1)
                        h = bass.ds(ip, 1)
                        nc.vector.tensor_tensor(hid_lo[:, h, :].rearrange("p a t -> p (a t)"), hid[:, :],
                                                hid_hi[:, h, :].rearrange("p a t -> p (a t)").bitcast(F32),
                                                ALU.subtract).then_inc(hid_done, 1)

                product(K, f"{name}_up{f}", w_up[f * 2 * FH * P:(f + 1) * 2 * FH * P, :], 2 * FH, DT, hi, lo,
                        0, T, act_part, dve_part, (w_down[f * DT * P:(f + 1) * DT * P, :], FH),
                        "conv0 conv1 conv2 silu_done hid_done hi_out")
            after = (w_up[2 * FH * P:4 * FH * P, :], DT) if f == 0 else nxt
            product(K, f"{name}_down{f}", w_down[f * DT * P:(f + 1) * DT * P, :], DT, FH, hid_hi, hid_lo,
                    0, T, no_evac, add_gated(K, x, gates, t0), after)


A_HEADS = 4
B_GROUPS = 4
LEVELS = (128, 64, 32, 16, 8)


def chunk_mlp(K, uv, ws_t, bs_row, out):
    nc = K.nc
    n_chunks = TOK // CHUNK
    with ExitStack() as c:
        ws = c.enter_context(nc.sbuf_tensor("cm_ws", [P, B_GROUPS * CHUNK], F32))
        bs = c.enter_context(nc.sbuf_tensor("cm_bs", [1, B_GROUPS * CHUNK], F32))
        vt = c.enter_context(nc.sbuf_tensor("cm_vt", [P, 2, B_GROUPS * P], F32))
        ps_t = [c.enter_context(nc.psum_tensor(f"cm_ps_t{j}", [P, 512], F32)) for j in range(2)]
        ps_s = [c.enter_context(nc.psum_tensor(f"cm_ps_s{j}", [P, 512], F32)) for j in range(2)]
        loaded, turned, vt_ready, mixed, gated = K.signals("cm", "loaded turned vt_ready mixed gated")
        with nc.Block() as block:
            @block.sync
            def _(sp):
                sp.dma_start(ws[:, :], ws_t).then_inc(loaded, 16)
                sp.dma_start(bs[:, :], bs_row).then_inc(loaded, 16)

            @block.tensor
            def _(pe):
                pe.wait_ge(loaded, 32)

                def turn(n):
                    if n >= 2:
                        pe.wait_ge(vt_ready, n - 1)
                    for g in range(B_GROUPS):
                        last = nc.tensor.transpose(ps_t[n % 2][:, g * P:(g + 1) * P],
                                                   uv[:, B_GROUPS + g, n * CHUNK:(n + 1) * CHUNK], K.ident[:, :])
                    last.then_inc(turned, 1)

                def mix(n):
                    pe.wait_ge(vt_ready, n + 1)
                    if n >= 2:
                        pe.wait_ge(gated, n - 1)
                    for g in range(B_GROUPS):
                        cols = slice(g * P, (g + 1) * P)
                        nc.tensor.matmul(ps_s[n % 2][:, cols], vt[:, n % 2, cols], ws[:, cols],
                                         start=True, stop=False)
                        last = nc.tensor.matmul(ps_s[n % 2][:, cols], K.ones[0:1, :], bs[:, cols],
                                                start=False, stop=True)
                    last.then_inc(mixed, 1)
                turn(0)
                for n in range(n_chunks):
                    if n + 1 < n_chunks:
                        turn(n + 1)
                    mix(n)

            @block.scalar
            def _(act):
                for n in range(n_chunks):
                    act.wait_ge(turned, n + 1)
                    if n >= 2:
                        act.wait_ge(mixed, n - 1)
                    nc.scalar.activation(vt[:, n % 2, :], ps_t[n % 2][:, :], ACT.Copy).then_inc(vt_ready, 1)

            @block.vector
            def _(dve):
                for n in range(n_chunks):
                    dve.wait_ge(mixed, n + 1)
                    nc.vector.tensor_tensor(out[:, :, n * CHUNK:(n + 1) * CHUNK],
                                            uv[:, 0:B_GROUPS, n * CHUNK:(n + 1) * CHUNK],
                                            ps_s[n % 2][:, :].rearrange("p (g t) -> p g t", g=B_GROUPS),
                                            ALU.mult).then_inc(gated, 1)


def gla_features(K, zf, kf, lb_cols):
    nc = K.nc
    n_dir = 2 * A_HEADS
    with ExitStack() as c:
        lb = c.enter_context(nc.sbuf_tensor("gf_lb", [P, 5, n_dir], F32))
        keep = c.enter_context(nc.sbuf_tensor("gf_keep", [P, 2, TOK], F32))
        logits_up, e_done, p_inv, p_done, lb_done, sig, f1, f2, k_done, logs, marks, one_minus = K.signals(
            "gf", "logits_up e_done p_inv p_done lb_done sig f1 f2 k_done logs marks one_minus")
        with nc.Block() as block:
            @block.scalar
            def _(act):
                for s in range(2):
                    nc.scalar.activation(zf[:, s * A_HEADS:(s + 1) * A_HEADS, :],
                                         zf[:, s * A_HEADS:(s + 1) * A_HEADS, :], ACT.Sigmoid).then_inc(sig, 1)
                act.wait_ge(logits_up, 1)
                nc.scalar.activation(lb[:, 1, :], lb[:, 0, :], ACT.Exp).then_inc(e_done, 1)
                for s in range(2):
                    act.wait_ge(k_done, s + 1)
                    nc.scalar.activation(zf[:, s * A_HEADS:(s + 1) * A_HEADS, :],
                                         zf[:, s * A_HEADS:(s + 1) * A_HEADS, :], ACT.Ln).then_inc(logs, 1)

            @block.vector
            def _(dve):
                nc.vector.tensor_tensor(lb[:, 0, :], lb_cols, lb_cols, ALU.subtract).then_inc(logits_up, 1)
                nc.vector.memset(keep[:, :, :], 1.0).then_inc(marks, 1)
                dve.wait_ge(marks, 1)
                nc.vector.memset(keep[:, 0, 0:TOK:CHUNK], 0.0)
                nc.vector.memset(keep[:, 1, CHUNK - 1:TOK:CHUNK], 0.0).then_inc(marks, 1)
                dve.wait_ge(e_done, 1)
                nc.vector.reciprocal(lb[:, 2, :], lb[:, 1, :]).then_inc(p_inv, 1)
                dve.wait_ge(p_inv, 1)
                nc.vector.tensor_tensor(lb[:, 2, :], lb[:, 1, :], lb[:, 2, :], ALU.mult).then_inc(p_done, 1)
                dve.wait_ge(p_done, 1)
                nc.vector.tensor_tensor(lb[:, 3, :], lb[:, 2, :], lb[:, 2, :], ALU.subtract).then_inc(lb_done, 1)
                dve.wait_ge(lb_done, 1)
                nc.vector.tensor_scalar(lb[:, 4, :], lb[:, 3, :], -1.0, 1.0, ALU.mult, ALU.add).then_inc(one_minus, 1)
                dve.wait_ge(one_minus, 1)
                for s in range(2):
                    rows = slice(s * A_HEADS, (s + 1) * A_HEADS)
                    dve.wait_ge(sig, s + 1)
                    for m in range(s * A_HEADS, (s + 1) * A_HEADS):
                        last = nc.vector.tensor_scalar(zf[:, m, :], zf[:, m, :], lb[:, 4, m:m + 1],
                                                       lb[:, 3, m:m + 1], ALU.mult, ALU.add)
                    last.then_inc(f1, 1)
                    dve.wait_ge(f1, s + 1)
                    nc.vector.tensor_scalar(zf[:, rows, :], zf[:, rows, :], F_MIN, None, ALU.max).then_inc(f2, 1)
                    dve.wait_ge(f2, s + 1)
                    nc.vector.tensor_scalar(kf[:, rows, :], zf[:, rows, :], -1.0, 1.0,
                                            ALU.mult, ALU.add).then_inc(k_done, 1)
                dve.wait_ge(marks, 2)
                for s in range(2):
                    dve.wait_ge(logs, s + 1)
                    for m in range(s * A_HEADS, (s + 1) * A_HEADS):
                        order = slice(None, None, -1) if s else slice(None)
                        nc.vector.tensor_tensor_scan(zf[:, m, order], keep[:, s, order], zf[:, m, order],
                                                     0.0, ALU.mult, ALU.add)


def gla_direction(K, d, q, v, k, b, masks, out):
    nc = K.nc
    H = A_HEADS
    NL = len(LEVELS)
    W = H * CHUNK
    with ExitStack() as c:
        def sb(n, shape):
            return c.enter_context(nc.sbuf_tensor(f"gl{d}_{n}", shape, F32))

        def bank(n):
            return c.enter_context(nc.psum_tensor(f"gl{d}_{n}", [P, 512], F32))
        qc, kc, vc, bc = (sb(n, [P, W]) for n in ("qc", "kc", "vc", "bc"))
        mask = sb("mask", [P, NL + 1, CHUNK])
        rel = sb("rel", [P, NL + 3, W])
        eb, qb = sb("eb", [P, W]), sb("qb", [P, W])
        kt, vt = sb("kt", [P, W]), sb("vt", [P, W])
        state = sb("state", [P, H, P])
        ps_s = [bank(f"ps_s{j}") for j in range(3)]
        ps_k, ps_v, ps_o, ps_u = bank("ps_k"), bank("ps_v"), bank("ps_o"), bank("ps_u")
        (m_loaded, turn_done, qk_in, v_in, b_in, rel_done, grown, eb_done, mixed_done, ends_done,
         turned, kt_done, vt_done, scored, masked, o_done, o_taken, u_done, state_done) = K.signals(
            f"gl{d}", "m_loaded turn_done qk_in v_in b_in rel_done grown eb_done mixed_done "
            "ends_done turned kt_done vt_done scored masked o_done o_taken u_done state_done")

        def chunks(eng, body):
            if d == 0:
                with eng.Fori(0, TOK // CHUNK) as s:
                    body(s, s * CHUNK)
            else:
                for s in range(CTX // CHUNK):
                    body(s, (CTX // CHUNK - 1 - s) * CHUNK)
                with eng.Fori(0, LAT // CHUNK) as r:
                    body(r + CTX // CHUNK, TOK - CHUNK - r * CHUNK)

        def heads(t, at):
            return t[:, :, bass.ds(at, CHUNK)]

        def flat(t):
            return t[:, :].rearrange("p (h t) -> p h t", h=H)

        with nc.Block() as block:
            @block.sync
            def _(sp):
                sp.dma_start(mask[:, :, :], masks).then_inc(m_loaded, 16)

            @block.scalar
            def _(act):
                def body(s, at):
                    act.wait_ge(turn_done, s + 1)
                    nc.scalar.activation(flat(bc), heads(b, at), ACT.Copy).then_inc(b_in, 1)
                    nc.scalar.activation(flat(qc), heads(q, at), ACT.Copy)
                    nc.scalar.activation(flat(kc), heads(k, at), ACT.Copy).then_inc(qk_in, 1)
                    nc.scalar.activation(flat(vc), heads(v, at), ACT.Copy).then_inc(v_in, 1)
                    act.wait_ge(b_in, s + 1)
                    nc.scalar.activation(eb[:, :], bc[:, :], ACT.Exp).then_inc(eb_done, 1)
                    act.wait_ge(rel_done, s + 1)
                    nc.scalar.activation(rel[:, :, :], rel[:, :, :], ACT.Exp).then_inc(grown, 1)
                    act.wait_ge(turned, 2 * s + 1)
                    nc.scalar.activation(vt[:, :], ps_v[:, :], ACT.Copy).then_inc(vt_done, 1)
                    act.wait_ge(turned, 2 * s + 2)
                    nc.scalar.activation(kt[:, :], ps_k[:, :], ACT.Copy).then_inc(kt_done, 1)
                chunks(act, body)

            @block.vector
            def _(dve):
                nc.vector.memset(state[:, :, :], 0.0).then_inc(turn_done, 1)
                dve.wait_ge(m_loaded, 16)

                def body(s, at):
                    dve.wait_ge(turn_done, s + 1)
                    dve.wait_ge(b_in, s + 1)
                    for l, size in enumerate(LEVELS):
                        ref = size // 2 if d else size // 2 - 1
                        bb = bc[:, :].rearrange("p (n e) -> p n e", e=size)
                        rr = rel[:, l, :].rearrange("p (n e) -> p n e", e=size)
                        h = size // 2
                        rb = bb[:, :, ref:ref + 1].to_broadcast([P, W // size, h])
                        late, early = (slice(0, h), slice(h, size)) if d else (slice(h, size), slice(0, h))
                        nc.vector.tensor_tensor(rr[:, :, late], bb[:, :, late], rb, ALU.subtract)
                        nc.vector.tensor_tensor(rr[:, :, early], rb, bb[:, :, early], ALU.subtract)
                    bb = bc[:, :].rearrange("p (n e) -> p n e", e=4)
                    ref = bb[:, :, (2 if d else 1):(3 if d else 2)].to_broadcast([P, W // 4, 4])
                    nc.vector.tensor_tensor(rel[:, NL, :].rearrange("p (n e) -> p n e", e=4), bb, ref, ALU.subtract)
                    nc.vector.tensor_tensor(rel[:, NL + 1, :].rearrange("p (n e) -> p n e", e=4), ref, bb,
                                            ALU.subtract)
                    bh = flat(bc)
                    end = bh[:, :, (0 if d else CHUNK - 1):(1 if d else CHUNK)].to_broadcast([P, H, CHUNK])
                    nc.vector.tensor_tensor(rel[:, NL + 2, :].rearrange("p (h t) -> p h t", h=H), end, bh, ALU.subtract).then_inc(rel_done, 1)
                    dve.wait_ge(qk_in, s + 1)
                    dve.wait_ge(eb_done, s + 1)
                    nc.vector.tensor_tensor(qb[:, :], qc[:, :], eb[:, :], ALU.mult)
                    dve.wait_ge(grown, s + 1)
                    nc.vector.tensor_tensor(rel[:, NL + 2, :], kc[:, :], rel[:, NL + 2, :], ALU.mult).then_inc(ends_done, 1)
                    for l, size in enumerate(LEVELS):
                        h = size // 2
                        for src, half in ((qc, slice(0, h) if d else slice(h, size)),
                                          (kc, slice(h, size) if d else slice(0, h))):
                            def blocks(t):
                                return t.rearrange("p (n e) -> p n e", e=size)[:, :, half]
                            nc.vector.tensor_tensor(blocks(rel[:, l, :]), blocks(src[:, :]),
                                                    blocks(rel[:, l, :]), ALU.mult)
                    nc.vector.tensor_tensor(rel[:, NL, :], qc[:, :], rel[:, NL, :], ALU.mult)
                    nc.vector.tensor_tensor(rel[:, NL + 1, :], kc[:, :], rel[:, NL + 1, :], ALU.mult).then_inc(mixed_done, 1)
                    for l in range(NL + 1):
                        dve.wait_ge(scored, (NL + 1) * s + l + 1)
                        nc.vector.tensor_tensor(
                            rel[:, l, :].rearrange("p (h t) -> p h t", h=H), flat(ps_s[l % 3]),
                            mask[:, l, :].unsqueeze(1).to_broadcast([P, H, CHUNK]), ALU.mult).then_inc(masked, 1)
                    dve.wait_ge(o_done, s + 1)
                    if d == 0:
                        nc.vector.tensor_copy(heads(out, at), flat(ps_o)).then_inc(o_taken, 1)
                    else:
                        nc.vector.tensor_tensor(heads(out, at), heads(out, at), flat(ps_o), ALU.add).then_inc(o_taken, 1)
                    dve.wait_ge(u_done, s + 1)
                    for h in range(H):
                        at_end = h * CHUNK + (0 if d else CHUNK - 1)
                        last = nc.vector.scalar_tensor_tensor(
                            out=state[:, h, :], in0=state[:, h, :], scalar=eb[:, at_end:at_end + 1],
                            in1=ps_u[:, h * P:(h + 1) * P], op0=ALU.mult, op1=ALU.add)
                    last.then_inc(turn_done, 1)
                chunks(dve, body)

            @block.tensor
            def _(pe):
                def body(s, at):
                    pe.wait_ge(turn_done, s + 1)
                    pe.wait_ge(v_in, s + 1)
                    for h in range(H):
                        last = nc.tensor.transpose(ps_v[:, h * P:(h + 1) * P], vc[:, h * P:(h + 1) * P], K.ident[:, :])
                    last.then_inc(turned, 1)
                    pe.wait_ge(ends_done, s + 1)
                    for h in range(H):
                        last = nc.tensor.transpose(ps_k[:, h * P:(h + 1) * P], rel[:, NL + 2, h * P:(h + 1) * P], K.ident[:, :])
                    last.then_inc(turned, 1)
                    pe.wait_ge(mixed_done, s + 1)
                    for l in range(NL + 1):
                        if l >= 3:
                            pe.wait_ge(masked, (NL + 1) * s + l - 2)
                        for h in range(H):
                            cols = slice(h * CHUNK, (h + 1) * CHUNK)
                            a, bq = rel[:, l if l < NL else NL + 1, cols], rel[:, l, cols]
                            last = nc.tensor.matmul(ps_s[l % 3][:, cols], a, bq, start=True, stop=True)
                        last.then_inc(scored, 1)
                    pe.wait_ge(vt_done, s + 1)
                    pe.wait_ge(masked, (NL + 1) * (s + 1))
                    for h in range(H):
                        cols = slice(h * CHUNK, (h + 1) * CHUNK)
                        nc.tensor.matmul(ps_o[:, cols], state[:, h, :], qb[:, cols], start=True, stop=False)
                        for l in range(NL + 1):
                            last = nc.tensor.matmul(ps_o[:, cols], vt[:, cols], rel[:, l, cols],
                                                    start=False, stop=(l == NL))
                    last.then_inc(o_done, 1)
                    pe.wait_ge(kt_done, s + 1)
                    for h in range(H):
                        cols = slice(h * CHUNK, (h + 1) * CHUNK)
                        last = nc.tensor.matmul(ps_u[:, cols], kt[:, cols], vt[:, cols], start=True, stop=True)
                    last.then_inc(u_done, 1)
                chunks(pe, body)


def gated_readout(K, name, o, g, hi, lo, tile0):
    nc = K.nc
    n = o.shape[1]
    gated, hi_done = K.signals(name, "gated hi_done")
    with nc.Block() as block:
        @block.vector
        def _(dve):
            nc.vector.tensor_tensor(o[:, :, :], o[:, :, :], g[:, :, :], ALU.mult).then_inc(gated, 1)
            dve.wait_ge(hi_done, 1)
            nc.vector.tensor_tensor(lo[:, tile0:tile0 + n, :], o[:, :, :],
                                    hi[:, tile0:tile0 + n, :].bitcast(F32), ALU.subtract)

        @block.scalar
        def _(act):
            act.wait_ge(gated, 1)
            nc.scalar.activation(hi[:, tile0:tile0 + n, :], o[:, :, :], ACT.Copy).then_inc(hi_done, 1)


class Columns:

    def __init__(self, widths):
        self.at, self.width = {}, 0
        for name, width in widths:
            self.at[name] = (self.width, width)
            self.width += width

    def of(self, tile, name):
        a, n = self.at[name]
        return tile[:, a:a + n]


COLUMNS = Columns([
    ("c", 2 * DT), ("c_2", DT), ("ada_b0", 48), ("ada_b1", 48), ("ada_b_2", 24),
    ("norm_mix0", DT), ("norm_mix1", DT), ("norm_ffn0", DT), ("norm_ffn1", DT), ("norm_2", DT), ("final", DT),
    ("lb", 8), ("onorm", 4), ("vnorm", 4), ("conv_w0", 3 * FT), ("conv_w1", 3 * FT), ("conv_b0", FT),
    ("conv_b1", FT), ("qa_norm", 3), ("kva_norm", 2), ("q_nope", 6), ("k_nope", 6), ("q_pe", 3), ("k_pe", 1),
    ("conv_2", 4 * 24), ("dn_norm", 8), ("a_log", 1), ("dt_bias", 1),
])


def load_sbuf(K, name, pairs, also=None):
    arrived, = K.signals(name, "arrived")
    with K.nc.Block() as block:
        @block.sync
        def _(sp):
            for dst, src in pairs:
                sp.dma_start(dst, src).then_inc(arrived, 16)
            if also is not None:
                K.preload(sp, also)
            sp.wait_ge(arrived, 16 * len(pairs))


def program(nc, A, out, taps):
    with ExitStack() as ctx:
        K = Core(nc, ctx)
        K.ident = K.keep("ident", [P, P])
        K.ones = K.keep("ones", [P, P])
        K.eps = K.keep("eps", [P, 1])
        cols = K.keep("cols", [P, COLUMNS.width])
        mod = K.keep("mod", [P, 48, 2])
        scale1 = K.keep("scale1", [P, 2, DT])
        scale2 = K.keep("scale2", [P, 2, DT])

        def col(name):
            return COLUMNS.of(cols, name)

        def tap(name, ap):
            if taps is not None and name in taps:
                load_sbuf(K, "tap_" + name, [(taps[name], ap)])

        def mods(group, vec):
            return mod[:, group * DT:(group + 1) * DT, vec]

        x = K.keep("x", [P, DT, TOK])
        load_sbuf(K, "start", [(x[:, :, :], A["x"]), (cols[:, :], A["cols"]), (K.ident[:, :], A["ident"])], (A["ada0"], DT))
        (ones_set,) = K.signals("init", "ones_set")
        with nc.Block() as block:
            @block.vector
            def _(dve):
                nc.vector.memset(K.ones[:, :], 1.0)
                nc.vector.memset(K.eps[:, :], EPS)

            @block.scalar
            def _(act):
                nc.scalar.activation(col("c"), col("c"), ACT.Silu)
                nc.scalar.activation(col("c_2"), col("c_2"), ACT.Silu)
        c_cols = col("c").rearrange("p (k v) -> p k v", v=2)

        with ExitStack() as late:
            modulation(K, "mod0", A["ada0"], 48, c_cols, 2, col("ada_b0"), mod, (A["ev_uv"], DT))
            norm_scales(K, "sc0", [(scale1[:, v, :], col("norm_mix0"), mods(1, v)) for v in range(2)]
                        + [(scale2[:, v, :], col("norm_ffn0"), mods(4, v)) for v in range(2)])
            with ExitStack() as even:
                def ev(n, shape, dt=F32, where=even):
                    return where.enter_context(nc.sbuf_tensor(n, shape, dt))
                y_mlp = ev("y_mlp", [P, B_GROUPS, TOK])
                o = ev("ev_o", [P, A_HEADS, TOK])
                area = ev("ev_area", [P, 5 * A_HEADS, TOK])
                uv, qg, vz = area[:, 0:2 * B_GROUPS, :], area[:, 0:2 * A_HEADS, :], area[:, 2 * A_HEADS:, :]
                with ExitStack() as hctx:
                    h_hi = ev("h0_hi", [P, DT, TOK], F32R, hctx)
                    h_lo = ev("h0_lo", [P, DT, TOK], F32R, hctx)
                    model_norm(K, "n0", x, 0, TOK,
                               [(0, CTX, scale1[:, 1, :], mods(0, 1)), (CTX, TOK, scale1[:, 0, :], mods(0, 0))],
                               h_hi, h_lo, work=uv)
                    product(K, "uv", A["ev_uv"], 2 * B_GROUPS, DT, h_hi, h_lo, 0, TOK,
                            copy_out(K, uv, ACT.Gelu_apprx_tanh), no_evac, (A["ev_qg"], DT))
                    vs = uv[:, B_GROUPS:2 * B_GROUPS, :]
                    group_norm(K, "vn", vs, vs, B_GROUPS, 1, TOK, col("vnorm"), K.ones, 1.0 / P)
                    chunk_mlp(K, uv, A["ws_t"], A["bs"], y_mlp)
                    product(K, "qg", A["ev_qg"], 2 * A_HEADS, DT, h_hi, h_lo, 0, TOK,
                            copy_out(K, qg, ACT.Silu), no_evac, (A["ev_vz"], DT))
                    product(K, "vz", A["ev_vz"], 3 * A_HEADS, DT, h_hi, h_lo, 0, TOK,
                            copy_out(K, vz, ACT.Copy), no_evac, (A["ev_out"], DT))
                with ExitStack() as kctx:
                    kf = ev("ev_k", [P, 2 * A_HEADS, TOK], F32, kctx)
                    gla_features(K, vz[:, A_HEADS:3 * A_HEADS, :], kf, col("lb"))
                    for d in range(2):
                        gla_direction(K, d, qg[:, 0:A_HEADS, :], vz[:, 0:A_HEADS, :],
                                      kf[:, d * A_HEADS:(d + 1) * A_HEADS, :],
                                      vz[:, (1 + d) * A_HEADS:(2 + d) * A_HEADS, :], A["gla_masks"][d], o)
                tap("o", o[:, :, :])
                tap("mlp", y_mlp[:, :, :])
                group_norm(K, "on", o, o, A_HEADS, 1, TOK, col("onorm"), K.ones, 1.0 / P)
                with ExitStack() as yctx:
                    y_hi = ev("y0_hi", [P, DT, TOK], F32R, yctx)
                    y_lo = ev("y0_lo", [P, DT, TOK], F32R, yctx)
                    gated_readout(K, "ro", o, qg[:, A_HEADS:2 * A_HEADS, :], y_hi, y_lo, 0)
                    split_parts(K, "ym", y_mlp, y_hi[:, A_HEADS:DT, :], y_lo[:, A_HEADS:DT, :])
                    gates = [(0, CTX, mods(2, 1)), (CTX, TOK, mods(2, 0))]
                    product(K, "eo", A["ev_out"], DT, DT, y_hi, y_lo, 0, TOK, no_evac, add_gated(K, x, gates, 0),
                            (A["up0"], DT))
            tap("x_mix0", x[:, :, :])
            ffn(K, nc, "f0", x, 0, TOK,
                [(0, CTX, scale2[:, 1, :], mods(3, 1)), (CTX, TOK, scale2[:, 0, :], mods(3, 0))],
                A["up0"], A["down0"], col("conv_w0"), col("conv_b0"),
                [(0, CTX, mods(5, 1)), (CTX, TOK, mods(5, 0))], (A["ada1"], DT))
            tap("x0", x[:, :, :])
            rest(K, nc, A, out, x, col, c_cols, mod, mods, scale1, scale2, tap)


def ffn(K, nc, name, x, t0, T, norms, w_up, w_down, conv_w, conv_b, gates, nxt):
    with ExitStack() as c:
        h_hi = c.enter_context(nc.sbuf_tensor(name + "_hhi", [P, DT, T], F32R))
        h_lo = c.enter_context(nc.sbuf_tensor(name + "_hlo", [P, DT, T], F32R))
        model_norm(K, name + "_n", x, t0, T, norms, h_hi, h_lo)
        feed_forward(K, name, x, t0, T, h_hi, h_lo, w_up, w_down, conv_w, conv_b, gates, nxt)


MLA_HEADS = 6
MLA_SCALE = float(128 + 64) ** -0.5


def fourier(K, src, dft_c, dft_t, y):
    nc = K.nc
    NT = LAT // P
    with ExitStack() as c:
        fc = c.enter_context(nc.sbuf_tensor("ft_c", [P, 2 * P], F32))
        ft = c.enter_context(nc.sbuf_tensor("ft_t", [P, 2, NT, LAT], F32))
        chan = c.enter_context(nc.sbuf_tensor("ft_chan", [P, 2, NT, 2 * P], F32))
        ps_c = [c.enter_context(nc.psum_tensor(f"ft_psc{j}", [P, 512], F32)) for j in range(2)]
        ps_y = [c.enter_context(nc.psum_tensor(f"ft_psy{j}", [P, 512], F32)) for j in range(2)]
        loaded, by_channel, taken, done = K.signals("ft", "loaded by_channel taken done")
        with nc.Block() as block:
            @block.sync
            def _(sp):
                sp.dma_start(fc[:, :], dft_c).then_inc(loaded, 16)
                sp.dma_start(ft[:, :, :, :], dft_t).then_inc(loaded, 16)

            @block.tensor
            def _(pe):
                pe.wait_ge(loaded, 32)
                for f in range(2):
                    for n in range(NT):
                        m = f * NT + n
                        if m >= 2:
                            pe.wait_ge(taken, m - 1)
                        nc.tensor.matmul(ps_c[m % 2][:, 0:2 * P], src[:, f, n * P:(n + 1) * P], fc[:, :],
                                         start=True, stop=True).then_inc(by_channel, 1)
                for f in range(2):
                    pe.wait_ge(taken, (f + 1) * NT)
                    for n in range(NT):
                        for part in range(2):
                            last = nc.tensor.matmul(ps_y[f][:, :], chan[:, f, n, part * P:(part + 1) * P],
                                                    ft[:, part, n, :], start=(n + part == 0),
                                                    stop=(n == NT - 1 and part == 1))
                    last.then_inc(done, 1)

            @block.scalar
            def _(act):
                for m in range(2 * NT):
                    act.wait_ge(by_channel, m + 1)
                    nc.scalar.activation(chan[:, m // NT, m % NT, :], ps_c[m % 2][:, 0:2 * P],
                                         ACT.Copy).then_inc(taken, 1)
                for f in range(2):
                    act.wait_ge(done, f + 1)
                    nc.scalar.activation(y[:, f, :], ps_y[f][:, :], ACT.Copy)


def rotate(K, tiles, table, swap):
    nc = K.nc
    n = len(tiles)
    with ExitStack() as c:
        tab = c.enter_context(nc.sbuf_tensor("ro_tab", [P, 2, LAT], F32))
        sw = c.enter_context(nc.sbuf_tensor("ro_sw", [P, P], F32))
        other = c.enter_context(nc.sbuf_tensor("ro_other", [P, n, LAT], F32))
        ps = [c.enter_context(nc.psum_tensor(f"ro_ps{j}", [P, 512], F32)) for j in range(n)]
        loaded, swapped, by_sin, by_cos = K.signals("ro", "loaded swapped by_sin by_cos")
        with nc.Block() as block:
            @block.sync
            def _(sp):
                sp.dma_start(tab[:, :, :], table).then_inc(loaded, 16)
                sp.dma_start(sw[:, :], swap).then_inc(loaded, 16)

            @block.tensor
            def _(pe):
                pe.wait_ge(loaded, 32)
                for i, t in enumerate(tiles):
                    nc.tensor.matmul(ps[i][:, :], sw[:, :], t, start=True, stop=True).then_inc(swapped, 1)

            @block.vector
            def _(dve):
                dve.wait_ge(loaded, 32)
                for i, t in enumerate(tiles):
                    dve.wait_ge(swapped, i + 1)
                    nc.vector.tensor_tensor(other[:, i, :], ps[i][:, :], tab[:, 1, :], ALU.mult).then_inc(by_sin, 1)
                    nc.vector.tensor_tensor(t, t, tab[:, 0, :], ALU.mult).then_inc(by_cos, 1)
                for i, t in enumerate(tiles):
                    dve.wait_ge(by_sin, i + 1)
                    dve.wait_ge(by_cos, i + 1)
                    nc.vector.tensor_tensor(t, t, other[:, i, :], ALU.add)


def latent_attention(K, q, kn, kp, v, y):
    nc = K.nc
    NQ, NK = LAT // P, TOK // P
    with ExitStack() as c:
        def sb(n, shape):
            return c.enter_context(nc.sbuf_tensor("la_" + n, shape, F32))
        qn, qp, vs = sb("qn", [P, LAT]), sb("qp", [P, LAT]), sb("vs", [P, TOK])
        vt = sb("vt", [P, NK * P])
        probs = sb("probs", [P, 2, TOK])
        pt = sb("pt", [P, NK, LAT])
        nmax, bias, total, inv = (sb(n, [P, 2]) for n in ("nmax", "bias", "total", "inv"))
        ps_s = [c.enter_context(nc.psum_tensor(f"la_ps_s{j}", [P, 1024], F32)) for j in range(2)]
        ps_t = c.enter_context(nc.psum_tensor("la_ps_t", [P, 1024], F32))
        ps_v = c.enter_context(nc.psum_tensor("la_ps_v", [P, 512], F32))
        ps_o = c.enter_context(nc.psum_tensor("la_ps_o", [P, 512], F32))
        (q_in, qp_in, v_in, v_turned, vt_in, scored, max_done, bias_done, exp_done, inv_done, normed, p_turned,
         pt_in, o_done, o_out) = K.signals(
            "la", "q_in qp_in v_in v_turned vt_in scored max_done bias_done exp_done inv_done normed p_turned "
            "pt_in o_done o_out")

        def turns(eng, body):
            for r in range(2):
                body(r, 0, r, r == 0)
            with eng.Fori(1, MLA_HEADS // 2) as ip:
                for r in range(2):
                    body(2 * ip + r, ip, r, False)

        def tile(t, i):
            return t[:, bass.ds(i, 1), :].rearrange("p a t -> p (a t)")

        with nc.Block() as block:
            @block.scalar
            def _(act):
                def body(h, ip, r, first):
                    if not first:
                        act.wait_ge(scored, NQ * h)
                    nc.scalar.activation(qn[:, :], tile(q, h), ACT.Copy).then_inc(q_in, 1)
                    if r == 0:
                        nc.scalar.activation(qp[:, :], tile(q, MLA_HEADS + ip), ACT.Copy).then_inc(qp_in, 1)
                    if not first:
                        act.wait_ge(v_turned, 2 * h)
                    nc.scalar.activation(vs[:, :], tile(v, h), ACT.Copy).then_inc(v_in, 1)
                    if not first:
                        act.wait_ge(o_done, h)
                    for m, (a, b) in enumerate([(0, 4), (4, NK)]):
                        act.wait_ge(v_turned, 2 * h + m + 1)
                        nc.scalar.activation(vt[:, a * P:b * P], ps_v[:, 0:(b - a) * P], ACT.Copy).then_inc(vt_in, 1)
                    for n in range(NQ):
                        if not (first and n < 2):
                            act.wait_ge(p_turned, NQ * h + n - 1)
                        act.wait_ge(bias_done, NQ * h + n + 1)
                        nc.scalar.activation(probs[:, n % 2, :], ps_s[n % 2][:, 256:1024], ACT.Exp,
                                             bias=bias[:, n % 2:n % 2 + 1], scale=MLA_SCALE,
                                             accum_out=total[:, n % 2:n % 2 + 1]).then_inc(exp_done, 1)
                        act.wait_ge(p_turned, NQ * h + n + 1)
                        nc.scalar.activation(pt[:, :, n * P:(n + 1) * P],
                                             ps_t[:, 0:NK * P].rearrange("p (k t) -> p k t", k=NK),
                                             ACT.Copy).then_inc(pt_in, 1)
                turns(act, body)

            @block.vector
            def _(dve):
                def body(h, ip, r, first):
                    for n in range(NQ):
                        j = n % 2
                        dve.wait_ge(scored, NQ * h + n + 1)
                        if not (first and n < 2):
                            dve.wait_ge(exp_done, NQ * h + n - 1)
                        nc.vector.tensor_reduce(nmax[:, j:j + 1], ps_s[j][:, 256:1024], AX.X,
                                                ALU.max).then_inc(max_done, 1)
                        dve.wait_ge(max_done, NQ * h + n + 1)
                        nc.vector.tensor_scalar(bias[:, j:j + 1], nmax[:, j:j + 1], -MLA_SCALE, None,
                                                ALU.mult).then_inc(bias_done, 1)
                        dve.wait_ge(exp_done, NQ * h + n + 1)
                        nc.vector.reciprocal(inv[:, j:j + 1], total[:, j:j + 1]).then_inc(inv_done, 1)
                        dve.wait_ge(inv_done, NQ * h + n + 1)
                        nc.vector.tensor_scalar(probs[:, j, :], probs[:, j, :], inv[:, j:j + 1], None,
                                                ALU.mult).then_inc(normed, 1)
                    dve.wait_ge(o_done, h + 1)
                    nc.vector.tensor_copy(tile(y, h), ps_o[:, :]).then_inc(o_out, 1)
                turns(dve, body)

            @block.tensor
            def _(pe):
                def body(h, ip, r, first):
                    half = slice(64 * r, 64 * r + 64)

                    def score(n):
                        if not (first and n < 2):
                            pe.wait_ge(exp_done, NQ * h + n - 1)
                        for a, b, col in ((0, CTX, 256), (CTX, TOK, 512)):
                            nc.tensor.matmul(ps_s[n % 2][:, col:col + b - a], qn[:, n * P:(n + 1) * P],
                                             tile(kn, h)[:, a:b], start=True, stop=False)
                            last = nc.tensor.matmul(ps_s[n % 2][:, col:col + b - a], qp[half, n * P:(n + 1) * P],
                                                    kp[half, a:b], start=False, stop=True)
                        last.then_inc(scored, 1)

                    def turn(n):
                        pe.wait_ge(normed, NQ * h + n + 1)
                        if not (first and n == 0):
                            pe.wait_ge(pt_in, NQ * h + n)
                        for k in range(NK):
                            last = nc.tensor.transpose(ps_t[:, k * P:(k + 1) * P],
                                                       probs[:, n % 2, k * P:(k + 1) * P], K.ident[:, :])
                        last.then_inc(p_turned, 1)
                    pe.wait_ge(v_in, h + 1)
                    for m, (a, b) in enumerate([(0, 4), (4, NK)]):
                        if not (first and m == 0):
                            pe.wait_ge(vt_in, 2 * h + m)
                        for k in range(a, b):
                            last = nc.tensor.transpose(ps_v[:, (k - a) * P:(k - a + 1) * P],
                                                       vs[:, k * P:(k + 1) * P], K.ident[:, :])
                        last.then_inc(v_turned, 1)
                    pe.wait_ge(q_in, h + 1)
                    pe.wait_ge(qp_in, ip + 1)
                    score(0)
                    for n in range(NQ):
                        if n + 1 < NQ:
                            score(n + 1)
                        turn(n)
                    pe.wait_ge(vt_in, 2 * h + 2)
                    pe.wait_ge(pt_in, NQ * (h + 1))
                    if not first:
                        pe.wait_ge(o_out, h)
                    for k in range(NK):
                        last = nc.tensor.matmul(ps_o[:, :], vt[:, k * P:(k + 1) * P], pt[:, k, :],
                                                start=(k == 0), stop=(k == NK - 1))
                    last.then_inc(o_done, 1)
                turns(pe, body)


def layer1(K, nc, A, x, col, c_cols, mod, mods, scale1, scale2, tap, nxt):
    modulation(K, "mod1", A["ada1"], 48, c_cols, 2, col("ada_b1"), mod, (A["od_kv"], DT))
    norm_scales(K, "sc1", [(scale1[:, v, :], col("norm_mix1"), mods(1, v)) for v in range(2)]
                + [(scale2[:, 0, :], col("norm_ffn1"), mods(4, 0))])
    with ExitStack() as odd:
        def sb(n, shape, dt=F32, where=odd):
            return where.enter_context(nc.sbuf_tensor("od_s_" + n, shape, dt))
        y = sb("y", [P, DT, LAT])
        ones64 = sb("ones64", [P, P])
        with ExitStack() as att:
            kv = sb("kv", [P, 3, TOK], F32, att)
            fq = sb("fq", [P, 5, LAT], F32, att)
            with ExitStack() as hctx:
                h_hi = sb("h_hi", [P, DT, TOK], F32R, hctx)
                h_lo = sb("h_lo", [P, DT, TOK], F32R, hctx)
                model_norm(K, "n1", x, 0, TOK,
                           [(0, CTX, scale1[:, 1, :], mods(0, 1)), (CTX, TOK, scale1[:, 0, :], mods(0, 0))],
                           h_hi, h_lo)
                product(K, "okv", A["od_kv"], 3, DT, h_hi, h_lo, 0, TOK, copy_out(K, kv, ACT.Copy), no_evac,
                        (A["od_fq"], DT))
                product(K, "ofq", A["od_fq"], 5, DT, h_hi, h_lo, CTX, LAT, copy_out(K, fq, ACT.Copy), no_evac,
                        (A["od_qb"], 3))
            load_sbuf(K, "ones64", [(ones64[:, :], A["ones64"])])
            fourier(K, fq, A["dft_c"], A["dft_t"], y)
            group_norm(K, "qan", fq[:, 2:5, :], fq[:, 2:5, :], 1, 3, LAT, col("qa_norm"), K.ones, 1.0 / 384)
            group_norm(K, "kvan", kv[:, 0:2, :], kv[:, 0:2, :], 1, 2, TOK, col("kva_norm"), K.ones, 1.0 / 256)
            group_norm(K, "kpn", kv[:, 2:3, :], kv[:, 2:3, :], 1, 1, TOK, col("k_pe"), ones64, 1.0 / 64)
            q = sb("q", [P, 9, LAT], F32, att)
            kn = sb("kn", [P, MLA_HEADS, TOK], F32, att)
            v = sb("v", [P, MLA_HEADS, TOK], F32, att)
            with ExitStack() as lctx:
                q_hi, q_lo = (sb(n, [P, 3, LAT], F32R, lctx) for n in ("q_hi", "q_lo"))
                kv_hi, kv_lo = (sb(n, [P, 2, TOK], F32R, lctx) for n in ("kv_hi", "kv_lo"))
                split_parts(K, "qs", fq[:, 2:5, :], q_hi, q_lo)
                split_parts(K, "kvs", kv[:, 0:2, :], kv_hi, kv_lo)
                product(K, "oqb", A["od_qb"], 9, 3, q_hi, q_lo, 0, LAT, copy_out(K, q, ACT.Copy), no_evac,
                        (A["od_kb"], 2))
                product(K, "okb", A["od_kb"], 6, 2, kv_hi, kv_lo, 0, TOK, copy_out(K, kn, ACT.Copy), no_evac,
                        (A["od_vb"], 2))
                product(K, "ovb", A["od_vb"], 6, 2, kv_hi, kv_lo, 0, TOK, copy_out(K, v, ACT.Copy), no_evac,
                        (A["od_out"], DT))
            group_norm(K, "qnn", q[:, 0:6, :], q[:, 0:6, :], 6, 1, LAT, col("q_nope"), K.ones, 1.0 / P)
            group_norm(K, "qpn", q[:, 6:9, :], q[:, 6:9, :], 3, 1, LAT, col("q_pe"), ones64, 1.0 / 64)
            group_norm(K, "knn", kn, kn, 6, 1, TOK, col("k_nope"), K.ones, 1.0 / P)
            rotate(K, [q[:, 6 + m, :] for m in range(3)] + [kv[:, 2, CTX:TOK]], A["rope"], A["rope_swap"])
            latent_attention(K, q, kn, kv[:, 2, :], v, y[:, 2:DT, :])
        tap("four", y[:, 0:2, :])
        tap("att", y[:, 2:8, :])
        y_hi, y_lo = sb("y_hi", [P, DT, LAT], F32R), sb("y_lo", [P, DT, LAT], F32R)
        split_parts(K, "ys1", y, y_hi, y_lo)
        product(K, "oo", A["od_out"], DT, DT, y_hi, y_lo, 0, LAT, no_evac,
                add_gated(K, x, [(CTX, TOK, mods(2, 0))], CTX), (A["up1"], DT))
    tap("x_mix1", x[:, :, CTX:TOK])
    ffn(K, nc, "f1", x, CTX, LAT, [(0, LAT, scale2[:, 0, :], mods(3, 0))], A["up1"], A["down1"],
        col("conv_w1"), col("conv_b1"), [(CTX, TOK, mods(5, 0))], nxt)
    tap("x1", x[:, :, CTX:TOK])


def layout1(np, I, A, blocks):
    w = I["od_w_in"][0]
    k_pe = w[:, 896:960]
    A["od_kv"] = blocks(np.concatenate([w[:, 640:896], k_pe, k_pe], axis=1))
    A["od_fq"] = blocks(w[:, 0:640])
    qb = I["od_w_qb"][0].reshape(384, MLA_HEADS, 192)
    A["od_qb"] = blocks(np.concatenate([qb[:, :, :P].reshape(384, -1), qb[:, :, P:].reshape(384, -1)], axis=1))
    kvb = I["od_w_kvb"][0].reshape(256, MLA_HEADS, 2, P)
    A["od_kb"] = blocks(kvb[:, :, 0].reshape(256, -1))
    A["od_vb"] = blocks(kvb[:, :, 1].reshape(256, -1))
    A["od_out"] = blocks(I["od_w_out"][0])
    two = np.kron(np.eye(2), np.ones((64, 64)))
    A["ones64"] = two.astype(np.float32)
    a = 2 * np.pi * np.outer(np.arange(64), np.arange(64)) / 64
    A["dft_c"] = np.concatenate([np.kron(np.eye(2), np.cos(a)), np.kron(np.eye(2), np.sin(a))],
                                axis=1).astype(np.float32)
    a = 2 * np.pi * (np.outer(np.arange(LAT), np.arange(LAT)) % LAT) / LAT
    norm = 1 / np.sqrt(64.0 * LAT)
    A["dft_t"] = (np.stack([np.cos(a), -np.sin(a)]) * norm).reshape(2, LAT // P, P, LAT).transpose(
        2, 0, 1, 3).astype(np.float32)
    t = np.arange(LAT)
    inv_freq = np.float32(10000.0) ** (-np.arange(0, 32, 2, dtype=np.float32) / np.float32(32))
    ang = np.stack([t // 64, t % 64]).astype(np.float32)[:, None, :] * inv_freq[None, :, None]
    rope = np.stack([np.cos(ang), np.sin(ang)])
    rope = np.repeat(rope[:, :, None], 2, axis=2).reshape(2, 64, LAT)
    A["rope"] = np.concatenate([rope, rope], axis=1).transpose(1, 0, 2).astype(np.float32)
    swap = np.zeros((P, P), np.float32)
    for m in range(P):
        swap[m ^ 16, m] = 1.0 if m & 16 else -1.0
    A["rope_swap"] = swap


DN_HEADS = 8
NG = 2
GH = DN_HEADS // NG
DN_SCALE = float(P) ** -0.5


def delta_projections(K, name, w, h_hi, h_lo, dst, taps_w, nxt):
    nc = K.nc
    with ExitStack() as c:
        src = c.enter_context(nc.sbuf_tensor(name + "_src", [P, 2, 3 + LAT], F32))
        conv = c.enter_context(nc.sbuf_tensor(name + "_conv", [P, 2, LAT], F32))
        (padded,) = K.signals(name + "_pad", "padded")
        with nc.Block() as block:
            @block.vector
            def _(dve):
                nc.vector.memset(src[:, :, 0:3], 0.0).then_inc(padded, 1)

        def act_part(act, g, ip, j, i, first):
            conv0, conv1, conv2, conv3, silu_done = g.more
            act.wait_ge(g.mm_done, i + 1)
            if not first:
                act.wait_ge(conv3, i - 1)
            nc.scalar.activation(src[:, j, 3:3 + LAT], g.out[j], ACT.Copy).then_inc(g.free[j], 1)
            act.wait_ge(conv3, i + 1)
            nc.scalar.activation(dst[:, bass.ds(i, 1), :].rearrange("p a t -> p (a t)"), conv[:, j, :],
                                 ACT.Silu).then_inc(silu_done, 1)

        def dve_part(dve, g, ip, j, i, first):
            steps = g.more[0:4]
            silu_done = g.more[4]
            dve.wait_ge(g.free[j], ip + 1)
            if not first:
                dve.wait_ge(silu_done, i - 1)
            nc.vector.tensor_scalar(conv[:, j, :], src[:, j, 0:LAT], taps_w[:, bass.ds(i * 4, 1)], None,
                                    ALU.mult).then_inc(steps[0], 1)
            for m in range(1, 4):
                dve.wait_ge(steps[m - 1], i + 1)
                nc.vector.scalar_tensor_tensor(out=conv[:, j, :], in0=src[:, j, m:m + LAT],
                                               scalar=taps_w[:, bass.ds(i * 4 + m, 1)], in1=conv[:, j, :],
                                               op0=ALU.mult, op1=ALU.add).then_inc(steps[m], 1)

        product(K, name, w, dst.shape[1], DT, h_hi, h_lo, 0, LAT, act_part, dve_part, nxt,
                "conv0 conv1 conv2 conv3 silu_done")


def delta_gates(K, ab, a_log, dt_bias, by_token):
    nc = K.nc
    H = DN_HEADS
    NC = LAT // CHUNK
    with ExitStack() as c:
        z = c.enter_context(nc.sbuf_tensor("dg_z", [H, 8, LAT], F32))
        e_log = c.enter_context(nc.sbuf_tensor("dg_elog", [H, 2], F32))
        ps = c.enter_context(nc.psum_tensor("dg_ps", [P, NC * P], F32))
        (shifted, folded, tail, up, back, lost, inv, kept, logged, soft, rate, neg_rate, pos, summed, g_done, b_done,
         turned) = K.signals(
            "dg", "shifted folded tail up back lost inv kept logged soft rate neg_rate pos summed g_done b_done turned")
        with nc.Block() as block:
            @block.vector
            def _(dve):
                nc.vector.tensor_scalar(z[:, 0, :], ab[0:H, :], dt_bias[0:H, :], None, ALU.add).then_inc(shifted, 1)
                dve.wait_ge(shifted, 1)
                nc.vector.scalar_tensor_tensor(out=z[:, 1, :], in0=z[:, 0, :], scalar=-1.0, in1=z[:, 0, :],
                                               op0=ALU.mult, op1=ALU.min).then_inc(folded, 1)
                nc.vector.tensor_scalar(z[:, 6, :], z[:, 0, :], 0.0, None, ALU.max).then_inc(pos, 1)
                dve.wait_ge(tail, 1)
                nc.vector.tensor_scalar(z[:, 2, :], z[:, 1, :], 1.0, None, ALU.add).then_inc(up, 1)
                dve.wait_ge(up, 1)
                nc.vector.tensor_scalar(z[:, 3, :], z[:, 2, :], -1.0, None, ALU.add).then_inc(back, 1)
                nc.vector.reciprocal(z[:, 4, :], z[:, 2, :]).then_inc(inv, 1)
                dve.wait_ge(back, 1)
                nc.vector.tensor_tensor(z[:, 3, :], z[:, 1, :], z[:, 3, :], ALU.subtract).then_inc(lost, 1)
                dve.wait_ge(lost, 1)
                dve.wait_ge(inv, 1)
                nc.vector.tensor_tensor(z[:, 3, :], z[:, 3, :], z[:, 4, :], ALU.mult).then_inc(kept, 1)
                dve.wait_ge(kept, 1)
                dve.wait_ge(pos, 1)
                nc.vector.tensor_tensor(z[:, 6, :], z[:, 6, :], z[:, 3, :], ALU.add).then_inc(soft, 1)
                dve.wait_ge(soft, 1)
                dve.wait_ge(logged, 1)
                nc.vector.tensor_tensor(z[:, 6, :], z[:, 6, :], z[:, 5, :], ALU.add).then_inc(summed, 1)
                dve.wait_ge(rate, 1)
                nc.vector.tensor_scalar(e_log[:, 1:2], e_log[:, 0:1], -1.0, None, ALU.mult).then_inc(neg_rate, 1)
                dve.wait_ge(neg_rate, 1)
                dve.wait_ge(summed, 1)
                nc.vector.tensor_scalar(ab[0:H, :], z[:, 6, :], e_log[:, 1:2], None, ALU.mult).then_inc(g_done, 1)
                dve.wait_ge(turned, 1)
                pv = ps[:, :].rearrange("p (c f) -> p c f", c=NC)
                nc.vector.tensor_copy(by_token[:, :, 0:H], pv[:, :, 0:H])
                nc.vector.tensor_copy(by_token[:, :, H:2 * H], pv[:, :, 32:32 + H])

            @block.scalar
            def _(act):
                nc.scalar.activation(ab[32:32 + H, :], ab[32:32 + H, :], ACT.Sigmoid).then_inc(b_done, 1)
                nc.scalar.activation(e_log[:, 0:1], a_log[0:H, :], ACT.Exp).then_inc(rate, 1)
                act.wait_ge(folded, 1)
                nc.scalar.activation(z[:, 1, :], z[:, 1, :], ACT.Exp).then_inc(tail, 1)
                act.wait_ge(up, 1)
                nc.scalar.activation(z[:, 5, :], z[:, 2, :], ACT.Ln).then_inc(logged, 1)

            @block.tensor
            def _(pe):
                pe.wait_ge(g_done, 1)
                pe.wait_ge(b_done, 1)
                for n in range(NC):
                    last = nc.tensor.transpose(ps[:, n * P:(n + 1) * P], ab[:, n * CHUNK:(n + 1) * CHUNK],
                                               K.ident[:, :])
                last.then_inc(turned, 1)


class Fills:

    def __init__(self, full, empty, per_turn, emptied_per_turn=None):
        self.full, self.empty = full, empty
        self.per_turn, self.emptied = per_turn, emptied_per_turn or per_turn

    def wait_full(self, eng, turn, k):
        eng.wait_ge(self.full, turn * self.per_turn + k)

    def wait_empty(self, eng, turn, k):
        eng.wait_ge(self.empty, turn * self.emptied + k)


JOINS = (2, 4, 8, 16, 32, 64, 128)


def delta_rule(K, qkv, by_token, consts, join_masks):
    nc = K.nc
    H, W, NL = DN_HEADS, GH * P, len(JOINS)
    with ExitStack() as c:
        def sb(n, shape):
            return c.enter_context(nc.sbuf_tensor("dr_" + n, shape, F32))
        cst = sb("cst", [P, 3, P])
        joins = sb("joins", [P, NL + 1, P])
        upto, after, upto_scaled = cst[:, 0, :], cst[:, 1, :], cst[:, 2, :]
        gb = sb("gb", [P, 2 * H])
        g_rows, g_after = sb("g_rows", [P, H, P]), sb("g_after", [P, H, P])
        ecol = sb("ecol", [P, 3, H])
        bcol = sb("bcol", [P, H])
        S = [[sb(f"{n}{G}", [P, W]) for G in range(NG)] for n in
             ("kc", "qc", "vc", "low", "attn", "grow", "lowt", "part", "x", "xt", "xl", "kb", "kend", "vb", "state")]
        kc, qc, vc, low, attn, grow, lowt, part, X, XT, XL, kb, kend, vb, state = S
        bank = [[c.enter_context(nc.psum_tensor(f"dr_bank{n}{G}", [P, 512], F32)) for n in range(4)] for G in range(NG)]
        each = ("turn_done k_in q_in v_in low1 low2 low3 xt1 x_first xt_first part_done mask_q kb_done qd_done "
                "fullA emptyA fullB emptyB fullC emptyC fullD emptyD").split()
        made = K.signals("dr", "loaded gb_in rows_in after_in bcol_done "
                         + " ".join(f"{n}{G}" for G in range(NG) for n in each))
        loaded, gb_in, rows_in, after_in, bcol_done = made[:5]
        sig = [made[5 + G * len(each):5 + (G + 1) * len(each)] for G in range(NG)]
        (turn_done, k_in, q_in, v_in, low1, low2, low3, xt1, x_first, xt_first, part_done, mask_q, kb_done,
         qd_done) = [[sig[G][m] for G in range(NG)] for m in range(14)]
        A = [Fills(sig[G][14], sig[G][15], NL + 1 + (G == 0)) for G in range(NG)]
        B = [Fills(sig[G][16], sig[G][17], NL) for G in range(NG)]
        C = [Fills(sig[G][18], sig[G][19], NL + 2) for G in range(NG)]
        Dk = [Fills(sig[G][20], sig[G][21], 5, 4) for G in range(NG)]

        def a_fill(G, k):
            return k + (G == 0)

        def v3(t):
            return t.rearrange("p (h t) -> p h t", h=GH)

        def per_head(colv):
            return colv.unsqueeze(2).to_broadcast([P, GH, P])

        def over_heads(m):
            return m.unsqueeze(1).to_broadcast([P, GH, P])

        def turns(eng, body):
            with eng.Fori(0, LAT // CHUNK) as s:
                body(s)

        def src(part_, G, s):
            return qkv[:, part_ * H + G * GH:part_ * H + (G + 1) * GH, bass.ds(s * CHUNK, CHUNK)]

        def hc(h):
            return slice(h * P, (h + 1) * P)

        with nc.Block() as block:
            @block.sync
            def _(sp):
                sp.dma_start(cst[:, :, :], consts).then_inc(loaded, 16)
                sp.dma_start(joins[:, :, :], join_masks).then_inc(loaded, 16)

            @block.scalar
            def _(act):
                act.wait_ge(loaded, 32)

                def body(s):
                    for G in range(NG):
                        act.wait_ge(turn_done[G], s + 1)
                    nc.scalar.activation(gb[:, :], by_token[:, bass.ds(s, 1), :].rearrange("p a b -> p (a b)"),
                                         ACT.Copy).then_inc(gb_in, 1)
                    for G in range(NG):
                        nc.scalar.activation(v3(kc[G][:, :]), src(1, G, s), ACT.Copy).then_inc(k_in[G], 1)
                        if G == 0:
                            act.wait_ge(gb_in, s + 1)
                            nc.scalar.activation(g_rows[:, :, :], gb[:, 0:H].unsqueeze(2).to_broadcast([P, H, P]),
                                                 ACT.Copy).then_inc(rows_in, 1)
                        nc.scalar.activation(v3(qc[G][:, :]), src(0, G, s), ACT.Copy).then_inc(q_in[G], 1)
                        nc.scalar.activation(v3(vc[G][:, :]), src(2, G, s), ACT.Copy).then_inc(v_in[G], 1)
                    A[0].wait_full(act, s, 1)
                    nc.scalar.activation(ecol[:, :, :], bank[0][0][:, 0:3 * H].rearrange("p (a h) -> p a h", a=3),
                                         ACT.Exp).then_inc(A[0].empty, 1)
                    for G in range(NG):
                        A[G].wait_full(act, s, a_fill(G, 1))
                        nc.scalar.activation(low[G][:, :], bank[G][0][:, :], ACT.Exp).then_inc(A[G].empty, 1)
                        B[G].wait_full(act, s, 1)
                        nc.scalar.activation(attn[G][:, :], bank[G][1][:, :], ACT.Exp).then_inc(B[G].empty, 1)
                        Dk[G].wait_full(act, s, 1)
                        nc.scalar.activation(grow[G][:, :], bank[G][3][:, :], ACT.Exp).then_inc(Dk[G].empty, 1)
                    for G in range(NG):
                        C[G].wait_full(act, s, 2)
                        nc.scalar.activation(lowt[G][:, :], bank[G][2][:, :], ACT.Copy).then_inc(C[G].empty, 1)
                    for n in range(1, NL):
                        for G in range(NG):
                            A[G].wait_full(act, s, a_fill(G, 1 + n))
                            nc.scalar.activation(XL[G][:, :], bank[G][0][:, :], ACT.Copy).then_inc(A[G].empty, 1)
                    for G in range(NG):
                        A[G].wait_full(act, s, a_fill(G, NL + 1))
                        nc.scalar.activation(kc[G][:, :], bank[G][0][:, :], ACT.Copy, scale=-1.0).then_inc(A[G].empty, 1)
                    for G in range(NG):
                        B[G].wait_full(act, s, NL)
                        nc.scalar.activation(vc[G][:, :], bank[G][1][:, :], ACT.Copy).then_inc(B[G].empty, 1)
                turns(act, body)

            @block.vector
            def _(dve):
                for G in range(NG):
                    nc.vector.memset(state[G][:, :], 0.0).then_inc(turn_done[G], 1)
                dve.wait_ge(loaded, 32)

                def body(s):
                    for G in range(NG):
                        dve.wait_ge(turn_done[G], s + 1)
                    dve.wait_ge(gb_in, s + 1)
                    nc.vector.tensor_tensor(g_after[:, :, :], after.unsqueeze(1).to_broadcast([P, H, P]),
                                            gb[:, 0:H].unsqueeze(2).to_broadcast([P, H, P]),
                                            ALU.mult).then_inc(after_in, 1)
                    A[0].wait_empty(dve, s, 1)
                    nc.vector.tensor_tensor(bcol[:, :], gb[:, H:2 * H], ecol[:, 0, :], ALU.mult).then_inc(bcol_done, 1)
                    for G in range(NG):
                        heads = slice(G * GH, (G + 1) * GH)
                        beta = gb[:, H + G * GH:H + (G + 1) * GH]
                        A[G].wait_empty(dve, s, a_fill(G, 1))
                        nc.vector.tensor_tensor(v3(low[G][:, :]), v3(low[G][:, :]), over_heads(after),
                                                ALU.mult).then_inc(low1[G], 1)
                        B[G].wait_empty(dve, s, 1)
                        nc.vector.tensor_tensor(v3(attn[G][:, :]), v3(attn[G][:, :]), over_heads(upto_scaled),
                                                ALU.mult).then_inc(mask_q[G], 1)
                        dve.wait_ge(low1[G], s + 1)
                        C[G].wait_full(dve, s, 1)
                        nc.vector.tensor_tensor(low[G][:, :], low[G][:, :], bank[G][2][:, :],
                                                ALU.mult).then_inc(C[G].empty, 1)
                        C[G].wait_empty(dve, s, 1)
                        nc.vector.tensor_tensor(v3(low[G][:, :]), v3(low[G][:, :]), per_head(beta),
                                                ALU.mult).then_inc(low2[G], 1)
                        Dk[G].wait_empty(dve, s, 1)
                        dve.wait_ge(q_in[G], s + 1)
                        nc.vector.scalar_tensor_tensor(out=grow[G][:, :], in0=qc[G][:, :], scalar=DN_SCALE,
                                                       in1=grow[G][:, :], op0=ALU.mult, op1=ALU.mult).then_inc(qd_done[G], 1)
                        dve.wait_ge(mask_q[G], s + 1)
                        Dk[G].wait_full(dve, s, 2)
                        nc.vector.tensor_tensor(attn[G][:, :], attn[G][:, :], bank[G][3][:, :],
                                                ALU.mult).then_inc(Dk[G].empty, 1)
                        dve.wait_ge(bcol_done, s + 1)
                        Dk[G].wait_full(dve, s, 3)
                        nc.vector.tensor_tensor(v3(kb[G][:, :]), v3(bank[G][3][:, :]), per_head(bcol[:, heads]),
                                                ALU.mult).then_inc(kb_done[G], 1)
                        nc.vector.tensor_tensor(v3(kend[G][:, :]), v3(bank[G][3][:, :]), per_head(ecol[:, 1, heads]),
                                                ALU.mult).then_inc(Dk[G].empty, 1)
                        Dk[G].wait_full(dve, s, 4)
                        nc.vector.tensor_tensor(v3(vb[G][:, :]), v3(bank[G][3][:, :]), per_head(beta),
                                                ALU.mult).then_inc(Dk[G].empty, 1)
                        dve.wait_ge(low2[G], s + 1)
                        nc.vector.tensor_tensor(v3(X[G][:, :]), v3(low[G][:, :]), over_heads(joins[:, NL, :]),
                                                ALU.mult).then_inc(low3[G], 1)
                        C[G].wait_empty(dve, s, 2)
                        nc.vector.tensor_tensor(v3(XT[G][:, :]), v3(lowt[G][:, :]), over_heads(joins[:, 0, :]),
                                                ALU.mult).then_inc(xt1[G], 1)
                        dve.wait_ge(low3[G], s + 1)
                        nc.vector.tensor_tensor(v3(X[G][:, :]), over_heads(K.ident[:, :]), v3(X[G][:, :]),
                                                ALU.subtract).then_inc(x_first[G], 1)
                        dve.wait_ge(xt1[G], s + 1)
                        nc.vector.tensor_tensor(v3(XT[G][:, :]), over_heads(K.ident[:, :]), v3(XT[G][:, :]),
                                                ALU.subtract).then_inc(xt_first[G], 1)
                    for n in range(1, NL):
                        for G in range(NG):
                            if n > 1:
                                A[G].wait_full(dve, s, a_fill(G, n))
                            nc.vector.tensor_tensor(v3(part[G][:, :]), v3(lowt[G][:, :]), over_heads(joins[:, n, :]),
                                                    ALU.mult).then_inc(part_done[G], 1)
                        for G in range(NG):
                            if n < NL - 1:
                                B[G].wait_full(dve, s, n + 1)
                                C[G].wait_full(dve, s, n + 2)
                                if n == 1:
                                    dve.wait_ge(x_first[G], s + 1)
                                else:
                                    B[G].wait_empty(dve, s, n)
                                nc.vector.tensor_tensor(X[G][:, :], X[G][:, :], bank[G][1][:, :],
                                                        ALU.subtract).then_inc(B[G].empty, 1)
                            C[G].wait_full(dve, s, n + 2)
                            if n == 1:
                                dve.wait_ge(xt_first[G], s + 1)
                            else:
                                C[G].wait_empty(dve, s, n + 1)
                            nc.vector.tensor_tensor(XT[G][:, :], XT[G][:, :], bank[G][2][:, :],
                                                    ALU.subtract).then_inc(C[G].empty, 1)
                    for G in range(NG):
                        C[G].wait_full(dve, s, NL + 2)
                        nc.vector.tensor_scalar(src(0, G, s), v3(bank[G][2][:, :]), 1.0, None,
                                                ALU.mult).then_inc(C[G].empty, 1)
                        Dk[G].wait_full(dve, s, 5)
                        for h in range(GH):
                            hh = G * GH + h
                            last = nc.vector.scalar_tensor_tensor(
                                out=state[G][:, hc(h)], in0=state[G][:, hc(h)], scalar=ecol[:, 2, hh:hh + 1],
                                in1=bank[G][3][:, hc(h)], op0=ALU.mult, op1=ALU.add)
                        last.then_inc(turn_done[G], 1)
                turns(dve, body)

            @block.tensor
            def _(pe):
                pe.wait_ge(loaded, 32)

                def each_head(G, k, out, lhsT, rhs, then):
                    for h in range(GH):
                        last = nc.tensor.matmul(out[:, hc(h)], lhsT(h), rhs(h), start=True, stop=True)
                    last.then_inc(then, 1)

                def turn_over(G, out, t, then):
                    for h in range(GH):
                        last = nc.tensor.transpose(out[:, hc(h)], t[:, hc(h)], K.ident[:, :])
                    last.then_inc(then, 1)

                def body(s):
                    for G in range(NG):
                        pe.wait_ge(turn_done[G], s + 1)
                    pe.wait_ge(gb_in, s + 1)
                    for m, left in enumerate((upto, after, K.ones[:, :])):
                        last = nc.tensor.matmul(bank[0][0][:, m * H:(m + 1) * H], left, gb[:, 0:H],
                                                start=True, stop=True)
                    last.then_inc(A[0].full, 1)
                    for G in range(NG):
                        pe.wait_ge(k_in[G], s + 1)
                        each_head(G, 1, bank[G][2], lambda h: kc[G][:, hc(h)], lambda h: kc[G][:, hc(h)], C[G].full)
                    pe.wait_ge(rows_in, s + 1)
                    pe.wait_ge(after_in, s + 1)
                    A[0].wait_empty(pe, s, 1)
                    for G in range(NG):
                        each_head(G, 1, bank[G][0], lambda h: upto, lambda h: g_after[:, G * GH + h, :], A[G].full)
                        each_head(G, 1, bank[G][1], lambda h: g_after[:, G * GH + h, :], lambda h: upto, B[G].full)
                        each_head(G, 1, bank[G][3], lambda h: g_rows[:, G * GH + h, :], lambda h: upto, Dk[G].full)
                    for G in range(NG):
                        pe.wait_ge(low2[G], s + 1)
                        C[G].wait_empty(pe, s, 1)
                        turn_over(G, bank[G][2], low[G], C[G].full)
                        Dk[G].wait_empty(pe, s, 1)
                        pe.wait_ge(q_in[G], s + 1)
                        each_head(G, 2, bank[G][3], lambda h: kc[G][:, hc(h)], lambda h: qc[G][:, hc(h)], Dk[G].full)
                        Dk[G].wait_empty(pe, s, 2)
                        turn_over(G, bank[G][3], kc[G], Dk[G].full)
                        pe.wait_ge(v_in[G], s + 1)
                        Dk[G].wait_empty(pe, s, 3)
                        turn_over(G, bank[G][3], vc[G], Dk[G].full)
                    for n in range(1, NL):
                        for G in range(NG):
                            pe.wait_ge(part_done[G], (NL - 1) * s + n)
                            if n == 1:
                                pe.wait_ge(x_first[G], s + 1)
                                pe.wait_ge(xt_first[G], s + 1)
                            else:
                                B[G].wait_empty(pe, s, n)
                                C[G].wait_empty(pe, s, n + 1)
                            A[G].wait_empty(pe, s, a_fill(G, n))
                            each_head(G, n, bank[G][0], lambda h: part[G][:, hc(h)], lambda h: X[G][:, hc(h)],
                                      A[G].full)
                        for G in range(NG):
                            A[G].wait_empty(pe, s, a_fill(G, n + 1))
                            if n == 1:
                                B[G].wait_empty(pe, s, 1)
                                C[G].wait_empty(pe, s, 2)
                            if n < NL - 1:
                                each_head(G, n, bank[G][1], lambda h: XT[G][:, hc(h)], lambda h: XL[G][:, hc(h)],
                                          B[G].full)
                            each_head(G, n, bank[G][2], lambda h: XL[G][:, hc(h)], lambda h: XT[G][:, hc(h)],
                                      C[G].full)
                    for G in range(NG):
                        C[G].wait_empty(pe, s, NL + 1)
                        pe.wait_ge(kb_done[G], s + 1)
                        each_head(G, 0, bank[G][0], lambda h: kb[G][:, hc(h)], lambda h: XT[G][:, hc(h)], A[G].full)
                    for G in range(NG):
                        A[G].wait_empty(pe, s, a_fill(G, NL + 1))
                        Dk[G].wait_empty(pe, s, 4)
                        for h in range(GH):
                            nc.tensor.matmul(bank[G][1][:, hc(h)], XT[G][:, hc(h)], vb[G][:, hc(h)], start=True,
                                             stop=False)
                            last = nc.tensor.matmul(bank[G][1][:, hc(h)], kc[G][:, hc(h)], state[G][:, hc(h)],
                                                    start=False, stop=True)
                        last.then_inc(B[G].full, 1)
                    for G in range(NG):
                        B[G].wait_empty(pe, s, NL)
                        pe.wait_ge(qd_done[G], s + 1)
                        for h in range(GH):
                            nc.tensor.matmul(bank[G][2][:, hc(h)], state[G][:, hc(h)], grow[G][:, hc(h)], start=True,
                                             stop=False)
                            last = nc.tensor.matmul(bank[G][2][:, hc(h)], vc[G][:, hc(h)], attn[G][:, hc(h)],
                                                    start=False, stop=True)
                        last.then_inc(C[G].full, 1)
                        each_head(G, 5, bank[G][3], lambda h: kend[G][:, hc(h)], lambda h: vc[G][:, hc(h)], Dk[G].full)
                turns(pe, body)


def dilated_attention(K, g, qkv, mask, out, lse):
    nc = K.nc
    NB = LAT // P
    WB = 2 * P if g == 0 else P
    WS = NB * WB
    SC = 64.0 ** -0.5
    with ExitStack() as c:
        def sb(n, shape):
            return c.enter_context(nc.sbuf_tensor(f"da{g}_{n}", shape, F32))
        msk = sb("msk", [P, WS])
        qs, ks, vs, vt = (sb(n, [P, LAT]) for n in ("qs", "ks", "vs", "vt"))
        p = sb("p", [P, 2, WS])
        pt = sb("pt", [P, 2, WS])
        nmax, den, inv, lcol = (sb(n, [P, 2, NB]) for n in ("nmax", "den", "inv", "lcol"))
        lrow = sb("lrow", [P, 2, NB, 64])
        ps_s = c.enter_context(nc.psum_tensor(f"da{g}_ps_s", [P, 1024], F32))
        ps_t = c.enter_context(nc.psum_tensor(f"da{g}_ps_t", [P, 1024], F32))
        ps_v = c.enter_context(nc.psum_tensor(f"da{g}_ps_v", [P, 512], F32))
        ps_o = c.enter_context(nc.psum_tensor(f"da{g}_ps_o", [P, 512], F32))
        ps_l = c.enter_context(nc.psum_tensor(f"da{g}_ps_l", [P, 512], F32))
        (loaded, qk_in, v_in, v_turned, vt_in, scored, scaled, maxed, less, exp_done, sums, inverted, normed, logged,
         lsum, rows, p_turned, pt_in, o_done, l_done, taken_l, turn_done) = K.signals(
            f"da{g}", "loaded qk_in v_in v_turned vt_in scored scaled maxed less exp_done sums inverted normed logged "
            "lsum rows p_turned pt_in o_done l_done taken_l turn_done")

        def order(t):
            if g == 0:
                return t
            if g == 1:
                return t.rearrange("p (i b) -> p b i", b=4)
            return t.rearrange("p (i b r) -> p b i r", b=4, r=4)

        def blocked(t):
            if g == 0:
                return t
            if g == 1:
                return t.rearrange("p (b i) -> p b i", b=4)
            return t.rearrange("p (b i r) -> p b i r", b=4, r=4)

        def tile(t, i):
            return t[:, bass.ds(i, 1), :].rearrange("p a t -> p (a t)")

        def pieces(dst_order, dst, src_order, src_):
            if g < 2:
                return [(dst_order(dst), src_order(src_))]
            d, s_ = dst_order(dst), src_order(src_)
            return [(d[:, b], s_[:, b]) for b in range(4)]

        def turns(eng, body):
            for u in range(2):
                body(u)

        with nc.Block() as block:
            @block.sync
            def _(sp):
                sp.dma_start(msk[:, :], mask).then_inc(loaded, 16)

            @block.scalar
            def _(act):
                def body(u):
                    if u > 0:
                        act.wait_ge(turn_done, u)
                    for dst, part in ((qs, 0), (ks, 1), (vs, 2)):
                        for d, s_ in pieces(blocked, dst[:, :], order, tile(qkv, 2 * part + u)):
                            last = nc.scalar.activation(d, s_, ACT.Copy)
                        if part:
                            last.then_inc((None, qk_in, v_in)[part], 1)
                    act.wait_ge(v_turned, u + 1)
                    nc.scalar.activation(vt[:, :], ps_v[:, :], ACT.Copy).then_inc(vt_in, 1)
                    for r in range(2):
                        n = 2 * u + r
                        act.wait_ge(less, n + 1)
                        nc.scalar.activation(p[:, r, :], p[:, r, :], ACT.Exp).then_inc(exp_done, 1)
                        act.wait_ge(sums, n + 1)
                        nc.scalar.activation(lcol[:, r, :], den[:, r, :], ACT.Ln).then_inc(logged, 1)
                        act.wait_ge(lsum, n + 1)
                        nc.scalar.activation(lrow[:, r, :, :], lcol[:, r, :].unsqueeze(2).to_broadcast([P, NB, 64]),
                                             ACT.Copy).then_inc(rows, 1)
                        act.wait_ge(p_turned, n + 1)
                        nc.scalar.activation(pt[:, r, :], ps_t[:, 0:WS], ACT.Copy).then_inc(pt_in, 1)
                    act.wait_ge(l_done, u + 1)
                    for d, s_ in pieces(order, tile(lse, u), blocked, ps_l[:, :]):
                        last = nc.scalar.activation(d, s_, ACT.Copy)
                    last.then_inc(taken_l, 1)
                turns(act, body)

            @block.vector
            def _(dve):
                dve.wait_ge(loaded, 16)

                def v4(t):
                    return t.rearrange("p (b k) -> p b k", b=NB)

                def body(u):
                    for r in range(2):
                        n = 2 * u + r
                        dve.wait_ge(scored, n + 1)
                        nc.vector.scalar_tensor_tensor(out=p[:, r, :], in0=ps_s[:, 0:WS], scalar=SC, in1=msk[:, :],
                                                       op0=ALU.mult, op1=ALU.add).then_inc(scaled, 1)
                        dve.wait_ge(scaled, n + 1)
                        nc.vector.tensor_reduce(nmax[:, r, :], v4(p[:, r, :]), AX.X, ALU.max).then_inc(maxed, 1)
                        dve.wait_ge(maxed, n + 1)
                        nc.vector.tensor_tensor(v4(p[:, r, :]), v4(p[:, r, :]),
                                                nmax[:, r, :].unsqueeze(2).to_broadcast([P, NB, WB]),
                                                ALU.subtract).then_inc(less, 1)
                        dve.wait_ge(exp_done, n + 1)
                        nc.vector.tensor_reduce(den[:, r, :], v4(p[:, r, :]), AX.X, ALU.add).then_inc(sums, 1)
                        dve.wait_ge(sums, n + 1)
                        nc.vector.reciprocal(inv[:, r, :], den[:, r, :]).then_inc(inverted, 1)
                        dve.wait_ge(inverted, n + 1)
                        nc.vector.tensor_tensor(v4(p[:, r, :]), v4(p[:, r, :]),
                                                inv[:, r, :].unsqueeze(2).to_broadcast([P, NB, WB]),
                                                ALU.mult).then_inc(normed, 1)
                        dve.wait_ge(logged, n + 1)
                        nc.vector.tensor_tensor(lcol[:, r, :], lcol[:, r, :], nmax[:, r, :], ALU.add).then_inc(lsum, 1)
                    dve.wait_ge(o_done, u + 1)
                    for d, s_ in pieces(order, tile(out, u), blocked, ps_o[:, :]):
                        last = nc.vector.tensor_copy(d, s_)
                    dve.wait_ge(taken_l, u + 1)
                    last.then_inc(turn_done, 1)
                turns(dve, body)

            @block.tensor
            def _(pe):
                def body(u):
                    if u > 0:
                        pe.wait_ge(turn_done, u)
                    pe.wait_ge(v_in, u + 1)
                    for b in range(NB):
                        last = nc.tensor.transpose(ps_v[:, b * P:(b + 1) * P], vs[:, b * P:(b + 1) * P], K.ident[:, :])
                    last.then_inc(v_turned, 1)
                    for r in range(2):
                        n = 2 * u + r
                        half = slice(64 * r, 64 * r + 64)
                        pe.wait_ge(qk_in, u + 1)
                        if n > 0:
                            pe.wait_ge(scaled, n)
                        for b in range(NB):
                            first = b if g else max(b - 1, 0)
                            spans = [(b * WB, b * P, P)] if g else [
                                (b * WB, first * P, P), (b * WB + P, b * P, P)]
                            for col, key, width in spans:
                                last = nc.tensor.matmul(ps_s[:, col:col + width], qs[half, b * P:(b + 1) * P],
                                                        ks[half, key:key + width], start=True, stop=True)
                        last.then_inc(scored, 1)
                        pe.wait_ge(rows, n + 1)
                        for b in range(NB):
                            last = nc.tensor.matmul(ps_l[half, b * P:(b + 1) * P], lrow[:, r, b, :], K.ident[:, :],
                                                    start=True, stop=True)
                        if r:
                            last.then_inc(l_done, 1)
                        pe.wait_ge(normed, n + 1)
                        if n > 0:
                            pe.wait_ge(pt_in, n)
                        for b in range(WS // P):
                            last = nc.tensor.transpose(ps_t[:, b * P:(b + 1) * P], p[:, r, b * P:(b + 1) * P],
                                                       K.ident[:, :])
                        last.then_inc(p_turned, 1)
                        pe.wait_ge(pt_in, n + 1)
                        pe.wait_ge(vt_in, u + 1)
                        for b in range(NB):
                            both = g == 0 and b > 0
                            if both:
                                nc.tensor.matmul(ps_o[half, b * P:(b + 1) * P], vt[:, (b - 1) * P + 64 * r:(b - 1) * P + 64 * r + 64],
                                                 pt[:, r, b * WB:b * WB + P], start=True, stop=False)
                            last = nc.tensor.matmul(ps_o[half, b * P:(b + 1) * P], vt[:, b * P + 64 * r:b * P + 64 * r + 64],
                                                    pt[:, r, (b + 1) * WB - P:(b + 1) * WB], start=not both, stop=True)
                        if r:
                            last.then_inc(o_done, 1)
                turns(pe, body)


def weigh_groups(K, out, lse):
    nc = K.nc
    with ExitStack() as c:
        top = c.enter_context(nc.sbuf_tensor("wg_top", [P, 2, LAT], F32))
        tot = c.enter_context(nc.sbuf_tensor("wg_tot", [P, 2, LAT], F32))
        m1, m2, less, e_done, t1, t2, inv, weighed = K.signals("wg", "m1 m2 less e_done t1 t2 inv weighed")
        g3 = [lse[:, 2 * g:2 * g + 2, :] for g in range(3)]
        o3 = [out[:, 2 * g:2 * g + 2, :] for g in range(3)]
        with nc.Block() as block:
            @block.vector
            def _(dve):
                nc.vector.tensor_tensor(top[:, :, :], g3[0], g3[1], ALU.max).then_inc(m1, 1)
                dve.wait_ge(m1, 1)
                nc.vector.tensor_tensor(top[:, :, :], top[:, :, :], g3[2], ALU.max).then_inc(m2, 1)
                dve.wait_ge(m2, 1)
                for g in range(3):
                    nc.vector.tensor_tensor(g3[g], g3[g], top[:, :, :], ALU.subtract).then_inc(less, 1)
                dve.wait_ge(e_done, 3)
                nc.vector.tensor_tensor(tot[:, :, :], g3[0], g3[1], ALU.add).then_inc(t1, 1)
                dve.wait_ge(t1, 1)
                nc.vector.tensor_tensor(tot[:, :, :], tot[:, :, :], g3[2], ALU.add).then_inc(t2, 1)
                dve.wait_ge(t2, 1)
                nc.vector.reciprocal(tot[:, :, :], tot[:, :, :]).then_inc(inv, 1)
                for g in range(3):
                    nc.vector.tensor_tensor(o3[g], o3[g], g3[g], ALU.mult).then_inc(weighed, 1)
                dve.wait_ge(inv, 1)
                for g in range(3):
                    dve.wait_ge(weighed, g + 1)
                    nc.vector.tensor_tensor(o3[g], o3[g], tot[:, :, :], ALU.mult)

            @block.scalar
            def _(act):
                for g in range(3):
                    act.wait_ge(less, g + 1)
                    nc.scalar.activation(g3[g], g3[g], ACT.Exp).then_inc(e_done, 1)


def silu_stage(K, name, t):
    with K.nc.Block() as block:
        @block.scalar
        def _(act):
            K.nc.scalar.activation(t, t, ACT.Silu)


def second(K, nc, A, out, x, col, mod, mods, scale1, tap):
    modulation(K, "mod2", A["ada2"], 24, col("c_2").unsqueeze(2), 1, col("ada_b_2"), mod[:, 0:24, :], (A["dn_qkv"], DT))
    norm_scales(K, "sc2", [(scale1[:, 0, :], col("norm_2"), mods(1, 0))])
    norms = [(0, LAT, scale1[:, 0, :], mods(0, 0))]
    with ExitStack() as body:
        def sb(n, shape, dt=F32, where=body):
            return where.enter_context(nc.sbuf_tensor("s2_" + n, shape, dt))
        qkv = sb("qkv", [P, 24, LAT])
        ob, ya, group_qkv = qkv[:, 0:6, :], qkv[:, DT:2 * DT, :], qkv[:, 2 * DT:2 * DT + 6, :]
        with ExitStack() as dn:
            zab = sb("zab", [P, 9, LAT], F32, dn)
            with ExitStack() as hctx:
                h_hi, h_lo = sb("h_hi", [P, DT, LAT], F32R, hctx), sb("h_lo", [P, DT, LAT], F32R, hctx)
                model_norm(K, "n2", x, CTX, LAT, norms, h_hi, h_lo, work=qkv[:, 0:DT, :])
                delta_projections(K, "dq", A["dn_qkv"], h_hi, h_lo, qkv, col("conv_2"), (A["dn_zab"], DT))
                product(K, "dz", A["dn_zab"], 9, DT, h_hi, h_lo, 0, LAT, copy_out(K, zab, ACT.Copy), no_evac,
                        (A["proj_a"], DT))
            group_norm(K, "l2", qkv[:, 0:16, :], qkv[:, 0:16, :], 16, 1, LAT, None, K.ones, 1.0)
            tap("k_dn", qkv[:, 8:16, :])
            tap("v_dn", qkv[:, 16:24, :])
            by_token = sb("by_token", [P, LAT // CHUNK, 2 * DN_HEADS], F32, dn)
            delta_gates(K, zab[:, 8, :], col("a_log"), col("dt_bias"), by_token)
            delta_rule(K, qkv, by_token, A["dr_consts"], A["dr_joins"])
            tap("o_a", qkv[:, 0:8, :])
            o = qkv[:, 0:8, :]
            group_norm(K, "dnn", o, o, 8, 1, LAT, col("dn_norm"), K.ones, 1.0 / P)
            silu_stage(K, "zs", zab[:, 0:8, :])
            o_hi, o_lo = sb("o_hi", [P, DT, LAT], F32R, dn), sb("o_lo", [P, DT, LAT], F32R, dn)
            gated_readout(K, "dro", o, zab[:, 0:8, :], o_hi, o_lo, 0)
            product(K, "pa", A["proj_a"], DT, DT, o_hi, o_lo, 0, LAT, copy_out(K, ya, ACT.Copy), no_evac,
                    (A["da0"], DT))
        h_hi, h_lo = sb("h2_hi", [P, DT, LAT], F32R), sb("h2_lo", [P, DT, LAT], F32R)
        model_norm(K, "n3", x, CTX, LAT, norms, h_hi, h_lo)
        yb = sb("yb", [P, DT, LAT])
        with ExitStack() as at:
            lse = sb("lse", [P, 6, LAT], F32, at)
            for g in range(3):
                product(K, f"dp{g}", A[f"da{g}"], 6, DT, h_hi, h_lo, 0, LAT, copy_out(K, group_qkv, ACT.Copy),
                        no_evac, (A[f"da{g + 1}"] if g < 2 else A["da_z"], DT))
                dilated_attention(K, g, group_qkv, A["da_mask0"] if g == 0 else A["da_mask12"][g - 1],
                                  ob[:, 2 * g:2 * g + 2, :], lse[:, 2 * g:2 * g + 2, :])
            weigh_groups(K, ob, lse)
            tap("o_b", ob[:, :, :])
            product(K, "dbz", A["da_z"], 6, DT, h_hi, h_lo, 0, LAT, copy_out(K, lse, ACT.Silu), no_evac,
                    (A["proj_b"], 6))
            b_hi, b_lo = sb("b_hi", [P, 6, LAT], F32R, at), sb("b_lo", [P, 6, LAT], F32R, at)
            gated_readout(K, "dbo", ob, lse, b_hi, b_lo, 0)
            product(K, "pb", A["proj_b"], DT, 6, b_hi, b_lo, 0, LAT, copy_out(K, yb, ACT.Copy), no_evac,
                    (A["gate_a"], DT))
        with ExitStack() as gt:
            ga = sb("ga", [P, DT, LAT], F32, gt)
            product(K, "pga", A["gate_a"], DT, DT, h_hi, h_lo, 0, LAT, copy_out(K, ga, ACT.Sigmoid), no_evac,
                    (A["gate_b"], DT))
            multiply_into(K, "ma", ya, ga, None)
            product(K, "pgb", A["gate_b"], DT, DT, h_hi, h_lo, 0, LAT, copy_out(K, ga, ACT.Sigmoid), no_evac,
                    (A["w_out2"], DT))
            multiply_into(K, "mb", ga, yb, ya)
        m_hi, m_lo = sb("m_hi", [P, DT, LAT], F32R), sb("m_lo", [P, DT, LAT], F32R)
        split_parts(K, "ms", ya, m_hi, m_lo)
        product(K, "po", A["w_out2"], DT, DT, m_hi, m_lo, 0, LAT, no_evac,
                add_gated(K, x, [(CTX, TOK, mods(2, 0))], CTX), None)
    with ExitStack() as fin:
        y = fin.enter_context(nc.sbuf_tensor("y_out", [P, DT, LAT], F32))
        model_norm(K, "nf", x, CTX, LAT, [(0, LAT, col("final"), None)], plain=y)
        load_sbuf(K, "store", [(out, y[:, :, :])])


def multiply_into(K, name, a, b, total):
    nc = K.nc
    (done,) = K.signals(name, "done")
    with nc.Block() as block:
        @block.vector
        def _(dve):
            nc.vector.tensor_tensor(a[:, :, :], a[:, :, :], b[:, :, :], ALU.mult).then_inc(done, 1)
            if total is not None:
                dve.wait_ge(done, 1)
                nc.vector.tensor_tensor(total[:, :, :], total[:, :, :], a[:, :, :], ALU.add)


def rest(K, nc, A, out, x, col, c_cols, mod, mods, scale1, scale2, tap):
    layer1(K, nc, A, x, col, c_cols, mod, mods, scale1, scale2, tap, (A["ada2"], DT))
    second(K, nc, A, out, x, col, mod, mods, scale1, tap)


def layout2(np, I, A, blocks):
    A["ada2"] = blocks(I["ada_w_2"][0])
    w = I["w_in_2"][0]
    A["dn_qkv"] = blocks(w[:, 0:3072])
    ab = np.zeros((D, P), np.float32)
    ab[:, 0:8] = w[:, 4104:4112]
    ab[:, 32:40] = w[:, 4096:4104]
    A["dn_zab"] = blocks(np.concatenate([w[:, 3072:4096], ab], axis=1))
    at = w[:, 4112:4112 + 4 * 768].reshape(D, 4, 3, 256)
    for g in range(3):
        A[f"da{g}"] = blocks(at[:, 0:3, g].reshape(D, 768))
    A["da_z"] = blocks(at[:, 3].reshape(D, 768))
    A["gate_a"] = blocks(w[:, 7184:8208])
    A["gate_b"] = blocks(w[:, 8208:9232])
    A["proj_a"] = blocks(I["w_proj_a_2"][0])
    A["proj_b"] = blocks(I["w_proj_b_2"][0])
    A["w_out2"] = blocks(I["w_out_2"][0])
    r, t = np.arange(P)[:, None], np.arange(P)[None, :]
    A["dr_consts"] = np.stack([r <= t, r > t, (r <= t) * DN_SCALE], axis=1).astype(np.float32)
    joins = [(r // n == t // n) & (r % n < n // 2) & (t % n >= n // 2) for n in JOINS]
    A["dr_joins"] = np.stack(joins + [joins[0].T], axis=1).astype(np.float32)
    off = np.float32(-1e30)
    own = np.where(r >= t, 0, off)
    before = np.where(t >= r, 0, off)
    none = np.full((P, P), off)
    A["da_mask0"] = np.concatenate([m for b in range(4) for m in ((before if b else none), own)],
                                   axis=1).astype(np.float32)
    cls = np.where((r >= t) & (r % 4 == t % 4), 0, off)
    A["da_mask12"] = np.stack([np.tile(own, 4), np.tile(cls, 4)]).astype(np.float32)


def more_layout(np, I, A, blocks, column):
    layout1(np, I, A, blocks)
    layout2(np, I, A, blocks)


def _layout(np, I):
    def blocks(w):
        k, n = w.shape
        return np.ascontiguousarray(w.reshape(k // P, P, n // P, P).transpose(2, 1, 0, 3)).reshape(n, k)

    def column(v):
        return v.reshape(-1, P).T

    def tokens(x):
        return x.T.reshape(DT, P, -1).transpose(1, 0, 2)
    A = {}
    A["x"] = np.concatenate([tokens(I["ctx"][0]), tokens(I["x"][0])], axis=2)
    for l in range(2):
        A[f"ada{l}"] = blocks(I["ada_w"][l])
        up = I["ffn_w_up"][l].reshape(D, 2, FT, P).transpose(0, 2, 1, 3).reshape(D, 2 * D_FF)
        A[f"up{l}"] = blocks(up)
        down = I["ffn_w_down"][l]
        A[f"down{l}"] = np.concatenate([blocks(down[:FH * P]), blocks(down[FH * P:])])
    w = I["ev_w_in"][0].reshape(D, 28, P)
    pick = {"ev_uv": list(range(20, 28)), "ev_qg": list(range(0, 4)) + list(range(16, 20)),
            "ev_vz": list(range(4, 16))}
    for name, tiles in pick.items():
        A[name] = blocks(w[:, tiles].reshape(D, -1))
    A["ev_out"] = blocks(I["ev_w_out"][0])
    A["ws_t"] = I["ev_ws"][0].transpose(2, 0, 1).reshape(P, -1)
    A["bs"] = I["ev_bs"][0].reshape(1, -1)
    t = np.arange(CHUNK)
    s_, t_ = t[:, None], t[None, :]
    masks = np.zeros((2, P, len(LEVELS) + 1, CHUNK), np.float32)
    for l, size in enumerate(LEVELS):
        same = s_ // size == t_ // size
        early_s, early_t = s_ % size < size // 2, t_ % size < size // 2
        masks[0, :, l] = same & early_s & ~early_t
        masks[1, :, l] = same & ~early_s & early_t
    masks[0, :, -1] = (s_ // 4 == t_ // 4) & (s_ <= t_)
    masks[1, :, -1] = (s_ // 4 == t_ // 4) & (s_ >= t_)
    A["gla_masks"] = masks
    A["ident"] = np.eye(P, dtype=np.float32)

    cc = np.stack([I["c"][0], I["c_ctx"]], axis=1).reshape(DT, P, 2).transpose(1, 0, 2).reshape(P, -1)
    qn, kn = I["od_q_norm_w"][0], I["od_k_norm_w"][0]
    parts = {
        "c": cc, "c_2": column(I["c_2"][0]), "ada_b0": column(I["ada_b"][0]), "ada_b1": column(I["ada_b"][1]),
        "ada_b_2": column(I["ada_b_2"][0]),
        "norm_mix0": column(I["norm_mix_w"][0]), "norm_mix1": column(I["norm_mix_w"][1]),
        "norm_ffn0": column(I["norm_ffn_w"][0]), "norm_ffn1": column(I["norm_ffn_w"][1]),
        "norm_2": column(I["norm_w_2"][0]), "final": column(I["final_norm_w_2"]),
        "lb": column(I["ev_lb_logits"][0].reshape(-1)), "onorm": np.repeat(column(I["ev_onorm_w"][0]), 4, axis=1),
        "vnorm": column(I["ev_vnorm_w"][0].reshape(-1)),
        "conv_b0": column(I["ffn_conv_b"][0]), "conv_b1": column(I["ffn_conv_b"][1]),
        "qa_norm": column(I["od_qa_norm_w"][0]), "kva_norm": column(I["od_kva_norm_w"][0]),
        "q_nope": np.repeat(column(qn[:P]), 6, axis=1), "k_nope": np.repeat(column(kn[:P]), 6, axis=1),
        "q_pe": np.repeat(column(np.concatenate([qn[P:], qn[P:]])), 3, axis=1),
        "k_pe": column(np.concatenate([kn[P:], kn[P:]])),
        "conv_2": I["conv_w_2"][0].reshape(4, 24, P).transpose(2, 1, 0).reshape(P, -1),
        "dn_norm": np.repeat(column(I["dn_norm_w_2"][0]), 8, axis=1),
    }
    for name in ("a_log", "dt_bias"):
        parts[name] = np.concatenate([I[name + "_2"][0], np.zeros(P - 8, np.float32)])[:, None]
    for l in range(2):
        parts[f"conv_w{l}"] = I["ffn_conv_w"][l].reshape(3, FT, P).transpose(2, 1, 0).reshape(P, -1)
    A["cols"] = np.concatenate([parts[n] for n in COLUMNS.at], axis=1)
    more_layout(np, I, A, blocks, column)
    return {n: np.ascontiguousarray(a) for n, a in A.items()}


def kernel(**inputs):
    import numpy as np
    import concourse.bacc as bacc
    from concourse.bass_utils import run_bass_kernel_spmd

    arrays = _layout(np, {n: np.asarray(a) for n, a in inputs.items()})
    nc = bacc.Bacc("TRN2", target_bir_lowering=False, num_devices=1)
    A = {n: nc.dram_tensor("in_" + n, a.shape, F32, kind="ExternalInput").ap() for n, a in arrays.items()}
    out = nc.dram_tensor("out_t", (P, DT, LAT), F32, kind="ExternalOutput").ap()
    program(nc, A, out, None)
    r = run_bass_kernel_spmd(nc, [{"in_" + n: a for n, a in arrays.items()}], core_ids=[0])
    got = r.results[0]["out_t"]
    return np.ascontiguousarray(got.transpose(2, 1, 0).reshape(1, LAT, D))
```

```python
import concourse.bass as bass
from concourse import mybir
from contextlib import ExitStack

F32 = mybir.dt.float32
F32R = mybir.dt.float32r
ALU = mybir.AluOpType
ACT = mybir.ActivationFunctionType
AX = mybir.AxisListType

P = 128
D = 1024
DT = D // P
CTX = 256
LAT = 512
TOK = CTX + LAT
CHUNK = 128
EPS = 1e-6
F_MIN = 1e-6
D_FF = 2816
FT = D_FF // P
FH = FT // 2
RING_W = FH * P


class Core:

    def __init__(self, nc, ctx):
        self.nc = nc
        self.ctx = ctx
        self.spent = []
        self.raw = self.keep("w_raw", [P, 2, RING_W])
        self.whi = self.keep("w_hi", [P, 2, RING_W], F32R)
        self.wlo = self.keep("w_lo", [P, 2, RING_W], F32R)
        self.w_loaded = [ctx.enter_context(nc.semaphore(f"w_loaded{j}")) for j in range(2)]
        self.loads = [0, 0]
        self.split_ahead = False
        self.marks = self.keep("marks", [P, 2])
        self.rstd = self.keep("rstd", [P, TOK])

    def keep(self, name, shape, dt=F32):
        return self.ctx.enter_context(self.nc.sbuf_tensor(name, shape, dt))

    def signals(self, stage, names):
        new = [self.nc.alloc_semaphore(f"{stage}_{n}") for n in names.split()]
        if self.spent:
            self.nc.clear_and_free_semaphores(self.spent)
        self.spent = new
        return new

    def load_weights(self, sp, w, kt, i, j):
        sp.dma_start(self.raw[:, j, 0:kt * P], w[bass.ds(i * P, P), :]).then_inc(self.w_loaded[j], 16)

    def preload(self, sp, nxt):
        if nxt is None:
            return
        w, kt = nxt
        for j in range(2):
            self.load_weights(sp, w, kt, j, j)
            self.loads[j] += 1


def tile_pairs(eng, n, body):
    pairs = n // 2

    def pair(ip, first, last):
        for j in range(2):
            body(ip, j, 2 * ip + j, first, n % 2 == 1 and j == 0 if last else True)

    if pairs:
        pair(0, True, pairs == 1)
    if pairs > 4:
        with eng.Fori(1, pairs - 1) as ip:
            pair(ip, False, False)
    else:
        for ip in range(1, pairs - 1):
            pair(ip, False, False)
    if pairs > 1:
        pair(pairs - 1, False, True)
    if n % 2:
        body(pairs, 0, n - 1, pairs == 0, False)


class Side:

    def __init__(self, w_t, w_first, first, n, rows, scratch, bias, mod):
        self.w_t, self.w_first, self.first, self.n = w_t, w_first, first, n
        self.rows, self.scratch, self.bias, self.mod = rows, scratch, bias, mod
        self.vecs = rows.shape[1]

    def has(self, i):
        return not isinstance(i, int) or i < self.n


class Product:
    pass


def product(K, name, w, n, kt, rhs_hi, rhs_lo, t0, T, evac_act, evac_dve, nxt, extra="", side=None, rms_of=None):
    nc = K.nc
    with ExitStack() as c:
        acc = [c.enter_context(nc.psum_tensor(f"{name}_acc{j}", [P, 1024], F32)) for j in range(2)]
        hi_done, lo_done, mm_done, free0, free1, next_hi, side_loaded0, side_loaded1, side_done, side_biased, squared, summed, total, logged, *more = K.signals(
            name, "hi_done lo_done mm_done free0 free1 next_hi side_loaded0 side_loaded1 side_done "
            "side_biased squared summed total logged " + extra)
        if rms_of is not None:
            square = c.enter_context(nc.sbuf_tensor(f"{name}_square", [P, 2, T], F32))
            rms_ps = c.enter_context(nc.psum_tensor(f"{name}_rms_ps", [P, 1024], F32))
        if side is not None:
            assert side.n == n or n <= 8 or n - 2 <= side.n < n
            side_raw = c.enter_context(nc.sbuf_tensor(f"{name}_side_raw", [P, 2, D], F32))
            side_sum = c.enter_context(nc.sbuf_tensor(f"{name}_side_sum", [P, 2, side.vecs], F32))
            side_loaded = [side_loaded0, side_loaded1]
        free = [free0, free1]
        g = Product()
        g.free, g.mm_done, g.more = free, mm_done, more
        g.out = [a[:, 1024 - T:1024] for a in acc]
        banks = [(1024 - T, T - LAT), (512, LAT)] if T > LAT else [(512, T)]
        base = [16 * x for x in K.loads]
        given, K.split_ahead = K.split_ahead, nxt is not None
        next_width = nxt[1] * P if nxt is not None else None

        def slot_width():
            return kt * P

        with nc.Block() as block:
            @block.sync
            def _(sp):
                def load(ip, j, i, first, more):
                    if not first:
                        sp.wait_ge(hi_done, i - 1)
                        sp.wait_ge(lo_done, i - 1)
                        K.load_weights(sp, w, kt, i, j)
                tile_pairs(sp, n, load)
                if nxt is not None:
                    sp.wait_ge(hi_done, n)
                    sp.wait_ge(lo_done, n)
                K.loads[0] += (n + 1) // 2 - 1
                K.loads[1] += n // 2 - 1
                K.preload(sp, nxt)

            @block.gpsimd
            def _(pool):
                def load_side(ip, j, i, first, more):
                    if side.has(i):
                        if not first:
                            pool.wait_ge(side_done, (i - 1) * side.vecs)
                        row = (side.first - side.w_first + i) * P
                        pool.dma_start(side_raw[:, j, :], side.w_t[bass.ds(row, P), :]).then_inc(side_loaded[j], 16)
                if side is not None:
                    tile_pairs(pool, n, load_side)

            @block.scalar
            def _(act):
                def split_hi(ip, j, i, first):
                    act.wait_ge(K.w_loaded[j], 16 * ip + base[j])
                    if not first:
                        act.wait_ge(mm_done, i - 1)
                    nc.scalar.activation(K.whi[:, j, 0:slot_width()], K.raw[:, j, 0:slot_width()],
                                         ACT.Copy).then_inc(hi_done, 1)

                def split_next():
                    if nxt is not None:
                        act.wait_ge(K.w_loaded[0], 16 * ((n + 1) // 2) + base[0])
                        act.wait_ge(mm_done, n - 1 if n % 2 == 0 else n)
                        nc.scalar.activation(K.whi[:, 0, 0:next_width], K.raw[:, 0, 0:next_width],
                                             ACT.Copy).then_inc(next_hi, 1)

                def step(ip, j, i, first, more):
                    if more:
                        split_hi(ip + 1, j, i + 2, False)
                    if isinstance(i, int) and i == n - 1 and n % 2 == 0:
                        split_next()
                    evac_act(act, g, ip, j, i, first)
                    if isinstance(i, int) and i == n - 1 and n % 2 == 1:
                        split_next()
                    if rms_of is not None:
                        act.wait_ge(free[j], ip + 1)
                        if not first:
                            act.wait_ge(summed, i - 1)
                        nc.scalar.activation(square[:, j, :], rms_of[:, i, TOK - T:TOK],
                                             ACT.Square).then_inc(squared, 1)
                for j in range(min(n, 2)):
                    if j == 0 and given:
                        nc.scalar.activation(K.marks[:, 0:1], K.eps[:, 0:1], ACT.Copy).then_inc(hi_done, 1)
                    else:
                        split_hi(0, j, j, True)
                tile_pairs(act, n, step)
                if rms_of is not None:
                    act.wait_ge(total, 1)
                    nc.scalar.activation(K.rstd[:, TOK - T:TOK], rms_ps[:, 1024 - T:1024], ACT.Ln,
                                         bias=K.eps[:, 0:1], scale=1.0 / D).then_inc(logged, 1)
                    act.wait_ge(logged, 1)
                    nc.scalar.activation(K.rstd[:, TOK - T:TOK], K.rstd[:, TOK - T:TOK], ACT.Exp, scale=-0.5)

            @block.vector
            def _(dve):
                def split_lo(ip, j, i, first):
                    dve.wait_ge(hi_done, i + 1)
                    if not first:
                        dve.wait_ge(mm_done, i - 1)
                    nc.vector.tensor_tensor(K.wlo[:, j, 0:slot_width()], K.raw[:, j, 0:slot_width()],
                                            K.whi[:, j, 0:slot_width()].bitcast(F32),
                                            ALU.subtract).then_inc(lo_done, 1)

                def split_next():
                    if nxt is not None:
                        dve.wait_ge(next_hi, 1)
                        nc.vector.tensor_tensor(K.wlo[:, 0, 0:next_width], K.raw[:, 0, 0:next_width],
                                                K.whi[:, 0, 0:next_width].bitcast(F32), ALU.subtract)

                def step(ip, j, i, first, more):
                    if more:
                        split_lo(ip + 1, j, i + 2, False)
                    if isinstance(i, int) and i == n - 1 and n % 2 == 0:
                        split_next()
                    evac_dve(dve, g, ip, j, i, first)
                    if isinstance(i, int) and i == n - 1 and n % 2 == 1:
                        split_next()
                    if side is not None and side.has(i):
                        dve.wait_ge(side_loaded[j], 16 * ip + 16)
                        for m in range(side.vecs):
                            if not (first and j == 0 and m == 0):
                                dve.wait_ge(side_done, i * side.vecs + m)
                            if not first and m == 0:
                                dve.wait_ge(side_biased, i - 1)
                            nc.vector.tensor_tensor_reduce(
                                out=side.scratch, in0=side_raw[:, j, :], in1=side.rows[:, m, :], scale=1.0,
                                scalar=0.0, op0=ALU.mult, op1=ALU.add,
                                accum_out=side_sum[:, j, m:m + 1]).then_inc(side_done, 1)
                        dve.wait_ge(side_done, (i + 1) * side.vecs)
                        nc.vector.tensor_scalar(
                            side.mod[:, bass.ds(side.first + i, 1), :].rearrange("p a v -> p (a v)"),
                            side_sum[:, j, :], side.bias[:, bass.ds(side.first + i, 1)], None,
                            ALU.add).then_inc(side_biased, 1)
                for j in range(min(n, 2)):
                    if j == 0 and given:
                        nc.vector.memset(K.marks[:, 1:2], 0.0).then_inc(lo_done, 1)
                    else:
                        split_lo(0, j, j, True)
                tile_pairs(dve, n, step)

            @block.tensor
            def _(pe):
                def multiply(ip, j, i, first, more):
                    pe.wait_ge(lo_done, i + 1)
                    if not first:
                        pe.wait_ge(free[j], ip)
                    for col, width in banks:
                        at = col - (1024 - T)
                        for k in range(kt):
                            cols = slice(k * P, (k + 1) * P)
                            for part, (a, b) in enumerate(
                                    [(K.whi, rhs_hi), (K.whi, rhs_lo), (K.wlo, rhs_hi)]):
                                last = nc.tensor.matmul(
                                    acc[j][:, col:col + width], a[:, j, cols],
                                    b[:, k, t0 + at:t0 + at + width],
                                    start=(k == 0 and part == 0), stop=(k == kt - 1 and part == 2))
                    last.then_inc(mm_done, 1)
                    if rms_of is not None and i > 0:
                        sum_squares(i - 1).then_inc(summed, 1)

                def sum_squares(i):
                    pe.wait_ge(squared, i + 1)
                    for col, width in banks:
                        at = col - (1024 - T)
                        last = nc.tensor.matmul(rms_ps[:, col:col + width], K.ones[:, :],
                                                square[:, i % 2, at:at + width], start=(i == 0), stop=(i == n - 1))
                    return last
                tile_pairs(pe, n, multiply)
                if rms_of is not None:
                    sum_squares(n - 1).then_inc(total, 1)


def no_evac(eng, g, ip, j, i, first):
    pass


def copy_out(K, dst, func, others=()):
    def evac(act, g, ip, j, i, first):
        act.wait_ge(g.mm_done, i + 1)
        T = dst.shape[2]
        f = others[i] if isinstance(i, int) and i in others else func
        K.nc.scalar.activation(dst[:, bass.ds(i, 1), :].rearrange("p a t -> p (a t)"), g.out[j],
                               f).then_inc(g.free[j], 1)
    return evac


def add_gated(K, x, segs, t0):
    def evac(dve, g, ip, j, i, first):
        dve.wait_ge(g.mm_done, i + 1)
        for a, b, gate in segs:
            xs = x[:, bass.ds(i, 1), a:b].rearrange("p a t -> p (a t)")
            last = K.nc.vector.scalar_tensor_tensor(
                out=xs, in0=g.out[j][:, a - t0:b - t0], scalar=gate[:, bass.ds(i, 1)], in1=xs,
                op0=ALU.mult, op1=ALU.add)
        last.then_inc(g.free[j], 1)
    return evac


def split_parts(K, name, src, hi, lo):
    nc = K.nc
    hi_done, lo_done = K.signals(name, "hi_done lo_done")
    n = src.shape[1]
    half = (n + 1) // 2
    parts = [(0, half), (half, n)]
    with nc.Block() as block:
        @block.scalar
        def _(act):
            for a, b in parts:
                nc.scalar.activation(hi[:, a:b, :], src[:, a:b, :], ACT.Copy).then_inc(hi_done, 1)

        @block.vector
        def _(dve):
            for m, (a, b) in enumerate(parts):
                dve.wait_ge(hi_done, m + 1)
                nc.vector.tensor_tensor(lo[:, a:b, :], src[:, a:b, :], hi[:, a:b, :].bitcast(F32),
                                        ALU.subtract)


def model_norm(K, name, x, t0, T, mods, hi=None, lo=None, plain=None, work=None,
               rows=None, given=True):
    nc = K.nc
    Q = 2
    pieces = [(s, s + Q) for s in range(0, DT, Q)]
    with ExitStack() as c:
        if work is None:
            work = c.enter_context(nc.sbuf_tensor(f"{name}_work", [P, DT, T], F32))
        rstd = K.rstd[:, t0:t0 + T]
        ps = c.enter_context(nc.psum_tensor(f"{name}_ps", [P, 1024], F32))
        squared, total, logged, rooted, scaled, hi_done, rows_in = K.signals(
            name, "squared total logged rooted scaled hi_done rows_in")
        banks = [(1024 - T, T - LAT), (512, LAT)] if T > LAT else [(512, T)]
        with nc.Block() as block:
            @block.scalar
            def _(act):
                if not given:
                    for a, b in pieces:
                        nc.scalar.activation(work[:, a:b, :], x[:, a:b, t0:t0 + T], ACT.Square).then_inc(squared, 1)
                    act.wait_ge(total, 1)
                    nc.scalar.activation(rstd, ps[:, 1024 - T:1024], ACT.Ln, bias=K.eps[:, 0:1],
                                         scale=1.0 / D).then_inc(logged, 1)
                    act.wait_ge(logged, 1)
                    nc.scalar.activation(rstd, rstd, ACT.Exp, scale=-0.5).then_inc(rooted, 1)
                if hi is not None:
                    for s, (a, b) in enumerate(pieces):
                        act.wait_ge(scaled, s + 1)
                        for k in range(a, b):
                            for f, t, scale, shift in mods:
                                last = nc.scalar.activation(hi[:, k, f:t], work[:, k, f:t], ACT.Identity,
                                                            bias=shift[:, k:k + 1])
                        last.then_inc(hi_done, 1)
                if rows is not None:
                    act.wait_ge(rows_in, 16)
                    nc.scalar.activation(rows[0], rows[0], ACT.Silu)

            @block.sync
            def _(sp):
                if rows is not None:
                    sp.dma_start(rows[0], rows[1]).then_inc(rows_in, 16)

            @block.tensor
            def _(pe):
                for s, (a, b) in enumerate([] if given else pieces):
                    pe.wait_ge(squared, s + 1)
                    for k in range(a, b):
                        for col, width in banks:
                            at = col - (1024 - T)
                            last = nc.tensor.matmul(ps[:, col:col + width], K.ones[:, :],
                                                    work[:, k, at:at + width], start=(k == 0), stop=(k == DT - 1))
                if not given:
                    last.then_inc(total, 1)

            @block.vector
            def _(dve):
                dst = work if plain is None else plain
                if not given:
                    dve.wait_ge(rooted, 1)

                def lower(s):
                    a, b = pieces[s]
                    dve.wait_ge(hi_done, s + 1)
                    for k in range(a, b):
                        for f, t, scale, shift in mods:
                            nc.vector.scalar_tensor_tensor(out=lo[:, k, f:t], in0=work[:, k, f:t],
                                                           scalar=shift[:, k:k + 1],
                                                           in1=hi[:, k, f:t].bitcast(F32),
                                                           op0=ALU.add, op1=ALU.subtract)
                for s, (a, b) in enumerate(pieces):
                    for k in range(a, b):
                        for f, t, scale, shift in mods:
                            last = nc.vector.scalar_tensor_tensor(out=dst[:, k, f:t], in0=x[:, k, t0 + f:t0 + t],
                                                                  scalar=scale[:, k:k + 1], in1=rstd[:, f:t],
                                                                  op0=ALU.mult, op1=ALU.mult)
                    last.then_inc(scaled, 1)
                    if hi is not None and s > 0:
                        lower(s - 1)
                if hi is not None:
                    lower(len(pieces) - 1)


def group_norm(K, name, src, dst, n, kt, T, weights, ones, scale, roots=None):
    nc = K.nc
    with ExitStack() as c:
        sq = c.enter_context(nc.sbuf_tensor(f"{name}_sq", [P, 2, kt, T], F32))
        if roots is None:
            roots = c.enter_context(nc.sbuf_tensor(f"{name}_roots", [P, n, T], F32))
        ps = [c.enter_context(nc.psum_tensor(f"{name}_ps{j}", [P, 1024], F32)) for j in range(2)]
        squared, total, logged, rooted = K.signals(name, "squared total logged rooted")
        banks = [(1024 - T, T - LAT), (512, LAT)] if T > LAT else [(512, T)]
        Q = min(n, 2)
        steps = [(a, min(a + Q, n)) for a in range(0, n, Q)]
        with nc.Block() as block:
            @block.scalar
            def _(act):
                for i in range(n):
                    act.wait_ge(total, i + 1)
                    nc.scalar.activation(roots[:, i, :], ps[i % 2][:, 1024 - T:1024], ACT.Ln,
                                         bias=K.eps[:, 0:1], scale=scale).then_inc(logged, 1)
                for a, b in steps:
                    act.wait_ge(logged, b)
                    nc.scalar.activation(roots[:, a:b, :], roots[:, a:b, :], ACT.Exp, scale=-0.5).then_inc(rooted, 1)

            @block.tensor
            def _(pe):
                for i in range(n):
                    pe.wait_ge(squared, i + 1)
                    if i >= 2:
                        pe.wait_ge(logged, i - 1)
                    for col, width in banks:
                        at = col - (1024 - T)
                        for k in range(kt):
                            last = nc.tensor.matmul(ps[i % 2][:, col:col + width], ones[:, :],
                                                    sq[:, i % 2, k, at:at + width],
                                                    start=(k == 0), stop=(k == kt - 1))
                    last.then_inc(total, 1)

            @block.vector
            def _(dve):
                for i in range(n):
                    if i >= 2:
                        dve.wait_ge(total, i - 1)
                    nc.vector.tensor_tensor(sq[:, i % 2], src[:, i * kt:(i + 1) * kt, :],
                                            src[:, i * kt:(i + 1) * kt, :], ALU.mult).then_inc(squared, 1)
                for s, (a, b) in enumerate(steps):
                    dve.wait_ge(rooted, s + 1)
                    if weights is None:
                        nc.vector.tensor_tensor(dst[:, a:b, :], src[:, a:b, :], roots[:, a:b, :], ALU.mult)
                        continue
                    for i in range(a, b):
                        for m in range(i * kt, (i + 1) * kt):
                            nc.vector.scalar_tensor_tensor(out=dst[:, m, :], in0=src[:, m, :],
                                                           scalar=weights[:, m:m + 1], in1=roots[:, i, :],
                                                           op0=ALU.mult, op1=ALU.mult)


def modulation(K, name, w, n, cols, vecs, bias, mod, nxt, also):
    nc = K.nc
    Q = 4
    with ExitStack() as c:
        raw = c.enter_context(nc.sbuf_tensor(f"{name}_raw", [P, n, D], F32))
        ps = [c.enter_context(nc.psum_tensor(f"{name}_ps{j}", [P, 512], F32)) for j in range(n // Q)]
        loaded = K.signals(name, " ".join(f"loaded{q}" for q in range(n // Q)) + " mm_done also_loaded")
        mm_done, also_loaded = loaded[n // Q:]
        with nc.Block() as block:
            @block.sync
            def _(sp):
                for q in range(n // Q):
                    for i in range(q * Q, (q + 1) * Q):
                        sp.dma_start(raw[:, i, :], w[i * P:(i + 1) * P, :]).then_inc(loaded[q], 16)
                sp.dma_start(also[0], also[1]).then_inc(also_loaded, 16)
                K.preload(sp, nxt)
                sp.wait_ge(also_loaded, 16)

            @block.tensor
            def _(pe):
                for q in range(n // Q):
                    pe.wait_ge(loaded[q], 16 * Q)
                    for m in range(Q):
                        for k in range(DT):
                            last = nc.tensor.matmul(ps[q][:, m * vecs:(m + 1) * vecs],
                                                    raw[:, q * Q + m, k * P:(k + 1) * P],
                                                    cols[:, k, 0:vecs], start=(k == 0), stop=(k == DT - 1))
                    last.then_inc(mm_done, 1)

            @block.vector
            def _(dve):
                for q in range(n // Q):
                    dve.wait_ge(mm_done, q + 1)
                    nc.vector.tensor_tensor(
                        mod[:, q * Q:(q + 1) * Q, 0:vecs],
                        ps[q][:, 0:Q * vecs].rearrange("p (m v) -> p m v", v=vecs),
                        bias[:, q * Q:(q + 1) * Q].unsqueeze(2).to_broadcast([P, Q, vecs]), ALU.add)


def norm_scales(K, name, pairs):
    nc = K.nc
    one_more, = K.signals(name, "one_more")
    with nc.Block() as block:
        @block.vector
        def _(dve):
            for n, (out, norm_w, scale) in enumerate(pairs):
                nc.vector.tensor_scalar(out, scale, 1.0, None, ALU.add).then_inc(one_more, 1)
            for n, (out, norm_w, scale) in enumerate(pairs):
                dve.wait_ge(one_more, n + 1)
                nc.vector.tensor_tensor(out, out, norm_w, ALU.mult)


def feed_forward(K, name, x, t0, T, hi, lo, w_up, w_down, conv_w, conv_b, gates, nxt, sides):
    nc = K.nc
    segs = [(0, CTX), (CTX, TOK)] if T > LAT else [(0, LAT)]
    with ExitStack() as c:
        hid_hi = c.enter_context(nc.sbuf_tensor(f"{name}_hid_hi", [P, FH, T], F32R))
        hid_lo = c.enter_context(nc.sbuf_tensor(f"{name}_hid_lo", [P, FH, T], F32R))
        for f in range(2):
            with ExitStack() as c2:
                gate_sb = c2.enter_context(nc.sbuf_tensor(f"{name}{f}_gate", [P, T], F32))
                conv = c2.enter_context(nc.sbuf_tensor(f"{name}{f}_conv", [P, T], F32))
                hid = c2.enter_context(nc.sbuf_tensor(f"{name}{f}_hid", [P, T], F32))

                def act_part(act, g, ip, j, i, first):
                    conv0, conv1, conv2, silu_done, hid_done, hi_out = g.more
                    act.wait_ge(g.mm_done, i + 1)
                    if j == 0:
                        if not first:
                            act.wait_ge(conv2, ip)
                        nc.scalar.activation(gate_sb[:, :], g.out[0], ACT.Copy).then_inc(g.free[0], 1)
                        act.wait_ge(conv2, ip + 1)
                        nc.scalar.activation(conv[:, :], conv[:, :], ACT.Silu).then_inc(silu_done, 1)
                    else:
                        act.wait_ge(g.free[1], ip + 1)
                        nc.scalar.activation(hid_hi[:, bass.ds(ip, 1), :].rearrange("p a t -> p (a t)"),
                                             hid[:, :], ACT.Copy).then_inc(hi_out, 1)

                def dve_part(dve, g, ip, j, i, first, f=f):
                    conv0, conv1, conv2, silu_done, hid_done, hi_out = g.more
                    if j == 0:
                        def tap(m):
                            return conv_w[:, bass.ds((ip + f * FH) * 3 + m, 1)]
                        dve.wait_ge(g.free[0], ip + 1)
                        if not first:
                            dve.wait_ge(g.free[1], ip)
                        nc.vector.tensor_scalar(conv[:, :], gate_sb[:, :], tap(1),
                                                conv_b[:, bass.ds(ip + f * FH, 1)],
                                                ALU.mult, ALU.add).then_inc(conv0, 1)
                        dve.wait_ge(conv0, ip + 1)
                        for a, b in segs:
                            last = nc.vector.scalar_tensor_tensor(
                                out=conv[:, a + 1:b], in0=gate_sb[:, a:b - 1], scalar=tap(0),
                                in1=conv[:, a + 1:b], op0=ALU.mult, op1=ALU.add)
                        last.then_inc(conv1, 1)
                        dve.wait_ge(conv1, ip + 1)
                        for a, b in segs:
                            last = nc.vector.scalar_tensor_tensor(
                                out=conv[:, a:b - 1], in0=gate_sb[:, a + 1:b], scalar=tap(2),
                                in1=conv[:, a:b - 1], op0=ALU.mult, op1=ALU.add)
                        last.then_inc(conv2, 1)
                    else:
                        dve.wait_ge(g.mm_done, i + 1)
                        dve.wait_ge(silu_done, ip + 1)
                        if not first:
                            dve.wait_ge(hid_done, ip)
                        nc.vector.tensor_tensor(hid[:, :], conv[:, :], g.out[1],
                                                ALU.mult).then_inc(g.free[1], 1)
                        dve.wait_ge(hi_out, ip + 1)
                        h = bass.ds(ip, 1)
                        nc.vector.tensor_tensor(hid_lo[:, h, :].rearrange("p a t -> p (a t)"), hid[:, :],
                                                hid_hi[:, h, :].rearrange("p a t -> p (a t)").bitcast(F32),
                                                ALU.subtract).then_inc(hid_done, 1)

                product(K, f"{name}_up{f}", w_up[f * 2 * FH * P:(f + 1) * 2 * FH * P, :], 2 * FH, DT, hi, lo,
                        0, T, act_part, dve_part, (w_down[f * DT * P:(f + 1) * DT * P, :], FH),
                        "conv0 conv1 conv2 silu_done hid_done hi_out", side=sides[2 * f])
            after = (w_up[2 * FH * P:4 * FH * P, :], DT) if f == 0 else nxt
            product(K, f"{name}_down{f}", w_down[f * DT * P:(f + 1) * DT * P, :], DT, FH, hid_hi, hid_lo,
                    0, T, no_evac, add_gated(K, x, gates, t0), after, side=sides[2 * f + 1],
                    rms_of=x if f == 1 else None)


A_HEADS = 4
B_GROUPS = 4
LEVELS = (128, 64, 32, 16, 8)


def chunk_mlp(K, uv, ws_t, bs_row, out):
    nc = K.nc
    n_chunks = TOK // CHUNK
    with ExitStack() as c:
        ws = c.enter_context(nc.sbuf_tensor("cm_ws", [P, B_GROUPS * CHUNK], F32))
        bs = c.enter_context(nc.sbuf_tensor("cm_bs", [1, B_GROUPS * CHUNK], F32))
        vt = c.enter_context(nc.sbuf_tensor("cm_vt", [P, 2, B_GROUPS * P], F32))
        ps_t = [c.enter_context(nc.psum_tensor(f"cm_ps_t{j}", [P, 512], F32)) for j in range(2)]
        ps_s = [c.enter_context(nc.psum_tensor(f"cm_ps_s{j}", [P, 512], F32)) for j in range(2)]
        loaded, turned, vt_ready, mixed, gated = K.signals("cm", "loaded turned vt_ready mixed gated")
        with nc.Block() as block:
            @block.sync
            def _(sp):
                sp.dma_start(ws[:, :], ws_t).then_inc(loaded, 16)
                sp.dma_start(bs[:, :], bs_row).then_inc(loaded, 16)

            @block.tensor
            def _(pe):
                pe.wait_ge(loaded, 32)

                def turn(n):
                    if n >= 2:
                        pe.wait_ge(vt_ready, n - 1)
                    for g in range(B_GROUPS):
                        last = nc.tensor.transpose(ps_t[n % 2][:, g * P:(g + 1) * P],
                                                   uv[:, B_GROUPS + g, n * CHUNK:(n + 1) * CHUNK], K.ident[:, :])
                    last.then_inc(turned, 1)

                def mix(n):
                    pe.wait_ge(vt_ready, n + 1)
                    if n >= 2:
                        pe.wait_ge(gated, n - 1)
                    for g in range(B_GROUPS):
                        cols = slice(g * P, (g + 1) * P)
                        nc.tensor.matmul(ps_s[n % 2][:, cols], vt[:, n % 2, cols], ws[:, cols],
                                         start=True, stop=False)
                        last = nc.tensor.matmul(ps_s[n % 2][:, cols], K.ones[0:1, :], bs[:, cols],
                                                start=False, stop=True)
                    last.then_inc(mixed, 1)
                turn(0)
                for n in range(n_chunks):
                    if n + 1 < n_chunks:
                        turn(n + 1)
                    mix(n)

            @block.scalar
            def _(act):
                for n in range(n_chunks):
                    act.wait_ge(turned, n + 1)
                    if n >= 2:
                        act.wait_ge(mixed, n - 1)
                    nc.scalar.activation(vt[:, n % 2, :], ps_t[n % 2][:, :], ACT.Copy).then_inc(vt_ready, 1)

            @block.vector
            def _(dve):
                for n in range(n_chunks):
                    dve.wait_ge(mixed, n + 1)
                    nc.vector.tensor_tensor(out[:, :, n * CHUNK:(n + 1) * CHUNK],
                                            uv[:, 0:B_GROUPS, n * CHUNK:(n + 1) * CHUNK],
                                            ps_s[n % 2][:, :].rearrange("p (g t) -> p g t", g=B_GROUPS),
                                            ALU.mult).then_inc(gated, 1)


def gla_features(K, zf, kf, lb_cols):
    nc = K.nc
    n_dir = 2 * A_HEADS
    with ExitStack() as c:
        lb = c.enter_context(nc.sbuf_tensor("gf_lb", [P, 5, n_dir], F32))
        keep = c.enter_context(nc.sbuf_tensor("gf_keep", [P, 2, TOK], F32))
        logits_up, e_done, p_inv, p_done, lb_done, sig, f1, f2, k_done, logs, marks, one_minus = K.signals(
            "gf", "logits_up e_done p_inv p_done lb_done sig f1 f2 k_done logs marks one_minus")
        with nc.Block() as block:
            @block.scalar
            def _(act):
                for s in range(2):
                    nc.scalar.activation(zf[:, s * A_HEADS:(s + 1) * A_HEADS, :],
                                         zf[:, s * A_HEADS:(s + 1) * A_HEADS, :], ACT.Sigmoid).then_inc(sig, 1)
                act.wait_ge(logits_up, 1)
                nc.scalar.activation(lb[:, 1, :], lb[:, 0, :], ACT.Exp).then_inc(e_done, 1)
                for s in range(2):
                    act.wait_ge(k_done, s + 1)
                    nc.scalar.activation(zf[:, s * A_HEADS:(s + 1) * A_HEADS, :],
                                         zf[:, s * A_HEADS:(s + 1) * A_HEADS, :], ACT.Ln).then_inc(logs, 1)

            @block.vector
            def _(dve):
                nc.vector.tensor_tensor(lb[:, 0, :], lb_cols, lb_cols, ALU.subtract).then_inc(logits_up, 1)
                nc.vector.memset(keep[:, :, :], 1.0).then_inc(marks, 1)
                dve.wait_ge(marks, 1)
                nc.vector.memset(keep[:, 0, 0:TOK:CHUNK], 0.0)
                nc.vector.memset(keep[:, 1, CHUNK - 1:TOK:CHUNK], 0.0).then_inc(marks, 1)
                dve.wait_ge(e_done, 1)
                nc.vector.reciprocal(lb[:, 2, :], lb[:, 1, :]).then_inc(p_inv, 1)
                dve.wait_ge(p_inv, 1)
                nc.vector.tensor_tensor(lb[:, 2, :], lb[:, 1, :], lb[:, 2, :], ALU.mult).then_inc(p_done, 1)
                dve.wait_ge(p_done, 1)
                nc.vector.tensor_tensor(lb[:, 3, :], lb[:, 2, :], lb[:, 2, :], ALU.subtract).then_inc(lb_done, 1)
                dve.wait_ge(lb_done, 1)
                nc.vector.tensor_scalar(lb[:, 4, :], lb[:, 3, :], -1.0, 1.0, ALU.mult, ALU.add).then_inc(one_minus, 1)
                dve.wait_ge(one_minus, 1)
                for s in range(2):
                    rows = slice(s * A_HEADS, (s + 1) * A_HEADS)
                    dve.wait_ge(sig, s + 1)
                    for m in range(s * A_HEADS, (s + 1) * A_HEADS):
                        last = nc.vector.tensor_scalar(zf[:, m, :], zf[:, m, :], lb[:, 4, m:m + 1],
                                                       lb[:, 3, m:m + 1], ALU.mult, ALU.add)
                    last.then_inc(f1, 1)
                    dve.wait_ge(f1, s + 1)
                    nc.vector.tensor_scalar(zf[:, rows, :], zf[:, rows, :], F_MIN, None, ALU.max).then_inc(f2, 1)
                    dve.wait_ge(f2, s + 1)
                    nc.vector.tensor_scalar(kf[:, rows, :], zf[:, rows, :], -1.0, 1.0,
                                            ALU.mult, ALU.add).then_inc(k_done, 1)
                dve.wait_ge(marks, 2)
                for s in range(2):
                    dve.wait_ge(logs, s + 1)
                    for m in range(s * A_HEADS, (s + 1) * A_HEADS):
                        order = slice(None, None, -1) if s else slice(None)
                        nc.vector.tensor_tensor_scan(zf[:, m, order], keep[:, s, order], zf[:, m, order],
                                                     0.0, ALU.mult, ALU.add)


def gla_both(K, q, v, k, b, masks, spare, spare2):
    nc = K.nc
    H = A_HEADS
    NL = len(LEVELS)
    W = H * CHUNK
    STEPS = TOK // CHUNK
    FIRST = CTX // CHUNK
    names = ("m_loaded turn_done q_in k_in v_in b_in rel_done grown eb_done mixed_done ends_done "
             "v_turned k_turned kt_done vt_done scored masked o_done u_done fours_done o_taken").split()
    with ExitStack() as c:
        made = K.signals("gl", " ".join(f"{n}{d}" for d in range(2) for n in names))
        (m_loaded, turn_done, q_in, k_in, v_in, b_in, rel_done, grown, eb_done, mixed_done, ends_done,
         v_turned, k_turned, kt_done, vt_done, scored, masked, o_done, u_done, fours_done, o_taken) = [
            (made[m], made[len(names) + m]) for m in range(len(names))]

        def sb(n, shape):
            return c.enter_context(nc.sbuf_tensor(f"gl_{n}", shape, F32))[tuple(slice(None) for _ in shape)]

        flat_a, flat_b = (a.rearrange("p a t -> p (a t)") for a in (spare[:, :, :], spare2[:, :, :]))
        rel = (sb("rel", [P, NL + 3, W]),
               flat_a[:, 0:(NL + 3) * W].rearrange("p (r w) -> p r w", w=W))
        small = [(sb(n, [P, W]), flat_a[:, (NL + 3 + m) * W:(NL + 4 + m) * W])
                 for m, n in enumerate(("qc", "kc", "vc", "bc"))]
        qc, kc, vc, bc = small
        small = [(sb(n, [P, W]), flat_b[:, m * W:(m + 1) * W]) for m, n in enumerate(("eb", "qb", "kt", "vt"))]
        eb, qb, kt, vt = small
        mask = (K.rstd[:, :].rearrange("p (l t) -> p l t", t=CHUNK),
                flat_b[:, 4 * W:4 * W + (NL + 1) * CHUNK].rearrange("p (l t) -> p l t", t=CHUNK))
        rest_b = flat_b[:, 4 * W + (NL + 1) * CHUNK:].rearrange("p (h t) -> p h t", t=P)
        state = [[sb("state0", [P, H, P])], [sb("state1", [P, H - rest_b.shape[1], P]), rest_b]]

        def state_of(d, h):
            for piece in state[d]:
                if h < piece.shape[1]:
                    return piece[:, h, :]
                h -= piece.shape[1]
        banks = [[c.enter_context(nc.psum_tensor(f"gl_bank{d}{m}", [P, 512], F32))[:, :] for m in range(4)]
                 for d in range(2)]
        ps_u, ps_o = [bk[2] for bk in banks], [bk[3] for bk in banks]

        def halves(eng, begin, whole, end):
            def at(d, s):
                if d == 0:
                    return s * CHUNK
                if isinstance(s, int):
                    return (FIRST - 1 - s if s < FIRST else STEPS - 1 - s + FIRST) * CHUNK
                return (STEPS - 1 + FIRST) * CHUNK - s * CHUNK

            def prior(s):
                return at(1, s - 1) if isinstance(s, int) else (STEPS + FIRST) * CHUNK - s * CHUNK
            for s in range(FIRST + 1):
                if s == 0:
                    begin(0, 0, at(0, 0))
                else:
                    whole(0, s, at(0, s), s - 1, prior(s))
                whole(1, s, at(1, s), s, at(0, s))
            with eng.Fori(FIRST + 1, STEPS) as s:
                whole(0, s, at(0, s), s - 1, prior(s))
                whole(1, s, at(1, s), s, TOK - (TOK - s * CHUNK))
            end(1, STEPS - 1, at(1, STEPS - 1))

        def heads(t, at):
            return t[:, :, bass.ds(at, CHUNK)]

        def flat(t):
            return t.rearrange("p (h t) -> p h t", h=H)

        def cols(h):
            return slice(h * P, (h + 1) * P)

        def own(t, d):
            return t[:, d * H:(d + 1) * H, :]

        with nc.Block() as block:
            @block.sync
            def _(sp):
                for d in range(2):
                    sp.dma_start(mask[d], masks[d]).then_inc(m_loaded[d], 16)

            @block.scalar
            def _(act):
                def copies(d, s, at):
                    if not (isinstance(s, int) and s == 0):
                        act.wait_ge(rel_done[d], s)
                        act.wait_ge(eb_done[d], s)
                    nc.scalar.activation(flat(bc[d]), heads(own(b, d), at), ACT.Copy).then_inc(b_in[d], 1)
                    if not (isinstance(s, int) and s == 0):
                        act.wait_ge(mixed_done[d], s)
                        act.wait_ge(v_turned[d], s)
                    nc.scalar.activation(flat(kc[d]), heads(own(k, d), at), ACT.Copy).then_inc(k_in[d], 1)
                    nc.scalar.activation(flat(qc[d]), heads(q, at), ACT.Copy).then_inc(q_in[d], 1)
                    nc.scalar.activation(flat(vc[d]), heads(v, at), ACT.Copy).then_inc(v_in[d], 1)

                def transposed(d, s):
                    act.wait_ge(v_turned[d], s + 1)
                    nc.scalar.activation(vt[d], ps_o[d], ACT.Copy).then_inc(vt_done[d], 1)
                    act.wait_ge(k_turned[d], s + 1)
                    nc.scalar.activation(kt[d], ps_u[d], ACT.Copy).then_inc(kt_done[d], 1)

                def grow(d, s):
                    act.wait_ge(b_in[d], s + 1)
                    act.wait_ge(rel_done[d], s + 1)
                    nc.scalar.activation(rel[d][:, NL + 1, :], rel[d][:, NL, :], ACT.Exp,
                                         scale=-1.0).then_inc(fours_done[d], 1)
                    nc.scalar.activation(rel[d][:, NL + 2, :], rel[d][:, NL + 2, :], ACT.Exp)
                    act.wait_ge(fours_done[d], s + 1)
                    nc.scalar.activation(rel[d][:, 0:NL + 1, :], rel[d][:, 0:NL + 1, :], ACT.Exp).then_inc(grown[d], 1)
                    nc.scalar.activation(eb[d], bc[d], ACT.Exp).then_inc(eb_done[d], 1)

                def begin(d, s, at):
                    copies(d, s, at)
                    grow(d, s)

                def whole(d, s, at, so, at_o):
                    copies(d, s, at)
                    transposed(1 - d, so)
                    grow(d, s)
                    take_out(1 - d, so, at_o)

                def take_out(d, s, at):
                    act.wait_ge(k_in[d], s + 1)
                    act.wait_ge(o_done[d], s + 1)
                    nc.scalar.activation(heads(own(k, d), at), flat(ps_o[d]), ACT.Copy).then_inc(o_taken[d], 1)

                def end(d, s, at):
                    transposed(d, s)
                    take_out(d, s, at)
                halves(act, begin, whole, end)

            @block.vector
            def _(dve):
                for d in range(2):
                    for piece in state[d]:
                        last = nc.vector.memset(piece, 0.0)
                    last.then_inc(turn_done[d], 1)
                for d in range(2):
                    dve.wait_ge(m_loaded[d], 16)

                def exponents(d, s):
                    dve.wait_ge(b_in[d], s + 1)
                    for l, size in enumerate(LEVELS):
                        ref = size // 2 if d else size // 2 - 1
                        bb = bc[d].rearrange("p (n e) -> p n e", e=size)
                        rr = rel[d][:, l, :].rearrange("p (n e) -> p n e", e=size)
                        h = size // 2
                        rb = bb[:, :, ref:ref + 1].to_broadcast([P, W // size, h])
                        late, early = (slice(0, h), slice(h, size)) if d else (slice(h, size), slice(0, h))
                        nc.vector.tensor_tensor(rr[:, :, late], bb[:, :, late], rb, ALU.subtract)
                        nc.vector.tensor_tensor(rr[:, :, early], rb, bb[:, :, early], ALU.subtract)
                    bb = bc[d].rearrange("p (n e) -> p n e", e=4)
                    ref = bb[:, :, (2 if d else 1):(3 if d else 2)].to_broadcast([P, W // 4, 4])
                    nc.vector.tensor_tensor(rel[d][:, NL, :].rearrange("p (n e) -> p n e", e=4), bb, ref,
                                            ALU.subtract)
                    bh = flat(bc[d])
                    end = bh[:, :, (0 if d else CHUNK - 1):(1 if d else CHUNK)].to_broadcast([P, H, CHUNK])
                    nc.vector.tensor_tensor(flat(rel[d][:, NL + 2, :]), end, bh, ALU.subtract).then_inc(rel_done[d], 1)

                def decayed(d, s):
                    dve.wait_ge(k_in[d], s + 1)
                    dve.wait_ge(grown[d], s + 1)
                    nc.vector.tensor_tensor(rel[d][:, NL + 2, :], kc[d], rel[d][:, NL + 2, :],
                                            ALU.mult).then_inc(ends_done[d], 1)
                    dve.wait_ge(q_in[d], s + 1)
                    for l, size in enumerate(LEVELS):
                        h = size // 2
                        for src, half in ((qc, slice(0, h) if d else slice(h, size)),
                                          (kc, slice(h, size) if d else slice(0, h))):
                            def blocks(t):
                                return t.rearrange("p (n e) -> p n e", e=size)[:, :, half]
                            nc.vector.tensor_tensor(blocks(rel[d][:, l, :]), blocks(src[d]),
                                                    blocks(rel[d][:, l, :]), ALU.mult)
                    nc.vector.tensor_tensor(rel[d][:, NL, :], qc[d], rel[d][:, NL, :], ALU.mult)
                    nc.vector.tensor_tensor(rel[d][:, NL + 1, :], kc[d], rel[d][:, NL + 1, :], ALU.mult)
                    dve.wait_ge(eb_done[d], s + 1)
                    nc.vector.tensor_tensor(qb[d], qc[d], eb[d], ALU.mult).then_inc(mixed_done[d], 1)

                def masking(d, s):
                    for l in range(NL + 1):
                        dve.wait_ge(scored[d], (NL + 1) * s + l + 1)
                        nc.vector.tensor_tensor(flat(rel[d][:, l, :]), flat(banks[d][l % 4]),
                                                mask[d][:, l, :].unsqueeze(1).to_broadcast([P, H, CHUNK]),
                                                ALU.mult).then_inc(masked[d], 1)

                def take(d, s, at):
                    dve.wait_ge(o_done[d], s + 1)
                    dve.wait_ge(turn_done[d], s + 1)
                    dve.wait_ge(u_done[d], s + 1)
                    for h in range(H):
                        at_end = h * CHUNK + (0 if d else CHUNK - 1)
                        last = nc.vector.scalar_tensor_tensor(
                            out=state_of(d, h), in0=state_of(d, h), scalar=eb[d][:, at_end:at_end + 1],
                            in1=ps_u[d][:, cols(h)], op0=ALU.mult, op1=ALU.add)
                    last.then_inc(turn_done[d], 1)

                def begin(d, s, at):
                    exponents(d, s)
                    decayed(d, s)

                def whole(d, s, at, so, at_o):
                    exponents(d, s)
                    masking(1 - d, so)
                    decayed(d, s)
                    take(1 - d, so, at_o)

                def end(d, s, at):
                    masking(d, s)
                    take(d, s, at)
                halves(dve, begin, whole, end)

            @block.tensor
            def _(pe):
                def score(d, s):
                    pe.wait_ge(turn_done[d], s + 1)
                    if not (isinstance(s, int) and s == 0):
                        pe.wait_ge(o_taken[d], s)
                    pe.wait_ge(v_in[d], s + 1)
                    for h in range(H):
                        last = nc.tensor.transpose(ps_o[d][:, cols(h)], vc[d][:, cols(h)], K.ident[:, :])
                    last.then_inc(v_turned[d], 1)
                    pe.wait_ge(ends_done[d], s + 1)
                    for h in range(H):
                        last = nc.tensor.transpose(ps_u[d][:, cols(h)], rel[d][:, NL + 2, cols(h)], K.ident[:, :])
                    last.then_inc(k_turned[d], 1)
                    pe.wait_ge(mixed_done[d], s + 1)
                    for l in range(NL + 1):
                        if l == 2:
                            pe.wait_ge(kt_done[d], s + 1)
                        elif l == 3:
                            pe.wait_ge(vt_done[d], s + 1)
                        elif l > 3:
                            pe.wait_ge(masked[d], (NL + 1) * s + l - 3)
                        for h in range(H):
                            last = nc.tensor.matmul(banks[d][l % 4][:, cols(h)],
                                                    rel[d][:, l if l < NL else NL + 1, cols(h)],
                                                    rel[d][:, l, cols(h)], start=True, stop=True)
                        last.then_inc(scored[d], 1)

                def read_out(d, s):
                    pe.wait_ge(masked[d], (NL + 1) * s + NL + 1)
                    for h in range(H):
                        nc.tensor.matmul(ps_o[d][:, cols(h)], state_of(d, h), qb[d][:, cols(h)],
                                         start=True, stop=False)
                        for l in range(NL + 1):
                            last = nc.tensor.matmul(ps_o[d][:, cols(h)], vt[d][:, cols(h)], rel[d][:, l, cols(h)],
                                                    start=False, stop=(l == NL))
                    last.then_inc(o_done[d], 1)
                    for h in range(H):
                        last = nc.tensor.matmul(ps_u[d][:, cols(h)], kt[d][:, cols(h)], vt[d][:, cols(h)],
                                                start=True, stop=True)
                    last.then_inc(u_done[d], 1)

                def whole(d, s, at, so, at_o):
                    read_out(1 - d, so)
                    score(d, s)
                halves(pe, lambda d, s, at: score(d, s), whole, lambda d, s, at: read_out(d, s))


def add_directions(K, name, k, out, x, x_in, x_back):
    nc = K.nc
    H = A_HEADS
    K.signals(name, "none")
    with nc.Block() as block:
        @block.sync
        def _(sp):
            sp.dma_start(x, x_in).then_inc(x_back, 16)

        @block.vector
        def _(dve):
            nc.vector.tensor_tensor(out[:, :, :], k[:, 0:H, :], k[:, H:2 * H, :], ALU.add)


def gated_readout(K, name, o, g, hi, lo, also=None):
    nc = K.nc
    n = o.shape[1]
    gated, hi_done, also_done = K.signals(name, "gated hi_done also_done")
    n_all = n + (also.shape[1] if also is not None else 0)
    with nc.Block() as block:
        @block.vector
        def _(dve):
            nc.vector.tensor_tensor(o[:, :, :], o[:, :, :], g[:, :, :], ALU.mult).then_inc(gated, 1)
            if also is not None:
                dve.wait_ge(also_done, 1)
                nc.vector.tensor_tensor(lo[:, n:n_all, :], also[:, :, :], hi[:, n:n_all, :].bitcast(F32),
                                        ALU.subtract)
            dve.wait_ge(hi_done, 1)
            nc.vector.tensor_tensor(lo[:, 0:n, :], o[:, :, :],
                                    hi[:, 0:n, :].bitcast(F32), ALU.subtract)

        @block.scalar
        def _(act):
            if also is not None:
                nc.scalar.activation(hi[:, n:n_all, :], also[:, :, :], ACT.Copy).then_inc(also_done, 1)
            act.wait_ge(gated, 1)
            nc.scalar.activation(hi[:, 0:n, :], o[:, :, :], ACT.Copy).then_inc(hi_done, 1)


class Columns:

    def __init__(self, widths):
        self.at, self.width = {}, 0
        for name, width in widths:
            self.at[name] = (self.width, width)
            self.width += width

    def of(self, tile, name):
        a, n = self.at[name]
        return tile[:, a:a + n]


COLUMNS = Columns([
    ("c", 2 * DT), ("c_2", DT), ("ada_b0", 48), ("ada_b1", 48), ("ada_b_2", 24),
    ("norm_mix0", DT), ("norm_mix1", DT), ("norm_ffn0", DT), ("norm_ffn1", DT), ("norm_2", DT), ("final", DT),
    ("lb", 8), ("onorm", 4), ("vnorm", 4), ("conv_w0", 3 * FT), ("conv_w1", 3 * FT), ("conv_b0", FT),
    ("conv_b1", FT), ("qa_norm", 3), ("kva_norm", 2), ("q_nope", 6), ("k_nope", 6), ("q_pe", 3), ("k_pe", 1),
    ("conv_2", 4 * 24), ("dn_norm", 8), ("a_log", 1), ("dt_bias", 1),
])


MOD0_FIRST = 20


def load_sbuf(K, name, pairs):
    arrived, = K.signals(name, "arrived")
    with K.nc.Block() as block:
        @block.sync
        def _(sp):
            for dst, src in pairs:
                sp.dma_start(dst, src).then_inc(arrived, 16)
            sp.wait_ge(arrived, 16 * len(pairs))


def program(nc, A, out, taps):
    with ExitStack() as ctx:
        K = Core(nc, ctx)
        K.ident = K.keep("ident", [P, P])
        K.ones = K.keep("ones", [P, P])
        K.ones64 = K.keep("ones64", [P, P])
        K.eps = K.keep("eps", [P, 1])
        cols = K.keep("cols", [P, COLUMNS.width])
        mod0, mod1 = (K.keep(f"mod{l}", [P, 48, 2]) for l in range(2))
        mod2 = K.keep("mod2", [P, 24, 1])
        scale1 = K.keep("scale1", [P, 2, DT])
        scale2 = K.keep("scale2", [P, 2, DT])

        def col(name):
            return COLUMNS.of(cols, name)

        def tap(name, ap):
            if taps is not None and name in taps:
                load_sbuf(K, "tap_" + name, [(taps[name], ap)])

        def mods_of(mod):
            return lambda group, vec: mod[:, group * DT:(group + 1) * DT, vec]
        mods = mods_of(mod0)

        x = K.keep("x", [P, DT, TOK])
        x_back = ctx.enter_context(nc.semaphore("x_back"))
        load_sbuf(K, "start", [(cols[:, :], A["cols"]), (K.ident[:, :], A["ident"]), (K.ones64[:, :], A["ones64"])])
        (ones_set,) = K.signals("init", "ones_set")
        with nc.Block() as block:
            @block.vector
            def _(dve):
                nc.vector.memset(K.ones[:, :], 1.0)
                nc.vector.memset(K.eps[:, :], EPS)

            @block.scalar
            def _(act):
                nc.scalar.activation(col("c"), col("c"), ACT.Silu)
                nc.scalar.activation(col("c_2"), col("c_2"), ACT.Silu)
        c_cols = col("c").rearrange("p (k v) -> p k v", v=2)

        with ExitStack() as late:
            modulation(K, "mod0", A["ada0"], MOD0_FIRST, c_cols, 2, col("ada_b0"), mod0, (A["ev_uv"], DT),
                       (x[:, :, :], A["x"]))
            norm_scales(K, "sc0", [(scale1[:, v, :], col("norm_mix0"), mods(1, v)) for v in range(2)])

            with ExitStack() as even:
                def ev(n, shape, dt=F32, where=even):
                    return where.enter_context(nc.sbuf_tensor(n, shape, dt))
                def side0(first, n):
                    return Side(A["ada0_t"], MOD0_FIRST, first, n, o_rows[:, 0:2, :], o_rows[:, 2, :],
                                col("ada_b0"), mod0)
                y_mlp = ev("y_mlp", [P, B_GROUPS, TOK])
                o = ev("ev_o", [P, A_HEADS, TOK])
                o_rows = o[:, :, :].rearrange("p a t -> p (a t)").rearrange("p (v d) -> p v d", d=D)
                area = ev("ev_area", [P, 5 * A_HEADS, TOK])
                uv, qg, vz = area[:, 0:2 * B_GROUPS, :], area[:, 0:2 * A_HEADS, :], area[:, 2 * A_HEADS:, :]
                with ExitStack() as hctx:
                    h_hi = ev("h0_hi", [P, DT, TOK], F32R, hctx)
                    h_lo = ev("h0_lo", [P, DT, TOK], F32R, hctx)
                    model_norm(K, "n0", x, 0, TOK,
                               [(0, CTX, scale1[:, 1, :], mods(0, 1)), (CTX, TOK, scale1[:, 0, :], mods(0, 0))],
                               h_hi, h_lo, work=uv, rows=(o_rows[:, 0:2, :], A["c_rows"]),
                               given=False)
                    product(K, "uv", A["ev_uv"], 2 * B_GROUPS, DT, h_hi, h_lo, 0, TOK,
                            copy_out(K, uv, ACT.Gelu_apprx_tanh), no_evac, (A["ev_qg"], DT),
                            side=side0(20, 8))
                    vs = uv[:, B_GROUPS:2 * B_GROUPS, :]
                    group_norm(K, "vn", vs, vs, B_GROUPS, 1, TOK, col("vnorm"), K.ones, 1.0 / P,
                               roots=area[:, 8:12, :])
                    chunk_mlp(K, uv, A["ws_t"], A["bs"], y_mlp)
                    product(K, "qg", A["ev_qg"], 2 * A_HEADS, DT, h_hi, h_lo, 0, TOK,
                            copy_out(K, qg, ACT.Silu), no_evac, (A["ev_vz"], DT),
                            side=side0(28, 8))
                    product(K, "vz", A["ev_vz"], 3 * A_HEADS, DT, h_hi, h_lo, 0, TOK,
                            copy_out(K, vz, ACT.Copy), no_evac, (A["ev_out"], DT),
                            side=side0(36, 12))
                with ExitStack() as kctx:
                    kf = ev("ev_k", [P, 2 * A_HEADS, TOK], F32, kctx)
                    gla_features(K, vz[:, A_HEADS:3 * A_HEADS, :], kf, col("lb"))
                    gla_both(K, qg[:, 0:A_HEADS, :], vz[:, 0:A_HEADS, :], kf, vz[:, A_HEADS:3 * A_HEADS, :],
                             A["gla_masks"], x, o)
                    add_directions(K, "ad", kf, o, x[:, :, :], A["x"], x_back)
                tap("o", o[:, :, :])
                tap("mlp", y_mlp[:, :, :])
                group_norm(K, "on", o, o, A_HEADS, 1, TOK, col("onorm"), K.ones, 1.0 / P)
                with ExitStack() as yctx:
                    y_hi = ev("y0_hi", [P, DT, TOK], F32R, yctx)
                    y_lo = ev("y0_lo", [P, DT, TOK], F32R, yctx)
                    gated_readout(K, "ro", o, qg[:, A_HEADS:2 * A_HEADS, :], y_hi, y_lo, y_mlp)
                    gates = [(0, CTX, mods(2, 1)), (CTX, TOK, mods(2, 0))]
                    with nc.Block() as block:
                        @block.sync
                        def _(sp):
                            sp.wait_ge(x_back, 16)
                    product(K, "eo", A["ev_out"], DT, DT, y_hi, y_lo, 0, TOK, no_evac, add_gated(K, x, gates, 0),
                            (A["up0"], DT), rms_of=x)
            tap("x_mix0", x[:, :, :])
            norm_scales(K, "sc0f", [(scale2[:, v, :], col("norm_ffn0"), mods(4, v)) for v in range(2)])
            ffn(K, nc, "f0", x, 0, TOK,
                [(0, CTX, scale2[:, 1, :], mods(3, 1)), (CTX, TOK, scale2[:, 0, :], mods(3, 0))],
                A["up0"], A["down0"], col("conv_w0"), col("conv_b0"),
                [(0, CTX, mods(5, 1)), (CTX, TOK, mods(5, 0))], (A["od_kv"], DT),
                A["c_rows"], A["ada1_t"], col("ada_b1"), mod1)
            tap("x0", x[:, :, :])
            rest(K, nc, A, out, x, col, mods_of(mod1), mod2, mods_of(mod2), scale1, scale2, tap)


def ffn(K, nc, name, x, t0, T, norms, w_up, w_down, conv_w, conv_b, gates, nxt, c_rows, ada_t,
        ada_b, mod):
    with ExitStack() as c:
        h_hi = c.enter_context(nc.sbuf_tensor(name + "_hhi", [P, DT, T], F32R))
        h_lo = c.enter_context(nc.sbuf_tensor(name + "_hlo", [P, DT, T], F32R))
        rows = c.enter_context(nc.sbuf_tensor(name + "_rows", list(c_rows.shape), F32))
        scratch = c.enter_context(nc.sbuf_tensor(name + "_scratch", [P, D], F32))
        model_norm(K, name + "_n", x, t0, T, norms, h_hi, h_lo, rows=(rows[:, :, :], c_rows))

        def side(first, n):
            return Side(ada_t, 0, first, n, rows[:, :, :], scratch[:, :], ada_b, mod)
        up = 2 * FH
        rest = mod.shape[1] - 2 * up
        sides = [side(0, up), side(up, rest), side(up + rest, up), None] if rest > 0 else [
            side(0, up), side(up, mod.shape[1] - up), None, None]
        feed_forward(K, name, x, t0, T, h_hi, h_lo, w_up, w_down, conv_w, conv_b, gates, nxt, sides)


MLA_HEADS = 6
MLA_SCALE = float(128 + 64) ** -0.5


def fourier(K, src, dft_c, dft_t, y):
    nc = K.nc
    NT = LAT // P
    with ExitStack() as c:
        fc = c.enter_context(nc.sbuf_tensor("ft_c", [P, 2 * P], F32))
        ft = c.enter_context(nc.sbuf_tensor("ft_t", [P, 2, NT, LAT], F32))
        chan = c.enter_context(nc.sbuf_tensor("ft_chan", [P, 2, NT, 2 * P], F32))
        ps_c = [c.enter_context(nc.psum_tensor(f"ft_psc{j}", [P, 512], F32)) for j in range(2)]
        ps_y = [c.enter_context(nc.psum_tensor(f"ft_psy{j}", [P, 512], F32)) for j in range(2)]
        loaded, by_channel, taken, done = K.signals("ft", "loaded by_channel taken done")
        with nc.Block() as block:
            @block.sync
            def _(sp):
                sp.dma_start(fc[:, :], dft_c).then_inc(loaded, 16)
                sp.dma_start(ft[:, :, :, :], dft_t).then_inc(loaded, 16)

            @block.tensor
            def _(pe):
                pe.wait_ge(loaded, 32)
                for f in range(2):
                    for n in range(NT):
                        m = f * NT + n
                        if m >= 2:
                            pe.wait_ge(taken, m - 1)
                        nc.tensor.matmul(ps_c[m % 2][:, 0:2 * P], src[:, f, n * P:(n + 1) * P], fc[:, :],
                                         start=True, stop=True).then_inc(by_channel, 1)
                for f in range(2):
                    pe.wait_ge(taken, (f + 1) * NT)
                    for n in range(NT):
                        for part in range(2):
                            last = nc.tensor.matmul(ps_y[f][:, :], chan[:, f, n, part * P:(part + 1) * P],
                                                    ft[:, part, n, :], start=(n + part == 0),
                                                    stop=(n == NT - 1 and part == 1))
                    last.then_inc(done, 1)

            @block.scalar
            def _(act):
                for m in range(2 * NT):
                    act.wait_ge(by_channel, m + 1)
                    nc.scalar.activation(chan[:, m // NT, m % NT, :], ps_c[m % 2][:, 0:2 * P],
                                         ACT.Copy).then_inc(taken, 1)
                for f in range(2):
                    act.wait_ge(done, f + 1)
                    nc.scalar.activation(y[:, f, :], ps_y[f][:, :], ACT.Copy)


def rotate(K, tiles, table, swap):
    nc = K.nc
    n = len(tiles)
    with ExitStack() as c:
        tab = c.enter_context(nc.sbuf_tensor("ro_tab", [P, 2, LAT], F32))
        sw = c.enter_context(nc.sbuf_tensor("ro_sw", [P, P], F32))
        other = c.enter_context(nc.sbuf_tensor("ro_other", [P, n, LAT], F32))
        ps = [c.enter_context(nc.psum_tensor(f"ro_ps{j}", [P, 512], F32)) for j in range(n)]
        loaded, swapped, by_sin, by_cos = K.signals("ro", "loaded swapped by_sin by_cos")
        with nc.Block() as block:
            @block.sync
            def _(sp):
                sp.dma_start(tab[:, :, :], table).then_inc(loaded, 16)
                sp.dma_start(sw[:, :], swap).then_inc(loaded, 16)

            @block.tensor
            def _(pe):
                pe.wait_ge(loaded, 32)
                for i, t in enumerate(tiles):
                    nc.tensor.matmul(ps[i][:, :], sw[:, :], t, start=True, stop=True).then_inc(swapped, 1)

            @block.vector
            def _(dve):
                dve.wait_ge(loaded, 32)
                for i, t in enumerate(tiles):
                    dve.wait_ge(swapped, i + 1)
                    nc.vector.tensor_tensor(other[:, i, :], ps[i][:, :], tab[:, 1, :], ALU.mult).then_inc(by_sin, 1)
                    nc.vector.tensor_tensor(t, t, tab[:, 0, :], ALU.mult).then_inc(by_cos, 1)
                for i, t in enumerate(tiles):
                    dve.wait_ge(by_sin, i + 1)
                    dve.wait_ge(by_cos, i + 1)
                    nc.vector.tensor_tensor(t, t, other[:, i, :], ALU.add)


def latent_attention(K, q, kn, kp, v, y):
    nc = K.nc
    NQ, NK = LAT // P, TOK // P
    with ExitStack() as c:
        def sb(n, shape):
            return c.enter_context(nc.sbuf_tensor("la_" + n, shape, F32))
        qn, qp, vs = sb("qn", [P, LAT]), sb("qp", [P, LAT]), sb("vs", [P, TOK])
        vt = sb("vt", [P, NK * P])
        probs = sb("probs", [P, 2, TOK])
        pt = sb("pt", [P, NK, LAT])
        nmax, bias, total, inv = (sb(n, [P, 2]) for n in ("nmax", "bias", "total", "inv"))
        ps_s = [c.enter_context(nc.psum_tensor(f"la_ps_s{j}", [P, 1024], F32)) for j in range(2)]
        ps_t = c.enter_context(nc.psum_tensor("la_ps_t", [P, 1024], F32))
        ps_v = c.enter_context(nc.psum_tensor("la_ps_v", [P, 512], F32))
        ps_o = c.enter_context(nc.psum_tensor("la_ps_o", [P, 512], F32))
        (q_in, qp_in, v_in, v_turned, vt_in, scored, max_done, bias_done, exp_done, inv_done, normed, p_turned,
         pt_in, o_done, o_out) = K.signals(
            "la", "q_in qp_in v_in v_turned vt_in scored max_done bias_done exp_done inv_done normed p_turned "
            "pt_in o_done o_out")

        def turns(eng, body):
            for r in range(2):
                body(r, 0, r, r == 0)
            with eng.Fori(1, MLA_HEADS // 2) as ip:
                for r in range(2):
                    body(2 * ip + r, ip, r, False)

        def tile(t, i):
            return t[:, bass.ds(i, 1), :].rearrange("p a t -> p (a t)")

        with nc.Block() as block:
            @block.scalar
            def _(act):
                def body(h, ip, r, first):
                    if not first:
                        act.wait_ge(scored, NQ * h)
                    nc.scalar.activation(qn[:, :], tile(q, h), ACT.Copy).then_inc(q_in, 1)
                    if r == 0:
                        nc.scalar.activation(qp[:, :], tile(q, MLA_HEADS + ip), ACT.Copy).then_inc(qp_in, 1)
                    if not first:
                        act.wait_ge(v_turned, 2 * h)
                    nc.scalar.activation(vs[:, :], tile(v, h), ACT.Copy).then_inc(v_in, 1)
                    if not first:
                        act.wait_ge(o_done, h)
                    for m, (a, b) in enumerate([(0, 4), (4, NK)]):
                        act.wait_ge(v_turned, 2 * h + m + 1)
                        nc.scalar.activation(vt[:, a * P:b * P], ps_v[:, 0:(b - a) * P], ACT.Copy).then_inc(vt_in, 1)
                    for n in range(NQ):
                        if not (first and n < 2):
                            act.wait_ge(p_turned, NQ * h + n - 1)
                        act.wait_ge(bias_done, NQ * h + n + 1)
                        nc.scalar.activation(probs[:, n % 2, :], ps_s[n % 2][:, 256:1024], ACT.Exp,
                                             bias=bias[:, n % 2:n % 2 + 1], scale=MLA_SCALE,
                                             accum_out=total[:, n % 2:n % 2 + 1]).then_inc(exp_done, 1)
                        act.wait_ge(p_turned, NQ * h + n + 1)
                        nc.scalar.activation(pt[:, :, n * P:(n + 1) * P],
                                             ps_t[:, 0:NK * P].rearrange("p (k t) -> p k t", k=NK),
                                             ACT.Copy).then_inc(pt_in, 1)
                turns(act, body)

            @block.vector
            def _(dve):
                def body(h, ip, r, first):
                    for n in range(NQ):
                        j = n % 2
                        dve.wait_ge(scored, NQ * h + n + 1)
                        if not (first and n < 2):
                            dve.wait_ge(exp_done, NQ * h + n - 1)
                        nc.vector.tensor_reduce(nmax[:, j:j + 1], ps_s[j][:, 256:1024], AX.X,
                                                ALU.max).then_inc(max_done, 1)
                        dve.wait_ge(max_done, NQ * h + n + 1)
                        nc.vector.tensor_scalar(bias[:, j:j + 1], nmax[:, j:j + 1], -MLA_SCALE, None,
                                                ALU.mult).then_inc(bias_done, 1)
                        dve.wait_ge(exp_done, NQ * h + n + 1)
                        nc.vector.reciprocal(inv[:, j:j + 1], total[:, j:j + 1]).then_inc(inv_done, 1)
                        dve.wait_ge(inv_done, NQ * h + n + 1)
                        nc.vector.tensor_scalar(probs[:, j, :], probs[:, j, :], inv[:, j:j + 1], None,
                                                ALU.mult).then_inc(normed, 1)
                    dve.wait_ge(o_done, h + 1)
                    nc.vector.tensor_copy(tile(y, h), ps_o[:, :]).then_inc(o_out, 1)
                turns(dve, body)

            @block.tensor
            def _(pe):
                def body(h, ip, r, first):
                    half = slice(64 * r, 64 * r + 64)

                    def score(n):
                        if not (first and n < 2):
                            pe.wait_ge(exp_done, NQ * h + n - 1)
                        for a, b, col in ((0, CTX, 256), (CTX, TOK, 512)):
                            nc.tensor.matmul(ps_s[n % 2][:, col:col + b - a], qn[:, n * P:(n + 1) * P],
                                             tile(kn, h)[:, a:b], start=True, stop=False)
                            last = nc.tensor.matmul(ps_s[n % 2][:, col:col + b - a], qp[half, n * P:(n + 1) * P],
                                                    kp[half, a:b], start=False, stop=True)
                        last.then_inc(scored, 1)

                    def turn(n):
                        pe.wait_ge(normed, NQ * h + n + 1)
                        if not (first and n == 0):
                            pe.wait_ge(pt_in, NQ * h + n)
                        for k in range(NK):
                            last = nc.tensor.transpose(ps_t[:, k * P:(k + 1) * P],
                                                       probs[:, n % 2, k * P:(k + 1) * P], K.ident[:, :])
                        last.then_inc(p_turned, 1)
                    pe.wait_ge(v_in, h + 1)
                    for m, (a, b) in enumerate([(0, 4), (4, NK)]):
                        if not (first and m == 0):
                            pe.wait_ge(vt_in, 2 * h + m)
                        for k in range(a, b):
                            last = nc.tensor.transpose(ps_v[:, (k - a) * P:(k - a + 1) * P],
                                                       vs[:, k * P:(k + 1) * P], K.ident[:, :])
                        last.then_inc(v_turned, 1)
                    pe.wait_ge(q_in, h + 1)
                    pe.wait_ge(qp_in, ip + 1)
                    score(0)
                    for n in range(NQ):
                        if n + 1 < NQ:
                            score(n + 1)
                        turn(n)
                    pe.wait_ge(vt_in, 2 * h + 2)
                    pe.wait_ge(pt_in, NQ * (h + 1))
                    if not first:
                        pe.wait_ge(o_out, h)
                    for k in range(NK):
                        last = nc.tensor.matmul(ps_o[:, :], vt[:, k * P:(k + 1) * P], pt[:, k, :],
                                                start=(k == 0), stop=(k == NK - 1))
                    last.then_inc(o_done, 1)
                turns(pe, body)


def layer1(K, nc, A, x, col, mods, scale1, scale2, tap, nxt, next_mod):
    norm_scales(K, "sc1", [(scale1[:, v, :], col("norm_mix1"), mods(1, v)) for v in range(2)]
                + [(scale2[:, 0, :], col("norm_ffn1"), mods(4, 0))])
    with ExitStack() as odd:
        def sb(n, shape, dt=F32, where=odd):
            return where.enter_context(nc.sbuf_tensor("od_s_" + n, shape, dt))
        y = sb("y", [P, DT, LAT])
        with ExitStack() as att:
            kv = sb("kv", [P, 3, TOK], F32, att)
            fq = sb("fq", [P, 5, LAT], F32, att)
            with ExitStack() as hctx:
                h_hi = sb("h_hi", [P, DT, TOK], F32R, hctx)
                h_lo = sb("h_lo", [P, DT, TOK], F32R, hctx)
                model_norm(K, "n1", x, 0, TOK,
                           [(0, CTX, scale1[:, 1, :], mods(0, 1)), (CTX, TOK, scale1[:, 0, :], mods(0, 0))],
                           h_hi, h_lo)
                product(K, "okv", A["od_kv"], 3, DT, h_hi, h_lo, 0, TOK, copy_out(K, kv, ACT.Copy), no_evac,
                        (A["od_fq"], DT))
                product(K, "ofq", A["od_fq"], 5, DT, h_hi, h_lo, CTX, LAT, copy_out(K, fq, ACT.Copy), no_evac,
                        (A["od_qb"], 3))
            fourier(K, fq, A["dft_c"], A["dft_t"], y)
            group_norm(K, "qan", fq[:, 2:5, :], fq[:, 2:5, :], 1, 3, LAT, col("qa_norm"), K.ones, 1.0 / 384)
            group_norm(K, "kvan", kv[:, 0:2, :], kv[:, 0:2, :], 1, 2, TOK, col("kva_norm"), K.ones, 1.0 / 256)
            group_norm(K, "kpn", kv[:, 2:3, :], kv[:, 2:3, :], 1, 1, TOK, col("k_pe"), K.ones64, 1.0 / 64)
            q = sb("q", [P, 9, LAT], F32, att)
            kn = sb("kn", [P, MLA_HEADS, TOK], F32, att)
            v = sb("v", [P, MLA_HEADS, TOK], F32, att)
            with ExitStack() as lctx:
                q_hi, q_lo = (sb(n, [P, 3, LAT], F32R, lctx) for n in ("q_hi", "q_lo"))
                kv_hi, kv_lo = (sb(n, [P, 2, TOK], F32R, lctx) for n in ("kv_hi", "kv_lo"))
                split_parts(K, "qs", fq[:, 2:5, :], q_hi, q_lo)
                split_parts(K, "kvs", kv[:, 0:2, :], kv_hi, kv_lo)
                product(K, "oqb", A["od_qb"], 9, 3, q_hi, q_lo, 0, LAT, copy_out(K, q, ACT.Copy), no_evac,
                        (A["od_kb"], 2))
                product(K, "okb", A["od_kb"], 6, 2, kv_hi, kv_lo, 0, TOK, copy_out(K, kn, ACT.Copy), no_evac,
                        (A["od_vb"], 2))
                product(K, "ovb", A["od_vb"], 6, 2, kv_hi, kv_lo, 0, TOK, copy_out(K, v, ACT.Copy), no_evac,
                        (A["od_out"], DT))
            group_norm(K, "qnn", q[:, 0:6, :], q[:, 0:6, :], 6, 1, LAT, col("q_nope"), K.ones, 1.0 / P)
            group_norm(K, "qpn", q[:, 6:9, :], q[:, 6:9, :], 3, 1, LAT, col("q_pe"), K.ones64, 1.0 / 64)
            group_norm(K, "knn", kn, kn, 6, 1, TOK, col("k_nope"), K.ones, 1.0 / P)
            rotate(K, [q[:, 6 + m, :] for m in range(3)] + [kv[:, 2, CTX:TOK]], A["rope"], A["rope_swap"])
            latent_attention(K, q, kn, kv[:, 2, :], v, y[:, 2:DT, :])
        tap("four", y[:, 0:2, :])
        tap("att", y[:, 2:8, :])
        y_hi, y_lo = sb("y_hi", [P, DT, LAT], F32R), sb("y_lo", [P, DT, LAT], F32R)
        split_parts(K, "ys1", y, y_hi, y_lo)
        product(K, "oo", A["od_out"], DT, DT, y_hi, y_lo, 0, LAT, no_evac,
                add_gated(K, x, [(CTX, TOK, mods(2, 0))], CTX), (A["up1"], DT), rms_of=x)
    tap("x_mix1", x[:, :, CTX:TOK])
    ffn(K, nc, "f1", x, CTX, LAT, [(0, LAT, scale2[:, 0, :], mods(3, 0))], A["up1"], A["down1"],
        col("conv_w1"), col("conv_b1"), [(CTX, TOK, mods(5, 0))], nxt, *next_mod)
    tap("x1", x[:, :, CTX:TOK])


def layout1(np, I, A, blocks):
    w = I["od_w_in"][0]
    k_pe = w[:, 896:960]
    A["od_kv"] = blocks(np.concatenate([w[:, 640:896], k_pe, k_pe], axis=1))
    A["od_fq"] = blocks(w[:, 0:640])
    qb = I["od_w_qb"][0].reshape(384, MLA_HEADS, 192)
    A["od_qb"] = blocks(np.concatenate([qb[:, :, :P].reshape(384, -1), qb[:, :, P:].reshape(384, -1)], axis=1))
    kvb = I["od_w_kvb"][0].reshape(256, MLA_HEADS, 2, P)
    A["od_kb"] = blocks(kvb[:, :, 0].reshape(256, -1))
    A["od_vb"] = blocks(kvb[:, :, 1].reshape(256, -1))
    A["od_out"] = blocks(I["od_w_out"][0])
    two = np.kron(np.eye(2), np.ones((64, 64)))
    A["ones64"] = two.astype(np.float32)
    a = 2 * np.pi * np.outer(np.arange(64), np.arange(64)) / 64
    A["dft_c"] = np.concatenate([np.kron(np.eye(2), np.cos(a)), np.kron(np.eye(2), np.sin(a))],
                                axis=1).astype(np.float32)
    a = 2 * np.pi * (np.outer(np.arange(LAT), np.arange(LAT)) % LAT) / LAT
    norm = 1 / np.sqrt(64.0 * LAT)
    A["dft_t"] = (np.stack([np.cos(a), -np.sin(a)]) * norm).reshape(2, LAT // P, P, LAT).transpose(
        2, 0, 1, 3).astype(np.float32)
    t = np.arange(LAT)
    inv_freq = np.float32(10000.0) ** (-np.arange(0, 32, 2, dtype=np.float32) / np.float32(32))
    ang = np.stack([t // 64, t % 64]).astype(np.float32)[:, None, :] * inv_freq[None, :, None]
    rope = np.stack([np.cos(ang), np.sin(ang)])
    rope = np.repeat(rope[:, :, None], 2, axis=2).reshape(2, 64, LAT)
    A["rope"] = np.concatenate([rope, rope], axis=1).transpose(1, 0, 2).astype(np.float32)
    swap = np.zeros((P, P), np.float32)
    for m in range(P):
        swap[m ^ 16, m] = 1.0 if m & 16 else -1.0
    A["rope_swap"] = swap


DN_HEADS = 8
NG = 2
GH = DN_HEADS // NG
DN_SCALE = float(P) ** -0.5


def delta_projections(K, name, w, h_hi, h_lo, dst, taps_w, nxt):
    nc = K.nc
    with ExitStack() as c:
        src = c.enter_context(nc.sbuf_tensor(name + "_src", [P, 2, 3 + LAT], F32))
        conv = c.enter_context(nc.sbuf_tensor(name + "_conv", [P, 2, LAT], F32))
        (padded,) = K.signals(name + "_pad", "padded")
        with nc.Block() as block:
            @block.vector
            def _(dve):
                nc.vector.memset(src[:, :, 0:3], 0.0).then_inc(padded, 1)

        def act_part(act, g, ip, j, i, first):
            conv0, conv1, conv2, conv3, silu_done = g.more
            act.wait_ge(g.mm_done, i + 1)
            if not first:
                act.wait_ge(conv3, i - 1)
            nc.scalar.activation(src[:, j, 3:3 + LAT], g.out[j], ACT.Copy).then_inc(g.free[j], 1)
            act.wait_ge(conv3, i + 1)
            nc.scalar.activation(dst[:, bass.ds(i, 1), :].rearrange("p a t -> p (a t)"), conv[:, j, :],
                                 ACT.Silu).then_inc(silu_done, 1)

        def dve_part(dve, g, ip, j, i, first):
            steps = g.more[0:4]
            silu_done = g.more[4]
            dve.wait_ge(g.free[j], ip + 1)
            if not first:
                dve.wait_ge(silu_done, i - 1)
            nc.vector.tensor_scalar(conv[:, j, :], src[:, j, 0:LAT], taps_w[:, bass.ds(i * 4, 1)], None,
                                    ALU.mult).then_inc(steps[0], 1)
            for m in range(1, 4):
                dve.wait_ge(steps[m - 1], i + 1)
                nc.vector.scalar_tensor_tensor(out=conv[:, j, :], in0=src[:, j, m:m + LAT],
                                               scalar=taps_w[:, bass.ds(i * 4 + m, 1)], in1=conv[:, j, :],
                                               op0=ALU.mult, op1=ALU.add).then_inc(steps[m], 1)

        product(K, name, w, dst.shape[1], DT, h_hi, h_lo, 0, LAT, act_part, dve_part, nxt,
                "conv0 conv1 conv2 conv3 silu_done")


def delta_gates(K, ab, a_log, dt_bias, by_token):
    nc = K.nc
    H = DN_HEADS
    NC = LAT // CHUNK
    with ExitStack() as c:
        z = c.enter_context(nc.sbuf_tensor("dg_z", [H, 8, LAT], F32))
        e_log = c.enter_context(nc.sbuf_tensor("dg_elog", [H, 2], F32))
        ps = c.enter_context(nc.psum_tensor("dg_ps", [P, NC * P], F32))
        (shifted, folded, tail, up, back, lost, inv, kept, logged, soft, rate, neg_rate, pos, summed, g_done, b_done,
         turned) = K.signals(
            "dg", "shifted folded tail up back lost inv kept logged soft rate neg_rate pos summed g_done b_done turned")
        with nc.Block() as block:
            @block.vector
            def _(dve):
                nc.vector.tensor_scalar(z[:, 0, :], ab[0:H, :], dt_bias[0:H, :], None, ALU.add).then_inc(shifted, 1)
                dve.wait_ge(shifted, 1)
                nc.vector.scalar_tensor_tensor(out=z[:, 1, :], in0=z[:, 0, :], scalar=-1.0, in1=z[:, 0, :],
                                               op0=ALU.mult, op1=ALU.min).then_inc(folded, 1)
                nc.vector.tensor_scalar(z[:, 6, :], z[:, 0, :], 0.0, None, ALU.max).then_inc(pos, 1)
                dve.wait_ge(tail, 1)
                nc.vector.tensor_scalar(z[:, 2, :], z[:, 1, :], 1.0, None, ALU.add).then_inc(up, 1)
                dve.wait_ge(up, 1)
                nc.vector.tensor_scalar(z[:, 3, :], z[:, 2, :], -1.0, None, ALU.add).then_inc(back, 1)
                nc.vector.reciprocal(z[:, 4, :], z[:, 2, :]).then_inc(inv, 1)
                dve.wait_ge(back, 1)
                nc.vector.tensor_tensor(z[:, 3, :], z[:, 1, :], z[:, 3, :], ALU.subtract).then_inc(lost, 1)
                dve.wait_ge(lost, 1)
                dve.wait_ge(inv, 1)
                nc.vector.tensor_tensor(z[:, 3, :], z[:, 3, :], z[:, 4, :], ALU.mult).then_inc(kept, 1)
                dve.wait_ge(kept, 1)
                dve.wait_ge(pos, 1)
                nc.vector.tensor_tensor(z[:, 6, :], z[:, 6, :], z[:, 3, :], ALU.add).then_inc(soft, 1)
                dve.wait_ge(soft, 1)
                dve.wait_ge(logged, 1)
                nc.vector.tensor_tensor(z[:, 6, :], z[:, 6, :], z[:, 5, :], ALU.add).then_inc(summed, 1)
                dve.wait_ge(rate, 1)
                nc.vector.tensor_scalar(e_log[:, 1:2], e_log[:, 0:1], -1.0, None, ALU.mult).then_inc(neg_rate, 1)
                dve.wait_ge(neg_rate, 1)
                dve.wait_ge(summed, 1)
                nc.vector.tensor_scalar(ab[0:H, :], z[:, 6, :], e_log[:, 1:2], None, ALU.mult).then_inc(g_done, 1)
                dve.wait_ge(turned, 1)
                pv = ps[:, :].rearrange("p (c f) -> p c f", c=NC)
                nc.vector.tensor_copy(by_token[:, :, 0:H], pv[:, :, 0:H])
                nc.vector.tensor_copy(by_token[:, :, H:2 * H], pv[:, :, 32:32 + H])

            @block.scalar
            def _(act):
                nc.scalar.activation(ab[32:32 + H, :], ab[32:32 + H, :], ACT.Sigmoid).then_inc(b_done, 1)
                nc.scalar.activation(e_log[:, 0:1], a_log[0:H, :], ACT.Exp).then_inc(rate, 1)
                act.wait_ge(folded, 1)
                nc.scalar.activation(z[:, 1, :], z[:, 1, :], ACT.Exp).then_inc(tail, 1)
                act.wait_ge(up, 1)
                nc.scalar.activation(z[:, 5, :], z[:, 2, :], ACT.Ln).then_inc(logged, 1)

            @block.tensor
            def _(pe):
                pe.wait_ge(g_done, 1)
                pe.wait_ge(b_done, 1)
                for n in range(NC):
                    last = nc.tensor.transpose(ps[:, n * P:(n + 1) * P], ab[:, n * CHUNK:(n + 1) * CHUNK],
                                               K.ident[:, :])
                last.then_inc(turned, 1)


class Fills:

    def __init__(self, full, empty, per_turn, emptied_per_turn=None):
        self.full, self.empty = full, empty
        self.per_turn, self.emptied = per_turn, emptied_per_turn or per_turn

    def wait_full(self, eng, turn, k):
        eng.wait_ge(self.full, turn * self.per_turn + k)

    def wait_empty(self, eng, turn, k):
        eng.wait_ge(self.empty, turn * self.emptied + k)


JOINS = (2, 4, 8, 16, 32, 64, 128)


def delta_rule(K, qkv, by_token, consts, join_masks):
    nc = K.nc
    H, W, NL = DN_HEADS, GH * P, len(JOINS)
    TURNS = LAT // CHUNK
    with ExitStack() as c:
        def sb(n, shape):
            return c.enter_context(nc.sbuf_tensor("dr_" + n, shape, F32))
        cst = sb("cst", [P, 3, P])
        joins = sb("joins", [P, NL + 1, P])
        upto, after, upto_scaled = cst[:, 0, :], cst[:, 1, :], cst[:, 2, :]
        S = [[sb(f"{n}{G}", [P, W]) for G in range(NG)] for n in
             ("kc", "qc", "vc", "low", "attn", "grow", "lowt", "part", "x", "xt", "xl", "kb", "kend", "vb", "state")]
        kc, qc, vc, low, attn, grow, lowt, part, X, XT, XL, kb, kend, vb, state = S
        gb = [sb(f"gb{G}", [P, 2, GH]) for G in range(NG)]
        g_rows, g_after = ([sb(f"{n}{G}", [P, GH, P]) for G in range(NG)] for n in ("g_rows", "g_after"))
        ecol = [sb(f"ecol{G}", [P, 3, GH]) for G in range(NG)]
        bcol = [sb(f"bcol{G}", [P, GH]) for G in range(NG)]
        bank = [[c.enter_context(nc.psum_tensor(f"dr_bank{n}{G}", [P, 512], F32)) for n in range(4)] for G in range(NG)]
        each = ("turn_done gb_in rows_in after_in bcol_done k_in q_in v_in low1 low2 low3 xt1 x_first xt_first "
                "part_done mask_q kb_done qd_done fullA emptyA fullB emptyB fullC emptyC fullD emptyD").split()
        made = K.signals("dr", "loaded " + " ".join(f"{n}{G}" for G in range(NG) for n in each))
        loaded = made[0]
        sig = [made[1 + G * len(each):1 + (G + 1) * len(each)] for G in range(NG)]
        (turn_done, gb_in, rows_in, after_in, bcol_done, k_in, q_in, v_in, low1, low2, low3, xt1, x_first,
         xt_first, part_done, mask_q, kb_done, qd_done) = [[sig[G][m] for G in range(NG)] for m in range(18)]
        A = [Fills(sig[G][18], sig[G][19], NL + 2) for G in range(NG)]
        B = [Fills(sig[G][20], sig[G][21], NL) for G in range(NG)]
        C = [Fills(sig[G][22], sig[G][23], NL + 2) for G in range(NG)]
        Dk = [Fills(sig[G][24], sig[G][25], 5, 4) for G in range(NG)]

        def v3(t):
            return t.rearrange("p (h t) -> p h t", h=GH)

        def per_head(colv):
            return colv.unsqueeze(2).to_broadcast([P, GH, P])

        def over_heads(m):
            return m.unsqueeze(1).to_broadcast([P, GH, P])

        def src(part_, G, s):
            return qkv[:, part_ * H + G * GH:part_ * H + (G + 1) * GH, bass.ds(s * CHUNK, CHUNK)]

        def hc(h):
            return slice(h * P, (h + 1) * P)

        def in_order(eng, begin, product_in, change, finish):
            def half(G, s, between):
                for n in range(1, NL):
                    product_in(G, s, n)
                    for piece, o, so in between[2 * n - 2:2 * n - 1]:
                        piece(o, so)
                    change(G, s, n)
                    for piece, o, so in between[2 * n - 1:2 * n]:
                        piece(o, so)

            def ended(G, s):
                return [(piece, G, s) for piece in finish]

            def begun(G, s):
                return [(piece, G, s) for piece in begin]

            def turn(s, first, last):
                half(0, s, ([] if first else ended(1, s - 1)) + begun(1, s))
                half(1, s, ended(0, s) + ([] if last else begun(0, s + 1)))
            for piece in begin:
                piece(0, 0)
            turn(0, True, False)
            with eng.Fori(1, TURNS - 1) as s:
                turn(s, False, False)
            turn(TURNS - 1, False, True)
            for piece in finish:
                piece(1, TURNS - 1)

        def nothing(G, s):
            pass

        with nc.Block() as block:
            @block.sync
            def _(sp):
                sp.dma_start(cst[:, :, :], consts).then_inc(loaded, 16)
                sp.dma_start(joins[:, :, :], join_masks).then_inc(loaded, 16)

            @block.scalar
            def _(act):
                act.wait_ge(loaded, 32)

                def copies(G, s):
                    act.wait_ge(turn_done[G], s + 1)
                    for m in range(2):
                        last = nc.scalar.activation(
                            gb[G][:, m, :], by_token[:, bass.ds(s, 1), m * H + G * GH:m * H + (G + 1) * GH].rearrange(
                                "p a b -> p (a b)"), ACT.Copy)
                    last.then_inc(gb_in[G], 1)
                    nc.scalar.activation(v3(kc[G][:, :]), src(1, G, s), ACT.Copy).then_inc(k_in[G], 1)
                    act.wait_ge(gb_in[G], s + 1)
                    nc.scalar.activation(g_rows[G][:, :, :], per_head(gb[G][:, 0, :]), ACT.Copy).then_inc(rows_in[G], 1)

                def more_copies(G, s):
                    A[G].wait_full(act, s, 1)
                    nc.scalar.activation(ecol[G][:, :, :], bank[G][0][:, 0:3 * GH].rearrange("p (a h) -> p a h", a=3),
                                         ACT.Exp).then_inc(A[G].empty, 1)
                    nc.scalar.activation(v3(qc[G][:, :]), src(0, G, s), ACT.Copy).then_inc(q_in[G], 1)
                    nc.scalar.activation(v3(vc[G][:, :]), src(2, G, s), ACT.Copy).then_inc(v_in[G], 1)

                def decays_low(G, s):
                    A[G].wait_full(act, s, 2)
                    nc.scalar.activation(low[G][:, :], bank[G][0][:, :], ACT.Exp).then_inc(A[G].empty, 1)

                def decays(G, s):
                    B[G].wait_full(act, s, 1)
                    nc.scalar.activation(attn[G][:, :], bank[G][1][:, :], ACT.Exp).then_inc(B[G].empty, 1)
                    Dk[G].wait_full(act, s, 1)
                    nc.scalar.activation(grow[G][:, :], bank[G][3][:, :], ACT.Exp).then_inc(Dk[G].empty, 1)

                def lower(G, s):
                    C[G].wait_full(act, s, 2)
                    nc.scalar.activation(lowt[G][:, :], bank[G][2][:, :], ACT.Copy).then_inc(C[G].empty, 1)

                def product_in(G, s, n):
                    A[G].wait_full(act, s, 2 + n)
                    nc.scalar.activation(XL[G][:, :], bank[G][0][:, :], ACT.Copy).then_inc(A[G].empty, 1)

                def w_out(G, s):
                    A[G].wait_full(act, s, NL + 2)
                    nc.scalar.activation(kc[G][:, :], bank[G][0][:, :], ACT.Copy, scale=-1.0).then_inc(A[G].empty, 1)

                def values_out(G, s):
                    B[G].wait_full(act, s, NL)
                    nc.scalar.activation(vc[G][:, :], bank[G][1][:, :], ACT.Copy).then_inc(B[G].empty, 1)
                in_order(act, [copies, more_copies, decays, decays_low, lower, nothing, nothing, nothing], product_in, lambda G, s, n: None,
                         [w_out, values_out, nothing])

            @block.vector
            def _(dve):
                for G in range(NG):
                    nc.vector.memset(state[G][:, :], 0.0).then_inc(turn_done[G], 1)
                dve.wait_ge(loaded, 32)

                def columns(G, s):
                    dve.wait_ge(turn_done[G], s + 1)
                    dve.wait_ge(gb_in[G], s + 1)
                    nc.vector.tensor_tensor(g_after[G][:, :, :], over_heads(after), per_head(gb[G][:, 0, :]),
                                            ALU.mult).then_inc(after_in[G], 1)

                def beta_decayed(G, s):
                    A[G].wait_empty(dve, s, 1)
                    nc.vector.tensor_tensor(bcol[G][:, :], gb[G][:, 1, :], ecol[G][:, 0, :],
                                            ALU.mult).then_inc(bcol_done[G], 1)

                def mask_attn(G, s):
                    B[G].wait_empty(dve, s, 1)
                    nc.vector.tensor_tensor(v3(attn[G][:, :]), v3(attn[G][:, :]), over_heads(upto_scaled),
                                            ALU.mult).then_inc(mask_q[G], 1)

                def mask_low(G, s):
                    A[G].wait_empty(dve, s, 2)
                    nc.vector.tensor_tensor(v3(low[G][:, :]), v3(low[G][:, :]), over_heads(after),
                                            ALU.mult).then_inc(low1[G], 1)
                    dve.wait_ge(low1[G], s + 1)
                    C[G].wait_full(dve, s, 1)
                    nc.vector.tensor_tensor(low[G][:, :], low[G][:, :], bank[G][2][:, :],
                                            ALU.mult).then_inc(C[G].empty, 1)
                    C[G].wait_empty(dve, s, 1)
                    nc.vector.tensor_tensor(v3(low[G][:, :]), v3(low[G][:, :]), per_head(gb[G][:, 1, :]),
                                            ALU.mult).then_inc(low2[G], 1)

                def queries(G, s):
                    Dk[G].wait_empty(dve, s, 1)
                    dve.wait_ge(q_in[G], s + 1)
                    nc.vector.scalar_tensor_tensor(out=grow[G][:, :], in0=qc[G][:, :], scalar=DN_SCALE,
                                                   in1=grow[G][:, :], op0=ALU.mult, op1=ALU.mult).then_inc(qd_done[G], 1)
                    dve.wait_ge(mask_q[G], s + 1)
                    Dk[G].wait_full(dve, s, 2)
                    nc.vector.tensor_tensor(attn[G][:, :], attn[G][:, :], bank[G][3][:, :],
                                            ALU.mult).then_inc(Dk[G].empty, 1)

                def keys(G, s):
                    dve.wait_ge(bcol_done[G], s + 1)
                    Dk[G].wait_full(dve, s, 3)
                    nc.vector.tensor_tensor(v3(kb[G][:, :]), v3(bank[G][3][:, :]), per_head(bcol[G][:, :]),
                                            ALU.mult).then_inc(kb_done[G], 1)
                    nc.vector.tensor_tensor(v3(kend[G][:, :]), v3(bank[G][3][:, :]), per_head(ecol[G][:, 1, :]),
                                            ALU.mult).then_inc(Dk[G].empty, 1)

                def values(G, s):
                    Dk[G].wait_full(dve, s, 4)
                    nc.vector.tensor_tensor(v3(vb[G][:, :]), v3(bank[G][3][:, :]), per_head(gb[G][:, 1, :]),
                                            ALU.mult).then_inc(Dk[G].empty, 1)

                def part_of(G, n):
                    nc.vector.tensor_tensor(v3(part[G][:, :]), v3(lowt[G][:, :]), over_heads(joins[:, n, :]),
                                            ALU.mult).then_inc(part_done[G], 1)

                def single_tokens(G, s):
                    dve.wait_ge(low2[G], s + 1)
                    nc.vector.tensor_tensor(v3(X[G][:, :]), v3(low[G][:, :]), over_heads(joins[:, NL, :]),
                                            ALU.mult).then_inc(low3[G], 1)
                    C[G].wait_empty(dve, s, 2)
                    nc.vector.tensor_tensor(v3(XT[G][:, :]), v3(lowt[G][:, :]), over_heads(joins[:, 0, :]),
                                            ALU.mult).then_inc(xt1[G], 1)
                    part_of(G, 1)
                    dve.wait_ge(low3[G], s + 1)
                    nc.vector.tensor_tensor(v3(X[G][:, :]), over_heads(K.ident[:, :]), v3(X[G][:, :]),
                                            ALU.subtract).then_inc(x_first[G], 1)
                    dve.wait_ge(xt1[G], s + 1)
                    nc.vector.tensor_tensor(v3(XT[G][:, :]), over_heads(K.ident[:, :]), v3(XT[G][:, :]),
                                            ALU.subtract).then_inc(xt_first[G], 1)

                def change(G, s, n):
                    if n < NL - 1:
                        A[G].wait_full(dve, s, 2 + n)
                        part_of(G, n + 1)
                        B[G].wait_full(dve, s, n + 1)
                        C[G].wait_full(dve, s, n + 2)
                        if n == 1:
                            dve.wait_ge(x_first[G], s + 1)
                        else:
                            B[G].wait_empty(dve, s, n)
                        nc.vector.tensor_tensor(X[G][:, :], X[G][:, :], bank[G][1][:, :],
                                                ALU.subtract).then_inc(B[G].empty, 1)
                    C[G].wait_full(dve, s, n + 2)
                    if n == 1:
                        dve.wait_ge(xt_first[G], s + 1)
                    else:
                        C[G].wait_empty(dve, s, n + 1)
                    nc.vector.tensor_tensor(XT[G][:, :], XT[G][:, :], bank[G][2][:, :],
                                            ALU.subtract).then_inc(C[G].empty, 1)

                def take(G, s):
                    C[G].wait_full(dve, s, NL + 2)
                    nc.vector.tensor_scalar(src(0, G, s), v3(bank[G][2][:, :]), 1.0, None,
                                            ALU.mult).then_inc(C[G].empty, 1)
                    Dk[G].wait_full(dve, s, 5)
                    for h in range(GH):
                        last = nc.vector.scalar_tensor_tensor(
                            out=state[G][:, hc(h)], in0=state[G][:, hc(h)], scalar=ecol[G][:, 2, h:h + 1],
                            in1=bank[G][3][:, hc(h)], op0=ALU.mult, op1=ALU.add)
                    last.then_inc(turn_done[G], 1)
                in_order(dve, [columns, beta_decayed, mask_attn, mask_low, queries, keys, values, single_tokens],
                         lambda G, s, n: None, change, [nothing, nothing, take])

            @block.tensor
            def _(pe):
                pe.wait_ge(loaded, 32)

                def each_head(out, lhsT, rhs, then):
                    for h in range(GH):
                        last = nc.tensor.matmul(out[:, hc(h)], lhsT(h), rhs(h), start=True, stop=True)
                    last.then_inc(then, 1)

                def turn_over(out, t, then):
                    for h in range(GH):
                        last = nc.tensor.transpose(out[:, hc(h)], t[:, hc(h)], K.ident[:, :])
                    last.then_inc(then, 1)

                def sums(G, s):
                    pe.wait_ge(turn_done[G], s + 1)
                    pe.wait_ge(gb_in[G], s + 1)
                    for m, left in enumerate((upto, after, K.ones[:, :])):
                        last = nc.tensor.matmul(bank[G][0][:, m * GH:(m + 1) * GH], left, gb[G][:, 0, :],
                                                start=True, stop=True)
                    last.then_inc(A[G].full, 1)
                    pe.wait_ge(k_in[G], s + 1)
                    each_head(bank[G][2], lambda h: kc[G][:, hc(h)], lambda h: kc[G][:, hc(h)], C[G].full)

                def decays(G, s):
                    pe.wait_ge(rows_in[G], s + 1)
                    pe.wait_ge(after_in[G], s + 1)
                    each_head(bank[G][1], lambda h: g_after[G][:, h, :], lambda h: upto, B[G].full)
                    each_head(bank[G][3], lambda h: g_rows[G][:, h, :], lambda h: upto, Dk[G].full)

                def decays_low(G, s):
                    A[G].wait_empty(pe, s, 1)
                    each_head(bank[G][0], lambda h: upto, lambda h: g_after[G][:, h, :], A[G].full)

                def queries(G, s):
                    Dk[G].wait_empty(pe, s, 1)
                    pe.wait_ge(q_in[G], s + 1)
                    each_head(bank[G][3], lambda h: kc[G][:, hc(h)], lambda h: qc[G][:, hc(h)], Dk[G].full)

                def lower(G, s):
                    pe.wait_ge(low2[G], s + 1)
                    C[G].wait_empty(pe, s, 1)
                    turn_over(bank[G][2], low[G], C[G].full)

                def keys(G, s):
                    Dk[G].wait_empty(pe, s, 2)
                    turn_over(bank[G][3], kc[G], Dk[G].full)

                def values(G, s):
                    pe.wait_ge(v_in[G], s + 1)
                    Dk[G].wait_empty(pe, s, 3)
                    turn_over(bank[G][3], vc[G], Dk[G].full)

                def product_in(G, s, n):
                    pe.wait_ge(part_done[G], (NL - 1) * s + n)
                    if n == 1:
                        pe.wait_ge(x_first[G], s + 1)
                        pe.wait_ge(xt_first[G], s + 1)
                    else:
                        B[G].wait_empty(pe, s, n)
                        C[G].wait_empty(pe, s, n + 1)
                    A[G].wait_empty(pe, s, n + 1)
                    each_head(bank[G][0], lambda h: part[G][:, hc(h)], lambda h: X[G][:, hc(h)], A[G].full)

                def change(G, s, n):
                    A[G].wait_empty(pe, s, n + 2)
                    if n == 1:
                        B[G].wait_empty(pe, s, 1)
                        C[G].wait_empty(pe, s, 2)
                    if n < NL - 1:
                        each_head(bank[G][1], lambda h: XT[G][:, hc(h)], lambda h: XL[G][:, hc(h)], B[G].full)
                    each_head(bank[G][2], lambda h: XL[G][:, hc(h)], lambda h: XT[G][:, hc(h)], C[G].full)

                def w(G, s):
                    C[G].wait_empty(pe, s, NL + 1)
                    pe.wait_ge(kb_done[G], s + 1)
                    each_head(bank[G][0], lambda h: kb[G][:, hc(h)], lambda h: XT[G][:, hc(h)], A[G].full)

                def new_values(G, s):
                    A[G].wait_empty(pe, s, NL + 2)
                    Dk[G].wait_empty(pe, s, 4)
                    for h in range(GH):
                        nc.tensor.matmul(bank[G][1][:, hc(h)], XT[G][:, hc(h)], vb[G][:, hc(h)], start=True,
                                         stop=False)
                        last = nc.tensor.matmul(bank[G][1][:, hc(h)], kc[G][:, hc(h)], state[G][:, hc(h)],
                                                start=False, stop=True)
                    last.then_inc(B[G].full, 1)

                def read_out(G, s):
                    B[G].wait_empty(pe, s, NL)
                    pe.wait_ge(qd_done[G], s + 1)
                    for h in range(GH):
                        nc.tensor.matmul(bank[G][2][:, hc(h)], state[G][:, hc(h)], grow[G][:, hc(h)], start=True,
                                         stop=False)
                        last = nc.tensor.matmul(bank[G][2][:, hc(h)], vc[G][:, hc(h)], attn[G][:, hc(h)],
                                                start=False, stop=True)
                    last.then_inc(C[G].full, 1)
                    each_head(bank[G][3], lambda h: kend[G][:, hc(h)], lambda h: vc[G][:, hc(h)], Dk[G].full)
                in_order(pe, [sums, decays, decays_low, queries, lower, keys, values, nothing], product_in, change,
                         [w, new_values, read_out])


def dilated_attention(K, g, qkv, mask, out, lse):
    nc = K.nc
    NB = LAT // P
    WB = 2 * P if g == 0 else P
    WS = NB * WB
    SC = 64.0 ** -0.5
    with ExitStack() as c:
        def sb(n, shape):
            return c.enter_context(nc.sbuf_tensor(f"da{g}_{n}", shape, F32))
        msk = sb("msk", [P, WS])
        qs, ks, vs, vt = (sb(n, [P, LAT]) for n in ("qs", "ks", "vs", "vt"))
        p = sb("p", [P, 2, WS])
        pt = sb("pt", [P, 2, WS])
        nmax, den, inv, lcol = (sb(n, [P, 2, NB]) for n in ("nmax", "den", "inv", "lcol"))
        lrow = sb("lrow", [P, 2, NB, 64])
        ps_s = [c.enter_context(nc.psum_tensor(f"da{g}_ps_s{r}", [P, 1024], F32)) for r in range(2)]
        ps_t = c.enter_context(nc.psum_tensor(f"da{g}_ps_t", [P, 1024], F32))
        ps_v = ps_l = c.enter_context(nc.psum_tensor(f"da{g}_ps_v", [P, 512], F32))
        ps_o = c.enter_context(nc.psum_tensor(f"da{g}_ps_o", [P, 512], F32))
        (loaded, qk_in, v_in, v_turned, vt_in, scored, scaled, maxed, less, exp_done, sums, inverted, normed, logged,
         lsum, rows, p_turned, pt_in, o_done, l_done, taken_l, turn_done) = K.signals(
            f"da{g}", "loaded qk_in v_in v_turned vt_in scored scaled maxed less exp_done sums inverted normed logged "
            "lsum rows p_turned pt_in o_done l_done taken_l turn_done")

        def order(t):
            if g == 0:
                return t
            if g == 1:
                return t.rearrange("p (i b) -> p b i", b=4)
            return t.rearrange("p (i b r) -> p b i r", b=4, r=4)

        def blocked(t):
            if g == 0:
                return t
            if g == 1:
                return t.rearrange("p (b i) -> p b i", b=4)
            return t.rearrange("p (b i r) -> p b i r", b=4, r=4)

        def tile(t, i):
            return t[:, bass.ds(i, 1), :].rearrange("p a t -> p (a t)")

        def pieces(dst_order, dst, src_order, src_):
            if g < 2:
                return [(dst_order(dst), src_order(src_))]
            d, s_ = dst_order(dst), src_order(src_)
            return [(d[:, b], s_[:, b]) for b in range(4)]

        def turns(eng, body):
            for u in range(2):
                body(u)

        with nc.Block() as block:
            @block.sync
            def _(sp):
                sp.dma_start(msk[:, :], mask).then_inc(loaded, 16)

            @block.scalar
            def _(act):
                def body(u):
                    if u > 0:
                        act.wait_ge(turn_done, u)
                    for dst, part in ((qs, 0), (ks, 1), (vs, 2)):
                        for d, s_ in pieces(blocked, dst[:, :], order, tile(qkv, 2 * part + u)):
                            last = nc.scalar.activation(d, s_, ACT.Copy)
                        if part:
                            last.then_inc((None, qk_in, v_in)[part], 1)
                    act.wait_ge(v_turned, u + 1)
                    nc.scalar.activation(vt[:, :], ps_v[:, :], ACT.Copy).then_inc(vt_in, 1)
                    for r in range(2):
                        act.wait_ge(less, 2 * u + r + 1)
                        nc.scalar.activation(p[:, r, :], p[:, r, :], ACT.Exp).then_inc(exp_done, 1)
                    for r in range(2):
                        act.wait_ge(sums, 2 * u + r + 1)
                        nc.scalar.activation(lcol[:, r, :], den[:, r, :], ACT.Ln).then_inc(logged, 1)
                    for r in range(2):
                        n = 2 * u + r
                        act.wait_ge(lsum, n + 1)
                        nc.scalar.activation(lrow[:, r, :, :], lcol[:, r, :].unsqueeze(2).to_broadcast([P, NB, 64]),
                                             ACT.Copy).then_inc(rows, 1)
                        act.wait_ge(p_turned, n + 1)
                        nc.scalar.activation(pt[:, r, :], ps_t[:, 0:WS], ACT.Copy).then_inc(pt_in, 1)
                    act.wait_ge(l_done, u + 1)
                    for d, s_ in pieces(order, tile(lse, u), blocked, ps_l[:, :]):
                        last = nc.scalar.activation(d, s_, ACT.Copy)
                    last.then_inc(taken_l, 1)
                turns(act, body)

            @block.vector
            def _(dve):
                dve.wait_ge(loaded, 16)

                def v4(t):
                    return t.rearrange("p (b k) -> p b k", b=NB)

                def body(u):
                    for r in range(2):
                        n = 2 * u + r
                        dve.wait_ge(scored, n + 1)
                        nc.vector.scalar_tensor_tensor(out=p[:, r, :], in0=ps_s[r][:, 0:WS], scalar=SC, in1=msk[:, :],
                                                       op0=ALU.mult, op1=ALU.add).then_inc(scaled, 1)
                        dve.wait_ge(scaled, n + 1)
                        nc.vector.tensor_reduce(nmax[:, r, :], v4(p[:, r, :]), AX.X, ALU.max).then_inc(maxed, 1)
                        dve.wait_ge(maxed, n + 1)
                        nc.vector.tensor_tensor(v4(p[:, r, :]), v4(p[:, r, :]),
                                                nmax[:, r, :].unsqueeze(2).to_broadcast([P, NB, WB]),
                                                ALU.subtract).then_inc(less, 1)
                    for r in range(2):
                        dve.wait_ge(exp_done, 2 * u + r + 1)
                        nc.vector.tensor_reduce(den[:, r, :], v4(p[:, r, :]), AX.X, ALU.add).then_inc(sums, 1)
                    for r in range(2):
                        n = 2 * u + r
                        dve.wait_ge(sums, n + 1)
                        nc.vector.reciprocal(inv[:, r, :], den[:, r, :]).then_inc(inverted, 1)
                        dve.wait_ge(inverted, n + 1)
                        nc.vector.tensor_tensor(v4(p[:, r, :]), v4(p[:, r, :]),
                                                inv[:, r, :].unsqueeze(2).to_broadcast([P, NB, WB]),
                                                ALU.mult).then_inc(normed, 1)
                        dve.wait_ge(logged, n + 1)
                        nc.vector.tensor_tensor(lcol[:, r, :], lcol[:, r, :], nmax[:, r, :], ALU.add).then_inc(lsum, 1)
                    dve.wait_ge(o_done, u + 1)
                    for d, s_ in pieces(order, tile(out, u), blocked, ps_o[:, :]):
                        last = nc.vector.tensor_copy(d, s_)
                    dve.wait_ge(taken_l, u + 1)
                    last.then_inc(turn_done, 1)
                turns(dve, body)

            @block.tensor
            def _(pe):
                def body(u):
                    if u > 0:
                        pe.wait_ge(turn_done, u)
                    pe.wait_ge(v_in, u + 1)
                    for b in range(NB):
                        last = nc.tensor.transpose(ps_v[:, b * P:(b + 1) * P], vs[:, b * P:(b + 1) * P], K.ident[:, :])
                    last.then_inc(v_turned, 1)
                    pe.wait_ge(qk_in, u + 1)
                    for r in range(2):
                        half = slice(64 * r, 64 * r + 64)
                        for b in range(NB):
                            first = b if g else max(b - 1, 0)
                            spans = [(b * WB, b * P, P)] if g else [
                                (b * WB, first * P, P), (b * WB + P, b * P, P)]
                            for col, key, width in spans:
                                last = nc.tensor.matmul(ps_s[r][:, col:col + width], qs[half, b * P:(b + 1) * P],
                                                        ks[half, key:key + width], start=True, stop=True)
                        last.then_inc(scored, 1)
                    pe.wait_ge(vt_in, u + 1)
                    for r in range(2):
                        n = 2 * u + r
                        half = slice(64 * r, 64 * r + 64)
                        pe.wait_ge(rows, n + 1)
                        for b in range(NB):
                            last = nc.tensor.matmul(ps_l[half, b * P:(b + 1) * P], lrow[:, r, b, :], K.ident[:, :],
                                                    start=True, stop=True)
                        if r:
                            last.then_inc(l_done, 1)
                        pe.wait_ge(normed, n + 1)
                        if n > 0:
                            pe.wait_ge(pt_in, n)
                        for b in range(WS // P):
                            last = nc.tensor.transpose(ps_t[:, b * P:(b + 1) * P], p[:, r, b * P:(b + 1) * P],
                                                       K.ident[:, :])
                        last.then_inc(p_turned, 1)
                        pe.wait_ge(pt_in, n + 1)
                        for b in range(NB):
                            both = g == 0 and b > 0
                            if both:
                                nc.tensor.matmul(ps_o[half, b * P:(b + 1) * P], vt[:, (b - 1) * P + 64 * r:(b - 1) * P + 64 * r + 64],
                                                 pt[:, r, b * WB:b * WB + P], start=True, stop=False)
                            last = nc.tensor.matmul(ps_o[half, b * P:(b + 1) * P], vt[:, b * P + 64 * r:b * P + 64 * r + 64],
                                                    pt[:, r, (b + 1) * WB - P:(b + 1) * WB], start=not both, stop=True)
                        if r:
                            last.then_inc(o_done, 1)
                turns(pe, body)


def weigh_groups(K, out, lse):
    nc = K.nc
    with ExitStack() as c:
        top = c.enter_context(nc.sbuf_tensor("wg_top", [P, 2, LAT], F32))
        tot = c.enter_context(nc.sbuf_tensor("wg_tot", [P, 2, LAT], F32))
        m1, m2, less, e_done, t1, t2, log_done, inv, weighed = K.signals(
            "wg", "m1 m2 less e_done t1 t2 log_done inv weighed")
        g3 = [lse[:, 2 * g:2 * g + 2, :] for g in range(3)]
        o3 = [out[:, 2 * g:2 * g + 2, :] for g in range(3)]
        with nc.Block() as block:
            @block.vector
            def _(dve):
                nc.vector.tensor_tensor(top[:, :, :], g3[0], g3[1], ALU.max).then_inc(m1, 1)
                dve.wait_ge(m1, 1)
                nc.vector.tensor_tensor(top[:, :, :], top[:, :, :], g3[2], ALU.max).then_inc(m2, 1)
                dve.wait_ge(m2, 1)
                for g in range(3):
                    nc.vector.tensor_tensor(g3[g], g3[g], top[:, :, :], ALU.subtract).then_inc(less, 1)
                dve.wait_ge(e_done, 3)
                nc.vector.tensor_tensor(tot[:, :, :], g3[0], g3[1], ALU.add).then_inc(t1, 1)
                dve.wait_ge(t1, 1)
                nc.vector.tensor_tensor(tot[:, :, :], tot[:, :, :], g3[2], ALU.add).then_inc(t2, 1)
                for g in range(3):
                    nc.vector.tensor_tensor(o3[g], o3[g], g3[g], ALU.mult).then_inc(weighed, 1)
                dve.wait_ge(inv, 1)
                for g in range(3):
                    dve.wait_ge(weighed, g + 1)
                    nc.vector.tensor_tensor(o3[g], o3[g], tot[:, :, :], ALU.mult)

            @block.scalar
            def _(act):
                for g in range(3):
                    act.wait_ge(less, g + 1)
                    nc.scalar.activation(g3[g], g3[g], ACT.Exp).then_inc(e_done, 1)
                act.wait_ge(t2, 1)
                nc.scalar.activation(tot[:, :, :], tot[:, :, :], ACT.Ln).then_inc(log_done, 1)
                act.wait_ge(log_done, 1)
                nc.scalar.activation(tot[:, :, :], tot[:, :, :], ACT.Exp, scale=-1.0).then_inc(inv, 1)


def second(K, nc, A, out, x, col, mods, scale1, tap):
    norm_scales(K, "sc2", [(scale1[:, 0, :], col("norm_2"), mods(1, 0))])
    norms = [(0, LAT, scale1[:, 0, :], mods(0, 0))]
    with ExitStack() as body:
        def sb(n, shape, dt=F32, where=body):
            return where.enter_context(nc.sbuf_tensor("s2_" + n, shape, dt))
        qkv = sb("qkv", [P, 24, LAT])
        ob, ya, group_qkv = qkv[:, 0:6, :], qkv[:, DT:2 * DT, :], qkv[:, 2 * DT:2 * DT + 6, :]
        with ExitStack() as dn:
            zab = sb("zab", [P, 9, LAT], F32, dn)
            with ExitStack() as hctx:
                h_hi, h_lo = sb("h_hi", [P, DT, LAT], F32R, hctx), sb("h_lo", [P, DT, LAT], F32R, hctx)
                model_norm(K, "n2", x, CTX, LAT, norms, h_hi, h_lo, work=qkv[:, 0:DT, :])
                delta_projections(K, "dq", A["dn_qkv"], h_hi, h_lo, qkv, col("conv_2"), (A["dn_zab"], DT))
                product(K, "dz", A["dn_zab"], 9, DT, h_hi, h_lo, 0, LAT, copy_out(K, zab, ACT.Silu, {8: ACT.Copy}), no_evac,
                        (A["proj_a"], DT))
            group_norm(K, "l2", qkv[:, 0:16, :], qkv[:, 0:16, :], 16, 1, LAT, None, K.ones, 1.0)
            tap("k_dn", qkv[:, 8:16, :])
            tap("v_dn", qkv[:, 16:24, :])
            by_token = sb("by_token", [P, LAT // CHUNK, 2 * DN_HEADS], F32, dn)
            delta_gates(K, zab[:, 8, :], col("a_log"), col("dt_bias"), by_token)
            delta_rule(K, qkv, by_token, A["dr_consts"], A["dr_joins"])
            tap("o_a", qkv[:, 0:8, :])
            o = qkv[:, 0:8, :]
            group_norm(K, "dnn", o, o, 8, 1, LAT, col("dn_norm"), K.ones, 1.0 / P)
            o_hi, o_lo = sb("o_hi", [P, DT, LAT], F32R, dn), sb("o_lo", [P, DT, LAT], F32R, dn)
            gated_readout(K, "dro", o, zab[:, 0:8, :], o_hi, o_lo)
            product(K, "pa", A["proj_a"], DT, DT, o_hi, o_lo, 0, LAT, copy_out(K, ya, ACT.Copy), no_evac,
                    (A["da0"], DT))
        h_hi, h_lo = sb("h2_hi", [P, DT, LAT], F32R), sb("h2_lo", [P, DT, LAT], F32R)
        model_norm(K, "n3", x, CTX, LAT, norms, h_hi, h_lo)
        yb = sb("yb", [P, DT, LAT])
        with ExitStack() as at:
            lse = sb("lse", [P, 6, LAT], F32, at)
            for g in range(3):
                product(K, f"dp{g}", A[f"da{g}"], 6, DT, h_hi, h_lo, 0, LAT, copy_out(K, group_qkv, ACT.Copy),
                        no_evac, (A[f"da{g + 1}"] if g < 2 else A["da_z"], DT))
                dilated_attention(K, g, group_qkv, A["da_mask0"] if g == 0 else A["da_mask12"][g - 1],
                                  ob[:, 2 * g:2 * g + 2, :], lse[:, 2 * g:2 * g + 2, :])
            weigh_groups(K, ob, lse)
            tap("o_b", ob[:, :, :])
            product(K, "dbz", A["da_z"], 6, DT, h_hi, h_lo, 0, LAT, copy_out(K, lse, ACT.Silu), no_evac,
                    (A["proj_b"], 6))
            b_hi, b_lo = sb("b_hi", [P, 6, LAT], F32R, at), sb("b_lo", [P, 6, LAT], F32R, at)
            gated_readout(K, "dbo", ob, lse, b_hi, b_lo)
            product(K, "pb", A["proj_b"], DT, 6, b_hi, b_lo, 0, LAT, copy_out(K, yb, ACT.Copy), no_evac,
                    (A["gate_a"], DT))
        m_hi, m_lo = sb("m_hi", [P, DT, LAT], F32R), sb("m_lo", [P, DT, LAT], F32R)
        with ExitStack() as gt:
            sig = sb("sig", [P, 2, LAT], F32, gt)
            prod = sb("prod", [P, 2, LAT], F32, gt)
            def sigmoid(act, g, ip, j, i, first):
                act.wait_ge(g.mm_done, i + 1)
                if not first:
                    act.wait_ge(g.more[0], i - 1)
                nc.scalar.activation(sig[:, j, :], g.out[j], ACT.Sigmoid).then_inc(g.free[j], 1)

            def gate_a(dve, g, ip, j, i, first):
                dve.wait_ge(g.free[j], ip + 1)
                nc.vector.tensor_tensor(ya[:, i, :], ya[:, i, :], sig[:, j, :], ALU.mult).then_inc(g.more[0], 1)

            def sigmoid_and_part(act, g, ip, j, i, first):
                used, summed_up, upper, lower = g.more
                sigmoid(act, g, ip, j, i, first)
                act.wait_ge(summed_up, i + 1)
                nc.scalar.activation(m_hi[:, i, :], ya[:, i, :], ACT.Copy).then_inc(upper, 1)

            def gate_b(dve, g, ip, j, i, first):
                used, summed_up, upper, lower = g.more
                dve.wait_ge(g.free[j], ip + 1)
                if not first:
                    dve.wait_ge(summed_up, i - 1)
                nc.vector.tensor_tensor(prod[:, j, :], yb[:, i, :], sig[:, j, :], ALU.mult).then_inc(used, 1)
                dve.wait_ge(used, i + 1)
                nc.vector.tensor_tensor(ya[:, i, :], ya[:, i, :], prod[:, j, :], ALU.add).then_inc(summed_up, 1)
                dve.wait_ge(upper, i + 1)
                nc.vector.tensor_tensor(m_lo[:, i, :], ya[:, i, :], m_hi[:, i, :].bitcast(F32),
                                        ALU.subtract).then_inc(lower, 1)
            product(K, "pga", A["gate_a"], DT, DT, h_hi, h_lo, 0, LAT, sigmoid, gate_a, (A["gate_b"], DT), "used")
            product(K, "pgb", A["gate_b"], DT, DT, h_hi, h_lo, 0, LAT, sigmoid_and_part, gate_b,
                    (A["w_out2"], DT), "used summed_up upper lower")
        product(K, "po", A["w_out2"], DT, DT, m_hi, m_lo, 0, LAT, no_evac,
                add_gated(K, x, [(CTX, TOK, mods(2, 0))], CTX), None, rms_of=x)
    with ExitStack() as fin:
        y = fin.enter_context(nc.sbuf_tensor("y_out", [P, DT, LAT], F32))
        model_norm(K, "nf", x, CTX, LAT, [(0, LAT, col("final"), None)], plain=y)
        load_sbuf(K, "store", [(out, y[:, :, :])])


def rest(K, nc, A, out, x, col, mods1, mod2, mods2, scale1, scale2, tap):
    layer1(K, nc, A, x, col, mods1, scale1, scale2, tap, (A["dn_qkv"], DT),
           (A["c2_rows"], A["ada2_t"], col("ada_b_2"), mod2))
    second(K, nc, A, out, x, col, mods2, scale1, tap)


def layout2(np, I, A, blocks):
    A["ada2_t"] = I["ada_w_2"][0].T
    A["c2_rows"] = np.tile(I["c_2"].reshape(1, 1, D), (P, 1, 1))
    w = I["w_in_2"][0]
    A["dn_qkv"] = blocks(w[:, 0:3072])
    ab = np.zeros((D, P), np.float32)
    ab[:, 0:8] = w[:, 4104:4112]
    ab[:, 32:40] = w[:, 4096:4104]
    A["dn_zab"] = blocks(np.concatenate([w[:, 3072:4096], ab], axis=1))
    at = w[:, 4112:4112 + 4 * 768].reshape(D, 4, 3, 256)
    for g in range(3):
        A[f"da{g}"] = blocks(at[:, 0:3, g].reshape(D, 768))
    A["da_z"] = blocks(at[:, 3].reshape(D, 768))
    A["gate_a"] = blocks(w[:, 7184:8208])
    A["gate_b"] = blocks(w[:, 8208:9232])
    A["proj_a"] = blocks(I["w_proj_a_2"][0])
    A["proj_b"] = blocks(I["w_proj_b_2"][0])
    A["w_out2"] = blocks(I["w_out_2"][0])
    r, t = np.arange(P)[:, None], np.arange(P)[None, :]
    A["dr_consts"] = np.stack([r <= t, r > t, (r <= t) * DN_SCALE], axis=1).astype(np.float32)
    joins = [(r // n == t // n) & (r % n < n // 2) & (t % n >= n // 2) for n in JOINS]
    A["dr_joins"] = np.stack(joins + [joins[0].T], axis=1).astype(np.float32)
    off = np.float32(-1e30)
    own = np.where(r >= t, 0, off)
    before = np.where(t >= r, 0, off)
    none = np.full((P, P), off)
    A["da_mask0"] = np.concatenate([m for b in range(4) for m in ((before if b else none), own)],
                                   axis=1).astype(np.float32)
    cls = np.where((r >= t) & (r % 4 == t % 4), 0, off)
    A["da_mask12"] = np.stack([np.tile(own, 4), np.tile(cls, 4)]).astype(np.float32)


def more_layout(np, I, A, blocks, column):
    layout1(np, I, A, blocks)
    layout2(np, I, A, blocks)


def _layout(np, I):
    def blocks(w):
        k, n = w.shape
        return np.ascontiguousarray(w.reshape(k // P, P, n // P, P).transpose(2, 1, 0, 3)).reshape(n, k)

    def column(v):
        return v.reshape(-1, P).T

    def tokens(x):
        return x.T.reshape(DT, P, -1).transpose(1, 0, 2)
    A = {}
    A["x"] = np.concatenate([tokens(I["ctx"][0]), tokens(I["x"][0])], axis=2)
    A["ada0"] = blocks(I["ada_w"][0][:, 0:MOD0_FIRST * P])
    A["ada0_t"] = I["ada_w"][0][:, MOD0_FIRST * P:].T
    A["ada1_t"] = I["ada_w"][1].T
    A["c_rows"] = np.tile(np.stack([I["c"][0], I["c_ctx"]])[None], (P, 1, 1))
    for l in range(2):
        up = I["ffn_w_up"][l].reshape(D, 2, FT, P).transpose(0, 2, 1, 3).reshape(D, 2 * D_FF)
        A[f"up{l}"] = blocks(up)
        down = I["ffn_w_down"][l]
        A[f"down{l}"] = np.concatenate([blocks(down[:FH * P]), blocks(down[FH * P:])])
    w = I["ev_w_in"][0].reshape(D, 28, P)
    pick = {"ev_uv": list(range(20, 28)), "ev_qg": list(range(0, 4)) + list(range(16, 20)),
            "ev_vz": list(range(4, 16))}
    for name, tiles in pick.items():
        A[name] = blocks(w[:, tiles].reshape(D, -1))
    A["ev_out"] = blocks(I["ev_w_out"][0])
    A["ws_t"] = I["ev_ws"][0].transpose(2, 0, 1).reshape(P, -1)
    A["bs"] = I["ev_bs"][0].reshape(1, -1)
    t = np.arange(CHUNK)
    s_, t_ = t[:, None], t[None, :]
    masks = np.zeros((2, P, len(LEVELS) + 1, CHUNK), np.float32)
    for l, size in enumerate(LEVELS):
        same = s_ // size == t_ // size
        early_s, early_t = s_ % size < size // 2, t_ % size < size // 2
        masks[0, :, l] = same & early_s & ~early_t
        masks[1, :, l] = same & ~early_s & early_t
    masks[0, :, -1] = (s_ // 4 == t_ // 4) & (s_ <= t_)
    masks[1, :, -1] = (s_ // 4 == t_ // 4) & (s_ >= t_)
    A["gla_masks"] = masks
    A["ident"] = np.eye(P, dtype=np.float32)

    cc = np.stack([I["c"][0], I["c_ctx"]], axis=1).reshape(DT, P, 2).transpose(1, 0, 2).reshape(P, -1)
    qn, kn = I["od_q_norm_w"][0], I["od_k_norm_w"][0]
    parts = {
        "c": cc, "c_2": column(I["c_2"][0]), "ada_b0": column(I["ada_b"][0]), "ada_b1": column(I["ada_b"][1]),
        "ada_b_2": column(I["ada_b_2"][0]),
        "norm_mix0": column(I["norm_mix_w"][0]), "norm_mix1": column(I["norm_mix_w"][1]),
        "norm_ffn0": column(I["norm_ffn_w"][0]), "norm_ffn1": column(I["norm_ffn_w"][1]),
        "norm_2": column(I["norm_w_2"][0]), "final": column(I["final_norm_w_2"]),
        "lb": column(I["ev_lb_logits"][0].reshape(-1)), "onorm": np.repeat(column(I["ev_onorm_w"][0]), 4, axis=1),
        "vnorm": column(I["ev_vnorm_w"][0].reshape(-1)),
        "conv_b0": column(I["ffn_conv_b"][0]), "conv_b1": column(I["ffn_conv_b"][1]),
        "qa_norm": column(I["od_qa_norm_w"][0]), "kva_norm": column(I["od_kva_norm_w"][0]),
        "q_nope": np.repeat(column(qn[:P]), 6, axis=1), "k_nope": np.repeat(column(kn[:P]), 6, axis=1),
        "q_pe": np.repeat(column(np.concatenate([qn[P:], qn[P:]])), 3, axis=1),
        "k_pe": column(np.concatenate([kn[P:], kn[P:]])),
        "conv_2": I["conv_w_2"][0].reshape(4, 24, P).transpose(2, 1, 0).reshape(P, -1),
        "dn_norm": np.repeat(column(I["dn_norm_w_2"][0]), 8, axis=1),
    }
    for name in ("a_log", "dt_bias"):
        parts[name] = np.concatenate([I[name + "_2"][0], np.zeros(P - 8, np.float32)])[:, None]
    for l in range(2):
        parts[f"conv_w{l}"] = I["ffn_conv_w"][l].reshape(3, FT, P).transpose(2, 1, 0).reshape(P, -1)
    A["cols"] = np.concatenate([parts[n] for n in COLUMNS.at], axis=1)
    more_layout(np, I, A, blocks, column)
    return {n: np.ascontiguousarray(a) for n, a in A.items()}


def kernel(**inputs):
    import numpy as np
    import concourse.bacc as bacc
    from concourse.bass_utils import run_bass_kernel_spmd

    arrays = _layout(np, {n: np.asarray(a) for n, a in inputs.items()})
    nc = bacc.Bacc("TRN2", target_bir_lowering=False, num_devices=1)
    A = {n: nc.dram_tensor("in_" + n, a.shape, F32, kind="ExternalInput").ap() for n, a in arrays.items()}
    out = nc.dram_tensor("out_t", (P, DT, LAT), F32, kind="ExternalOutput").ap()
    program(nc, A, out, None)
    r = run_bass_kernel_spmd(nc, [{"in_" + n: a for n, a in arrays.items()}], core_ids=[0])
    got = r.results[0]["out_t"]
    return np.ascontiguousarray(got.transpose(2, 1, 0).reshape(1, LAT, D))
```
